# Optimizing a Trainium2 kernel written in Bass

```python
import math
import jax
import jax.numpy as jnp
from jax import lax
import numpy as np

D_MODEL = 1024
BATCH = 1
SEQ = 128
DEPTH = 2
DEC_BATCH = 1
DEC_SEQ = 256
PAST_LEN = 128

GRID_W = 64
ROPE_BASE = 10000.0
EPS = 1e-6
Q_BLOCK = 128
N_ATTN = (DEPTH + 1) // 2
N_SSD = DEPTH // 2

A_HEADS = 4
A_DQK = 64
A_DV = 2 * A_DQK
A_QK_W = A_HEADS * 2 * A_DQK
A_V_W = A_HEADS * A_DV
B_HEADS = 4
B_NOPE = 128
B_ROPE = 64
B_DQK = B_NOPE + B_ROPE
B_DV = 128
B_Q_LORA = 384
B_KV_LORA = 256
ATTN_SPLITS = (A_QK_W, 2 * A_QK_W, 2 * A_QK_W + A_V_W, 2 * A_QK_W + A_V_W + B_Q_LORA,
               2 * A_QK_W + A_V_W + B_Q_LORA + B_KV_LORA)
ATTN_IN = 2 * A_QK_W + A_V_W + B_Q_LORA + B_KV_LORA + B_ROPE
ATTN_OUT = A_HEADS * A_DV + B_HEADS * B_DV
SSD_DI = 2 * D_MODEL
SSD_P = 64
SSD_H = SSD_DI // SSD_P
SSD_N = 128
SSD_G = 4
SSD_CONV = 3
SSD_CHUNK = 128
SSD_CONV_DIM = SSD_DI + 2 * SSD_G * SSD_N
SSD_IN = SSD_DI + SSD_CONV_DIM + 2 * SSD_H
SSD_SPLITS = (SSD_DI, SSD_DI + SSD_CONV_DIM)
XBC_SPLITS = (SSD_DI, SSD_DI + SSD_G * SSD_N)
N_EXPERTS = 16
N_EXPERT_GROUPS = 4
EXPERTS_PER_GROUP = N_EXPERTS // N_EXPERT_GROUPS
TOP_K = 2
D_EXPERT = 256

kernel_name = 'hybrid_diffattn_mla_ssd_moe_dit_step'

def rmsnorm(x, g=None):
    xf = x.astype(jnp.float32)
    y = xf * lax.rsqrt(jnp.mean(xf * xf, axis=-1, keepdims=True) + EPS)
    if g is not None:
        y = y * g.astype(jnp.float32)
    return y.astype(x.dtype)

def modulate(x, g, shift, scale):
    return rmsnorm(x, g) * (1.0 + scale) + shift

def axial_rope(x):
    n_tok = x.shape[1]
    rows = n_tok // GRID_W
    t = jnp.arange(rows * GRID_W)
    row = (t // GRID_W).astype(jnp.float32)
    col = (t % GRID_W).astype(jnp.float32)
    half = x.shape[-1] // 2
    inv = ROPE_BASE ** (-2.0 * jnp.arange(half // 2, dtype=jnp.float32) / half)
    ang = jnp.concatenate([row[:, None] * inv, col[:, None] * inv], axis=-1)
    ang = ang.reshape((n_tok,) + (1,) * (x.ndim - 3) + (half,))
    cos, sin = jnp.cos(ang), jnp.sin(ang)
    xf = x.astype(jnp.float32)
    x1, x2 = xf[..., :half], xf[..., half:]
    return jnp.concatenate([x1 * cos - x2 * sin, x1 * sin + x2 * cos], axis=-1).astype(x.dtype)

def map_query_blocks(fn, q):
    bsz, n = q.shape[:2]
    nb = n // Q_BLOCK
    qb = jnp.moveaxis(q.reshape((bsz, nb, Q_BLOCK) + q.shape[2:]), 1, 0)
    out = lax.map(fn, qb)
    return jnp.moveaxis(out, 0, 1).reshape((bsz, n) + out.shape[3:])

def diff_attention(q, k, v, lam):
    scale = A_DQK ** -0.5
    def block(qb):
        s = jnp.einsum('bqhmd,bkhmd->bhmqk', qb, k).astype(jnp.float32) * scale
        p = jax.nn.softmax(s, axis=-1)
        w = (p[:, :, 0] - lam * p[:, :, 1]).astype(v.dtype)
        return jnp.einsum('bhqk,bkhd->bqhd', w, v)
    return map_query_blocks(block, q)

def softmax_attention(q, k, v):
    scale = B_DQK ** -0.5
    def block(qb):
        s = jnp.einsum('bqhd,bkhd->bhqk', qb, k).astype(jnp.float32) * scale
        p = jax.nn.softmax(s, axis=-1).astype(v.dtype)
        return jnp.einsum('bhqk,bkhd->bqhd', p, v)
    return map_query_blocks(block, q)

def attn_project(h, p):
    bsz, n, _ = h.shape
    a_q, a_k, a_v, b_qc, b_kvc, b_kr = jnp.split(h @ p['w_in'], ATTN_SPLITS, axis=-1)
    a_q = rmsnorm(a_q.reshape(bsz, n, A_HEADS, 2, A_DQK), p['a_qk_g'][0])
    a_k = rmsnorm(a_k.reshape(bsz, n, A_HEADS, 2, A_DQK), p['a_qk_g'][1])
    a_v = a_v.reshape(bsz, n, A_HEADS, A_DV)
    b_q = (rmsnorm(b_qc, p['b_qa_g']) @ p['b_wq_up']).reshape(bsz, n, B_HEADS, B_DQK)
    b_q = rmsnorm(b_q, p['b_qk_g'][0])
    b_ckv = rmsnorm(b_kvc, p['b_kva_g'])
    return a_q, a_k, a_v, b_q, b_ckv, b_kr

def mla_expand(ckv, krope, p):
    bsz, n, _ = ckv.shape
    kv = (ckv @ p['b_wkv_up']).reshape(bsz, n, B_HEADS, B_NOPE + B_DV)
    k = jnp.concatenate([kv[..., :B_NOPE],
                         jnp.broadcast_to(krope[:, :, None, :], (bsz, n, B_HEADS, B_ROPE))], axis=-1)
    return rmsnorm(k, p['b_qk_g'][1]), kv[..., B_NOPE:]

def rope_tail(x):
    return jnp.concatenate([x[..., :B_NOPE], axial_rope(x[..., B_NOPE:])], axis=-1)

def diff_lambda(p):
    lq1, lk1, lq2, lk2 = p['a_lambda'].astype(jnp.float32)
    return jnp.exp(jnp.sum(lq1 * lk1)) - jnp.exp(jnp.sum(lq2 * lk2)) + p['lam_init']

def attn_merge(o_a, o_b, p):
    bsz, n = o_a.shape[:2]
    o_a = rmsnorm(o_a, p['a_sub_g']) * (1.0 - p['lam_init'])
    o = jnp.concatenate([o_a.reshape(bsz, n, -1), o_b.reshape(bsz, n, -1)], axis=-1)
    return o @ p['w_out']

def attn_context(h, p):
    a_q, a_k, a_v, b_q, b_ckv, b_kr = attn_project(h, p)
    o_a = diff_attention(a_q, a_k, a_v, diff_lambda(p))
    b_k, b_v = mla_expand(b_ckv, b_kr, p)
    o_b = softmax_attention(b_q, b_k, b_v)
    return attn_merge(o_a, o_b, p), a_k, a_v, b_ckv, b_kr

def attn_latent(h, ctx_a_k, ctx_a_v, ctx_ckv, ctx_kr, p):
    a_q, a_k, a_v, b_q, b_ckv, b_kr = attn_project(h, p)
    k_a = jnp.concatenate([ctx_a_k, axial_rope(a_k)], axis=1)
    v_a = jnp.concatenate([ctx_a_v, a_v], axis=1)
    o_a = diff_attention(axial_rope(a_q), k_a, v_a, diff_lambda(p))
    kb_ctx, vb_ctx = mla_expand(ctx_ckv, ctx_kr, p)
    kb_lat, vb_lat = mla_expand(b_ckv, b_kr, p)
    k_b = jnp.concatenate([kb_ctx, rope_tail(kb_lat)], axis=1)
    v_b = jnp.concatenate([vb_ctx, vb_lat], axis=1)
    o_b = softmax_attention(rope_tail(b_q), k_b, v_b)
    return attn_merge(o_a, o_b, p)

def centred_depthwise_conv(x, w, b):
    ch = x.shape[-1]
    width = w.shape[0]
    y = lax.conv_general_dilated(x, w[:, None, :].astype(x.dtype), window_strides=(1,),
                                 padding=[((width - 1) // 2, width // 2)],
                                 dimension_numbers=('NWC', 'WIO', 'NWC'),
                                 feature_group_count=ch)
    return y + b

def ssd_chunk_scan(x, dt, a_head, bmat, cmat, s0):
    bsz, n = x.shape[:2]
    nc, q = n // SSD_CHUNK, SSD_CHUNK
    e = SSD_H // SSD_G
    x = x.astype(jnp.float32).reshape(bsz, nc, q, SSD_G, e, SSD_P)
    dt = dt.reshape(bsz, nc, q, SSD_G, e)
    bmat = bmat.astype(jnp.float32).reshape(bsz, nc, q, SSD_G, SSD_N)
    cmat = cmat.astype(jnp.float32).reshape(bsz, nc, q, SSD_G, SSD_N)
    a_cs = jnp.cumsum(dt * a_head.reshape(SSD_G, e), axis=2)
    seg = a_cs[:, :, :, None] - a_cs[:, :, None, :]
    lower = jnp.tril(jnp.ones((q, q), dtype=bool))[:, :, None, None]
    decay = jnp.exp(jnp.where(lower, seg, -jnp.inf))
    xdt = x * dt[..., None]
    cb = jnp.einsum('bclgn,bcsgn->bclsg', cmat, bmat)
    y_diag = jnp.einsum('bclsge,bcsgep->bclgep', cb[..., None] * decay, xdt)
    decay_end = jnp.exp(a_cs[:, :, -1:] - a_cs)
    chunk_states = jnp.einsum('bclgn,bclge,bclgep->bcgepn', bmat, decay_end, xdt)
    chunk_decay = jnp.exp(a_cs[:, :, -1])

    def step(s, inp):
        st, dec = inp
        return s * dec[..., None, None] + st, s

    s_final, s_in = lax.scan(step, s0.astype(jnp.float32).reshape(bsz, SSD_G, e, SSD_P, SSD_N),
                             (jnp.moveaxis(chunk_states, 1, 0), jnp.moveaxis(chunk_decay, 1, 0)))
    s_in = jnp.moveaxis(s_in, 0, 1)
    y_off = jnp.einsum('bclgn,bcgepn,bclge->bclgep', cmat, s_in, jnp.exp(a_cs))
    y = (y_diag + y_off).reshape(bsz, n, SSD_H, SSD_P)
    return y, s_final.reshape(bsz, SSD_H, SSD_P, SSD_N)

def ssd_mixer(h, s0_f, s0_b, p):
    bsz, n, _ = h.shape
    z, xbc, dt_raw = jnp.split(h @ p['w_in'], SSD_SPLITS, axis=-1)
    xbc = jax.nn.silu(centred_depthwise_conv(xbc, p['conv_w'], p['conv_b']))
    xs, bmat, cmat = jnp.split(xbc, XBC_SPLITS, axis=-1)
    xs = xs.reshape(bsz, n, SSD_H, SSD_P)
    bmat = bmat.reshape(bsz, n, SSD_G, SSD_N)
    cmat = cmat.reshape(bsz, n, SSD_G, SSD_N)
    dt = jax.nn.softplus(dt_raw.astype(jnp.float32).reshape(bsz, n, 2, SSD_H)
                         + p['dt_bias'].astype(jnp.float32))
    a = -jnp.exp(p['a_log'].astype(jnp.float32))
    y_f, s_f = ssd_chunk_scan(xs, dt[:, :, 0], a[0], bmat, cmat, s0_f)
    flip = lambda t: jnp.flip(t, axis=1)
    y_b, s_b = ssd_chunk_scan(flip(xs), flip(dt[:, :, 1]), a[1], flip(bmat), flip(cmat), s0_b)
    y = y_f + flip(y_b) + xs.astype(jnp.float32) * p['d'].astype(jnp.float32)[:, None]
    y = y.reshape(bsz, n, SSD_DI) * jax.nn.silu(z.astype(jnp.float32))
    y = rmsnorm(y.reshape(bsz, n, SSD_G, SSD_DI // SSD_G)).reshape(bsz, n, SSD_DI)
    y = y * p['norm_g'].astype(jnp.float32)
    return y.astype(h.dtype) @ p['w_out'], jnp.stack([s_f, s_b], axis=1)

def swiglu(u):
    return jax.nn.silu(u[..., :D_EXPERT]) * u[..., D_EXPERT:]

def grouped_moe(h, router_w, router_bias, w_in, w_out, sh_in, sh_out):
    bsz, n, d = h.shape
    t = h.reshape(-1, d)
    scores = jax.nn.sigmoid((t @ router_w).astype(jnp.float32))
    sel = scores + router_bias.astype(jnp.float32)
    grp_score = lax.top_k(sel.reshape(-1, N_EXPERT_GROUPS, EXPERTS_PER_GROUP), TOP_K)[0].sum(-1)
    best = jnp.argmax(grp_score, axis=-1)
    in_group = jnp.repeat(jnp.arange(N_EXPERT_GROUPS)[None, :] == best[:, None], EXPERTS_PER_GROUP, axis=-1)
    _, idx = lax.top_k(jnp.where(in_group, sel, -jnp.inf), TOP_K)
    w = jnp.take_along_axis(scores, idx, axis=-1)
    w = w / jnp.sum(w, axis=-1, keepdims=True)
    gates = jnp.sum(jax.nn.one_hot(idx, N_EXPERTS, dtype=jnp.float32) * w[..., None], axis=1)
    hid = swiglu(jnp.einsum('td,edf->tef', t, w_in))
    routed = jnp.einsum('tef,efd->td', hid * gates[..., None].astype(hid.dtype), w_out)
    shared = swiglu(t @ sh_in) @ sh_out
    return (routed + shared).reshape(bsz, n, d)

def setup_inputs(seed: int = 0) -> dict:
    key = jax.random.key(seed)
    ks = iter(jax.random.split(key, 64))
    def nrm(shape, scale=1.0):
        return jax.random.normal(next(ks), shape, jnp.float32) * scale
    def gain(shape):
        return 1.0 + nrm(shape, 0.02)
    dt0 = jnp.exp(jax.random.uniform(next(ks), (N_SSD, 2, SSD_H), jnp.float32,
                                     minval=math.log(1e-3), maxval=math.log(1e-1)))
    return {
        'x_prompt': nrm((BATCH, SEQ, D_MODEL)),
        'x_sample': nrm((DEC_BATCH, DEC_SEQ, D_MODEL)),
        'cache_a_k': nrm((DEC_BATCH, N_ATTN, PAST_LEN, A_HEADS, 2, A_DQK)),
        'cache_a_v': nrm((DEC_BATCH, N_ATTN, PAST_LEN, A_HEADS, A_DV)),
        'cache_b_ckv': nrm((DEC_BATCH, N_ATTN, PAST_LEN, B_KV_LORA)),
        'cache_b_krope': nrm((DEC_BATCH, N_ATTN, PAST_LEN, B_ROPE)),
        'state_ssd': nrm((DEC_BATCH, N_SSD, 2, SSD_H, SSD_P, SSD_N), 0.5),
        'c': nrm((DEC_BATCH, D_MODEL)),
        'c_ctx': nrm((D_MODEL,)),
        'mod_w': nrm((DEPTH, D_MODEL, 6 * D_MODEL), 0.5 * D_MODEL ** -0.5),
        'mod_b': nrm((DEPTH, 6 * D_MODEL), 0.02),
        'norm1_g': gain((DEPTH, D_MODEL)),
        'norm2_g': gain((DEPTH, D_MODEL)),
        'attn_w_in': nrm((N_ATTN, D_MODEL, ATTN_IN), D_MODEL ** -0.5),
        'a_qk_g': gain((N_ATTN, 2, A_DQK)),
        'a_lambda': nrm((N_ATTN, 4, A_DQK), 0.1),
        'a_sub_g': gain((N_ATTN, A_DV)),
        'b_qa_g': gain((N_ATTN, B_Q_LORA)),
        'b_wq_up': nrm((N_ATTN, B_Q_LORA, B_HEADS * B_DQK), B_Q_LORA ** -0.5),
        'b_kva_g': gain((N_ATTN, B_KV_LORA)),
        'b_wkv_up': nrm((N_ATTN, B_KV_LORA, B_HEADS * (B_NOPE + B_DV)), B_KV_LORA ** -0.5),
        'b_qk_g': gain((N_ATTN, 2, B_DQK)),
        'attn_w_out': nrm((N_ATTN, ATTN_OUT, D_MODEL), ATTN_OUT ** -0.5),
        'ssd_w_in': nrm((N_SSD, D_MODEL, SSD_IN), D_MODEL ** -0.5),
        'ssd_conv_w': nrm((N_SSD, SSD_CONV, SSD_CONV_DIM), SSD_CONV ** -0.5),
        'ssd_conv_b': nrm((N_SSD, SSD_CONV_DIM), 0.02),
        'ssd_dt_bias': dt0 + jnp.log(-jnp.expm1(-dt0)),
        'ssd_a_log': jnp.log(jax.random.uniform(next(ks), (N_SSD, 2, SSD_H), jnp.float32, minval=1.0, maxval=16.0)),
        'ssd_d': gain((N_SSD, SSD_H)),
        'ssd_norm_g': gain((N_SSD, SSD_DI)),
        'ssd_w_out': nrm((N_SSD, SSD_DI, D_MODEL), SSD_DI ** -0.5),
        'router_w': nrm((D_MODEL, N_EXPERTS), D_MODEL ** -0.5),
        'router_bias': nrm((N_EXPERTS,), 0.01),
        'moe_w_in': nrm((DEPTH, N_EXPERTS, D_MODEL, 2 * D_EXPERT), D_MODEL ** -0.5),
        'moe_w_out': nrm((DEPTH, N_EXPERTS, D_EXPERT, D_MODEL), D_EXPERT ** -0.5),
        'shared_w_in': nrm((DEPTH, D_MODEL, 2 * D_EXPERT), D_MODEL ** -0.5),
        'shared_w_out': nrm((DEPTH, D_EXPERT, D_MODEL), D_EXPERT ** -0.5),
    }

def reference(x_prompt, x_sample, cache_a_k, cache_a_v, cache_b_ckv, cache_b_krope, state_ssd,
              c, c_ctx, mod_w, mod_b, norm1_g, norm2_g, attn_w_in, a_qk_g, a_lambda, a_sub_g,
              b_qa_g, b_wq_up, b_kva_g, b_wkv_up, b_qk_g, attn_w_out, ssd_w_in, ssd_conv_w,
              ssd_conv_b, ssd_dt_bias, ssd_a_log, ssd_d, ssd_norm_g, ssd_w_out, router_w,
              router_bias, moe_w_in, moe_w_out, shared_w_in, shared_w_out):
    xp, xs = x_prompt, x_sample
    silu_ctx = jax.nn.silu(c_ctx)
    silu_c = jax.nn.silu(c)
    new_a_k, new_a_v, new_ckv, new_kr, new_ssd = [], [], [], [], []
    for l in range(DEPTH):
        i = l // 2
        mp = jnp.split(silu_ctx @ mod_w[l] + mod_b[l], 6, axis=-1)
        ms = jnp.split((silu_c @ mod_w[l] + mod_b[l])[:, None, :], 6, axis=-1)
        hp = modulate(xp, norm1_g[l], mp[0], mp[1])
        hs = modulate(xs, norm1_g[l], ms[0], ms[1])
        if l % 2 == 0:
            ap = {'w_in': attn_w_in[i], 'a_qk_g': a_qk_g[i], 'a_lambda': a_lambda[i],
                  'a_sub_g': a_sub_g[i], 'b_qa_g': b_qa_g[i], 'b_wq_up': b_wq_up[i],
                  'b_kva_g': b_kva_g[i], 'b_wkv_up': b_wkv_up[i], 'b_qk_g': b_qk_g[i],
                  'w_out': attn_w_out[i], 'lam_init': 0.8 - 0.6 * math.exp(-0.3 * l)}
            out_p, ak, av, ckv, kr = attn_context(hp, ap)
            out_s = attn_latent(hs, cache_a_k[:, i], cache_a_v[:, i], cache_b_ckv[:, i],
                                cache_b_krope[:, i], ap)
            new_a_k.append(ak)
            new_a_v.append(av)
            new_ckv.append(ckv)
            new_kr.append(kr)
        else:
            sp = {'w_in': ssd_w_in[i], 'conv_w': ssd_conv_w[i], 'conv_b': ssd_conv_b[i],
                  'dt_bias': ssd_dt_bias[i], 'a_log': ssd_a_log[i], 'd': ssd_d[i],
                  'norm_g': ssd_norm_g[i], 'w_out': ssd_w_out[i]}
            zero = jnp.zeros((xp.shape[0], SSD_H, SSD_P, SSD_N), jnp.float32)
            out_p, st = ssd_mixer(hp, zero, zero, sp)
            out_s, _ = ssd_mixer(hs, state_ssd[:, i, 0], state_ssd[:, i, 1], sp)
            new_ssd.append(st)
        xp = xp + mp[2] * out_p
        xs = xs + ms[2] * out_s
        hp = modulate(xp, norm2_g[l], mp[3], mp[4])
        hs = modulate(xs, norm2_g[l], ms[3], ms[4])
        xp = xp + mp[5] * grouped_moe(hp, router_w, router_bias, moe_w_in[l], moe_w_out[l],
                                      shared_w_in[l], shared_w_out[l])
        xs = xs + ms[5] * grouped_moe(hs, router_w, router_bias, moe_w_in[l], moe_w_out[l],
                                      shared_w_in[l], shared_w_out[l])
    return (xp, xs, jnp.stack(new_a_k, axis=1), jnp.stack(new_a_v, axis=1),
            jnp.stack(new_ckv, axis=1), jnp.stack(new_kr, axis=1), jnp.stack(new_ssd, axis=1))


_drawn_inputs = setup_inputs


def setup_inputs(seed=0):
    import zlib

    import numpy as np

    out = dict(_drawn_inputs(seed))
    spreads = {}
    factors = {'cache_b_krope': 3.628,
     'a_qk_g': 2.764,
     'a_sub_g': 3.7,
     'b_qa_g': 8.0,
     'b_kva_g': 2.897,
     'b_qk_g': 8.0,
     'ssd_d': 16.197,
     'ssd_norm_g': 13.931,
     'cache_a_k': 8.0,
     'cache_a_v': 8.0}
    for name, (base, spread) in spreads.items():
        noise = np.random.default_rng([zlib.crc32(name.encode()), seed]).standard_normal(out[name].shape)
        drawn = base * np.exp(spread * noise) if base else spread * noise
        out[name] = jnp.asarray(drawn.astype(out[name].dtype))
    for name, factor in factors.items():
        out[name] = (out[name] * factor).astype(out[name].dtype)
    return out
```

```python
from contextlib import ExitStack

import numpy as np
import concourse.bass as bass
from concourse import mybir

F32 = mybir.dt.float32
F32R = mybir.dt.float32r
ALU = mybir.AluOpType
ACT = mybir.ActivationFunctionType
AX = mybir.AxisListType

P = 128
D = 1024
KC = D // P
NPROMPT = 128
NLAT = 256
NTOK = NPROMPT + NLAT
TILES = NTOK // P
CLASSES = ((0, NPROMPT), (NPROMPT, NTOK))
DEPTH = 2
GRID_W = 64
ROPE_BASE = 10000.0
EPS = 1e-6
LAM_INIT = 0.8 - 0.6 * 1.0
HEADS = 4
DQK = 64
B_DQK = 192
A_SCALE = 64 ** -0.5
B_SCALE = B_DQK ** -0.5
KEYS = 512
PAST = slice(128, 256)
NEXP = 16
NGRP = 4
SSD_H = 32
SSD_P = 64
SSD_G = 4
XCH = 16
PIECE = 2048
RAW = 3
SPL = 3
JOB_BANKS = 6
MOD_BANK = 7
TURN_BANK = 6
MOD_SETS = 4
MOD_PIECES = 6
MOD_COLS = 1536
EXP_PER_BODY = 4
BODIES = NEXP // EXP_PER_BODY
BODY_SPLITS = 3 * EXP_PER_BODY
BODY_JOBS = 4 * EXP_PER_BODY + KC
BIG = 1e30

_VEC = [("c", 16), ("norm_g", 64), ("gq_a", 1), ("gk_a", 1), ("sub_g", 1), ("bqa_g", 3), ("bkva_g", 2),
        ("gq_bn", 1), ("gq_br", 1), ("gk_bn", 1), ("gk_br", 1), ("rbias", 16), 
        ("conv_w", 72), ("conv_b", 24), ("ssd_d", 16), ("ssd_g", 16), ("dt_bias", 64), ("a_log", 64),
        ("router", 128)]
_KONST = [("ident", 128), ("ones", 128), ("eps", 1), ("one", 1), ("rank16", 16), ("rank4", 4)]
_KATT = [("block", 128), ("rot", 128), ("cos", 256), ("sin", 256)]
_KSSD = [("upto", 128), ("since", 128)]


def offsets(table):
    out, at = {}, 0
    for name, w in table:
        out[name] = (at, at + w)
        at += w
    return out, at


VEC, VEC_W = offsets(_VEC)
KONST, KONST_W = offsets(_KONST)
KATT, KATT_W = offsets(_KATT)
KSSD, KSSD_W = offsets(_KSSD)

UNITS = [("A", h, t) for h in range(HEADS) for t in range(TILES)] + \
        [("B", h, t) for h in range(HEADS) for t in range(TILES)]
RMS_ORDER = ["aq0", "aq1", "aq2", "aq3", "bq0", "bq1", "bq2", "bq3", "bk0", "bk1", "bk2", "bk3",
             "ak0", "ak1", "ak2", "ak3"]


def numbered(prefix, n):
    return [f"{prefix}{i}" for i in range(n)]


def plan_jobs():
    names = ["norm0"] + numbered("bqc", 3) + ["bkr", "kv0", "kv1", "aq0", "aq1", "N_bqc", "aq2", "aq3", "N_kv"]
    names += numbered("wq", 6) + numbered("kn", 4) + numbered("vb", 4) + numbered("ak", 4)
    names += ["N_" + x for x in RMS_ORDER[:8]] + numbered("va", 3) + ["N_" + x for x in RMS_ORDER[8:]]
    names += numbered("rope", 6)
    for u in range(len(UNITS) + 1):
        if u < len(UNITS):
            names += [f"S{u}_0", f"S{u}_1"] if UNITS[u][0] == "A" else [f"S{u}_0"]
        if u >= 1:
            names.append(f"W{u - 1}")
    names += numbered("N_o", HEADS) + numbered("wo", KC)
    job, at = {}, 0

    def add(more):
        nonlocal at
        for n in more:
            job[n] = at
            at += 1

    def moe(layer):
        nonlocal at
        add([f"norm{2 * layer + 1}", f"router{layer}"] + numbered(f"shu{layer}_", 4) + [f"gt{layer}"] +
            numbered(f"shd{layer}_", KC))
        job[f"body{layer}"] = at
        at += BODIES * BODY_JOBS

    add(names)
    moe(0)
    add(["norm2", "dt"] + numbered("bc", 4) + ["cs0", "cs1"] + ["bc4", "bc5", "csT", "bc6", "bc7"])
    add(numbered("xs", XCH) + numbered("z", XCH))
    for g in range(SSD_G):
        add([f"bt{g}", f"cb{g}"])
        for hg in (2 * g, 2 * g + 1):
            add([f"xt{hg}_0", f"xt{hg}_1", f"st{hg}_0", f"st{hg}_1"] + numbered(f"y{hg}_", TILES))
    add(numbered("N_y", SSD_G) + numbered("so", KC))
    moe(1)
    return job, at


JOB, JOBS = plan_jobs()


def plan_stream():
    body = ["a0", "b0", None, "a1", None, "b1", "a2", None, "b2", None, "a3", "b3", None, "d0", None, "d1", "d2", "d3"]
    last = {}
    stream = [("mod", (0, s, m)) for s in range(2) for m in range(MOD_PIECES)]
    early = [("split", "bqc01", "bqc1"), ("split", "bqc2kr", "bkr"), ("split", "kv01", "kv1"),
             ("split", "aq01", "aq1"), ("split", "aq23", "aq3"), ("plain", "wq012", "wq2"),
             ("plain", "wq345", "wq5"), ("plain", "wkv", "vb3"), ("split", "ak01", "ak1"),
             ("split", "ak23", "ak3"), ("split", "va_lo", "va2"), ("split", "va_hi", "va2")]
    for i, (kind, name, job) in enumerate(early):
        stream += [(kind, name), ("mod", (0, 2 + i // MOD_PIECES, i % MOD_PIECES))]
        last[name] = JOB[job]
    for i in range(4):
        stream.append(("split", f"wo{i}"))
        last[f"wo{i}"] = JOB[f"wo{2 * i + 1}"]
    loops = {}

    def moe(layer):
        for name, job in (("sa", f"shu{layer}_1"), ("sb", f"shu{layer}_3"), ("sd", f"shd{layer}_7")):
            stream.append(("split", f"{name}{layer}"))
            last[f"{name}{layer}"] = JOB[job]
        loops[layer] = len(stream)
        for it in range(BODIES):
            m = 0
            for k, name in enumerate(body):
                if name is None:
                    if layer == 0:
                        stream.append(("mod", (1, it, m)))
                        m += 1
                    continue
                piece = f"{name}_{layer}_{it}"
                stream.append(("split", piece))
                i = int(name[1])
                local = {"a": 4 * i + 1, "b": 4 * i + 3, "d": 4 * EXP_PER_BODY + 2 * i + 1}[name[0]]
                last[piece] = JOB[f"body{layer}"] + it * BODY_JOBS + local

    moe(0)
    ssd = [("dtw", "dt"), ("bc01", "bc1"), ("bc23", "bc3"), ("bc45", "bc5"), ("bc67", "bc7")]
    ssd += [(f"xsw{i}", f"xs{2 * i + 1}") for i in range(8)] + [(f"zw{i}", f"z{2 * i + 1}") for i in range(8)]
    ssd += [(f"sow{i}", f"so{i}") for i in range(KC)]
    for name, job in ssd:
        stream.append(("split", name))
        last[name] = JOB[job]
    moe(1)
    return stream, last, loops


STREAM, LAST_JOB, LOOP_AT = plan_stream()
SPLITS = [name for kind, name in STREAM if kind == "split"]
SPLIT_NO = {name: i for i, name in enumerate(SPLITS)}
AT = {name: i for i, (kind, name) in enumerate(STREAM)}
MODS = [name for kind, name in STREAM if kind == "mod"]
MOD_NO = {name: i for i, name in enumerate(MODS)}
BODY_LEN = {0: BODY_SPLITS + MOD_PIECES, 1: BODY_SPLITS}


def rope_targets(q_a, k_a, q_br, k_br):
    q, ke = slice(NPROMPT, NTOK), slice(2 * P, KEYS)
    return [q_a[:, 0:2, q], q_a[:, 2:4, q], k_a[:, 0:2, ke], k_a[:, 2:4, ke], q_br[:, :, q], k_br[:, :, ke]]


def build(nc, inp, out):
    ctx = ExitStack()
    with ctx:
        base = 16512

        class Map:

            def __init__(self, at, end=229344):
                self.at, self.end = at, end

            def put(self, name, shape, dt=F32):
                t = nc.alloc_sbuf_tensor_at(name, [P] + shape, dt, offset=self.at)
                self.at += (int(np.prod(shape)) * 4 + 31) // 32 * 32
                assert self.at <= self.end, (name, self.at)
                return t

        m = Map(base)
        raw = m.put("raw", [RAW, PIECE])
        whi = m.put("whi", [SPL, PIECE], F32R)
        wlo = m.put("wlo", [SPL, PIECE], F32R)
        x = m.put("x", [KC, NTOK])
        vec = m.put("vec", [VEC_W])
        kon = m.put("kon", [KONST_W])
        modb = m.put("modb", [DEPTH, MOD_SETS, 24])
        mod = m.put("mod", [DEPTH, MOD_SETS, 24])
        gain = m.put("gain", [2 * DEPTH, 2 * KC])
        gq = m.put("gq", [4])
        lam = m.put("lamv", [8])
        low = m.at
        hhi = m.put("hhi", [KC, NTOK], F32R)
        hlo = m.put("hlo", [KC, NTOK], F32R)
        free = m.at
        mn = Map(free)
        sq = mn.put("sq", [2, NTOK])
        rstd = mn.put("rstd", [NTOK])
        xr = mn.put("xr", [2, NTOK])
        h32 = mn.put("h32", [2, NTOK])
        norm_end = mn.at

        ms = Map(229344 - (8 * 32 + 512) * 4 - 64)
        silc = ms.put("silc", [KC, 32])
        modrow = ms.put("modrow", [512])
        top = 229344 - (8 * 32 + 512) * 4 - 64
        ma = Map(free, top)
        katt = ma.put("katt", [KATT_W])
        q_a = ma.put("q_a", [HEADS, NTOK])
        k_a = ma.put("k_a", [HEADS, KEYS])
        v_a = ma.put("v_a", [4, HEADS * P])
        q_b = ma.put("q_b", [HEADS, NTOK])
        q_br = ma.put("q_br", [2, NTOK])
        k_b = ma.put("k_b", [HEADS, KEYS])
        k_br = ma.put("k_br", [2, KEYS])
        v_b = ma.put("v_b", [4, HEADS * P])
        ars = ma.put("ars", [3, KEYS])
        mi = Map(ma.at, top)
        ckv = mi.put("ckv", [2, KEYS])
        kr = mi.put("kr", [KEYS])
        krsq = mi.put("krsq", [KEYS])
        bqc = mi.put("bqc", [3, NTOK])
        asq = mi.put("asq", [6, KEYS])
        mc = Map(ma.at, top)
        stat = mc.put("stat", [2, 8])
        e_sb = mc.put("e_sb", [2, 2, NTOK])
        w_sb = mc.put("w_sb", [2, NTOK])
        wt_sb = mc.put("wt_sb", [2, NTOK])
        o_sb = mc.put("o_sb", [2 * HEADS, NTOK])
        osq = mc.put("osq", [2, NTOK])

        mm = Map(norm_end, top)
        rhi = mm.put("rhi", [KC, NEXP], F32R)
        rlo = mm.put("rlo", [KC, NEXP], F32R)
        rt = mm.put("rt", [14, TILES * NEXP])
        gt_sb = mm.put("gt_sb", [NTOK])
        gbc = mm.put("gbc", [NEXP, NTOK])
        sg = mm.put("sg", [2, NTOK])
        p1 = mm.put("p1", [2, NTOK])
        p2 = mm.put("p2", [2, NTOK])
        hidhi = mm.put("hidhi", [KC, NTOK], F32R)
        hidlo = mm.put("hidlo", [KC, NTOK], F32R)

        mz = Map(free)
        z = mz.put("z", [XCH, NTOK])
        xf = mz.put("xf", [XCH, NTOK])
        mzz = Map(free)
        yhi = mzz.put("yhi", [XCH, NTOK], F32R)
        ylo = mzz.put("ylo", [XCH, NTOK], F32R)
        bc = mz.put("bc", [8, NTOK])
        kssd = mz.put("kssd", [KSSD_W])
        dts = mz.put("dts", [8, TILES * 64])
        mw = Map(mz.at)
        kcum = mw.put("kcum", [2, P])
        acsT = mw.put("acsT", [NTOK])
        cv = mw.put("cv", [2, 388])
        ct = mw.put("ct", [2, 388])
        mk = Map(mz.at)
        s0 = mk.put("s0", [2, 512])
        s1 = mk.put("s1", [512])
        pf = mk.put("pf", [512])
        xw = mk.put("xw", [4, 256])
        rowb = mk.put("rowb", [2, 2, 512])
        seg = mk.put("seg", [2, 2, 512])
        mh = Map(low, free)
        ce = mh.put("ce", [2, 2, 512])
        xtok = mh.put("xtok", [2, TILES, 256])
        btok = mh.put("btok", [TILES, P])
        cbm = mh.put("cbm", [2, TILES, P])
        xdt = mh.put("xdt", [2, 2, 256])
        mg = Map(low, free)
        ysq = mg.put("ysq", [2, NTOK])
        yrs = mg.put("yrs", [NTOK])

        squares = [sq, sq, sq, ysq]

        bank = [ctx.enter_context(nc.psum_tensor(f"bank{i}", [P, 512], F32)) for i in range(8)]

        gates_dram = nc.dram_tensor("gates_rows", [DEPTH, NEXP, NTOK], F32).ap()
        acs_dram = nc.dram_tensor("acs_rows", [64, NTOK], F32).ap()

        def sem(name):
            return ctx.enter_context(nc.semaphore(name))

        raw_in = [sem(f"raw_in{i}") for i in range(RAW)]
        hi_done, lo_done, mod_used = sem("hi_done"), sem("lo_done"), sem("mod_used")
        jobs_done = sem("jobs_done")
        bank_taken = [sem(f"bank_taken{i}") for i in range(JOB_BANKS)]
        tables_in, x_in, katt_in, cache_in, kssd_in = (
            sem("tables_in"), sem("x_in"), sem("katt_in"), sem("cache_in"), sem("kssd_in"))
        silc_zero, silc_ready = sem("silc_zero"), sem("silc_ready")
        modrow_ready, mod_turned, mod_ready = sem("modrow_ready"), sem("mod_turned"), sem("mod_ready")
        sq_ready, sq_used, h32_ready, hhi_ready, hlo_ready = (
            sem("sq_ready"), sem("sq_used"), sem("h32_ready"), sem("hhi_ready"), sem("hlo_ready"))
        dve_step = sem("dve_step")
        lam_in, lam_prod, lam_exp = sem("lam_in"), sem("lam_prod"), sem("lam_exp")
        asq_ready, rms_ready, roped = sem("asq_ready"), sem("rms_ready"), sem("roped")
        nmax_ready, w_ready = sem("nmax_ready"), sem("w_ready")
        o_done, o_taken, osq_ready, o_normed, ohi_ready, olo_ready = (
            sem("o_done"), sem("o_taken"), sem("osq_ready"), sem("o_normed"), sem("ohi_ready"), sem("olo_ready"))
        rhi_ready, rlo_ready, gates_ready, gates_out, gates_in = (
            sem("rhi_ready"), sem("rlo_ready"), sem("gates_ready"), sem("gates_out"), sem("gates_in"))
        p2_ready, hid_hi_ready, hid_lo_ready = sem("p2_ready"), sem("hid_hi_ready"), sem("hid_lo_ready")
        dt_biased, dt_exp, dt_ln, dt_ready, acs_out, rowb_in = (
            sem("dt_biased"), sem("dt_exp"), sem("dt_ln"), sem("dt_ready"), sem("acs_out"),
            [sem("rowb_in0"), sem("rowb_in1")])
        pads_ready, conv_ready, conv_out = sem("pads_ready"), sem("conv_ready"), sem("conv_out")
        wdt_ready, xw_ready, cb_ready, s0_in, s0_decayed, s1_ready, pf_out = (
            sem("wdt_ready"), sem("xw_ready"), sem("cb_ready"), [sem("s0_in0"), sem("s0_in1")], sem("s0_decayed"), sem("s1_ready"),
            sem("pf_out"))
        seg_ready, seg_exp, seg_masked, row_exp, ce_ready, xdt_ready, y_ready = (
            sem("seg_ready"), sem("seg_exp"), sem("seg_masked"), sem("row_exp"), sem("ce_ready"),
            sem("xdt_ready"), sem("y_ready"))
        ysq_ready, ysq_used, yn_ready, yhi_ready, ylo_ready = (
            sem("ysq_ready"), sem("ysq_used"), sem("yn_ready"), sem("yhi_ready"), sem("ylo_ready"))
        stores = sem("stores")

        def v(name, i=0, n=None):
            a, b = VEC[name]
            return vec[:, a + i:(a + i + n if n else b)]

        def k(name, i=0, n=None):
            a, b = KONST[name]
            return kon[:, a + i:(a + i + n if n else b)]

        def ka(name):
            return katt[:, KATT[name][0]:KATT[name][1]]

        def ks(name):
            return kssd[:, KSSD[name][0]:KSSD[name][1]]

        def modcol(layer, section, kc, cls):
            j = (section * KC + kc) * 2 + cls
            return mod[:, layer, j // 24, j % 24:j % 24 + 1]

        def counted(n, it=None, per=0):
            return n if it is None else it * per + n

        def finished(eng, job, it=None):
            eng.wait_ge(jobs_done, counted(job + 1, it, BODY_JOBS))

        def taken(eng, job, it=None):
            eng.wait_ge(bank_taken[job % JOB_BANKS], counted(job // JOB_BANKS + 1, it, BODY_JOBS // JOB_BANKS))

        def bk(job):
            return bank[job % JOB_BANKS]

        def took(ins, job):
            ins.then_inc(bank_taken[job % JOB_BANKS], 1)

        def piece(t, name):
            return t[:, SPLIT_NO[name] % SPL, :]

        block = ctx.enter_context(nc.Block())

        @block.sync
        def _(sp):
            def load(pos, it=None, per=0):
                if pos >= RAW:
                    kind, name = STREAM[pos - RAW]
                    if kind == "mod":
                        sp.wait_ge(mod_used, counted(MOD_NO[name] + 1, it, MOD_PIECES))
                    elif kind == "split":
                        sp.wait_ge(lo_done, counted(SPLIT_NO[name] + 1, it, BODY_SPLITS))
                    else:
                        finished(sp, LAST_JOB[name])
                src = inp["stream"][pos] if it is None else inp["stream"][it * per + pos]
                sp.dma_start(raw[:, pos % RAW, :], src).then_inc(raw_in[pos % RAW], 16)

            def moe(layer):
                at, n = LOOP_AT[layer], BODY_LEN[layer]
                with sp.Fori(0, BODIES) as it:
                    for pos in range(at, at + n):
                        load(pos, it, n)
                return at + BODIES * n

            for pos in range(LOOP_AT[0]):
                load(pos)
            after = moe(0)
            for pos in range(after, LOOP_AT[1]):
                load(pos)
            moe(1)
            last = JOB["body1"] + BODIES * BODY_JOBS - KC
            for kc in range(KC):
                taken(sp, last + kc)
                sp.dma_start(out["yT"][:, kc, :], x[:, kc, :]).then_inc(stores, 16)
            sp.wait_ge(stores, 16 * (KC + 4))

        @block.gpsimd
        def _(pool):
            def low_part(q, it=None):
                pool.wait_ge(hi_done, counted(q + 1, it, BODY_SPLITS))
                pos = AT[SPLITS[q]]
                pool.tensor_tensor(wlo[:, q % SPL, :], raw[:, pos % RAW, :], whi[:, q % SPL, :].bitcast(F32),
                                   ALU.subtract).then_inc(lo_done, 1)

            def moe(layer):
                q = SPLIT_NO[f"a0_{layer}_0"]
                with pool.Fori(0, BODIES) as it:
                    for i in range(BODY_SPLITS):
                        low_part(q + i, it)

            for q in range(SPLIT_NO["a0_0_0"]):
                low_part(q)
            moe(0)
            first_so = SPLIT_NO["sow0"]
            for q in range(SPLIT_NO["dtw"], first_so + SPL):
                low_part(q)

            dt3 = dts[:, 0, :].rearrange("p (t d) -> p t d", t=TILES)
            wdt3 = dts[:, 4, :].rearrange("p (t d) -> p t d", t=TILES)
            pool.wait_ge(wdt_ready, 1)
            for hg in range(2 * SSD_G):
                taken(pool, JOB[f"xt{hg}_1"])
                if hg:
                    finished(pool, JOB[f"st{hg - 1}_1"])
                for i, (t, dr) in enumerate(((0, 0), (0, 1), (1, 0), (2, 1))):
                    h = dr * 32 + 4 * hg
                    pool.tensor_tensor(
                        xw[:, i, :].rearrange("p (h d) -> p h d", h=4),
                        xtok[:, hg % 2, t, :].rearrange("p (h d) -> p h d", h=4),
                        wdt3[:, t, h:h + 4].unsqueeze(2).to_broadcast([P, 4, 64]), ALU.mult).then_inc(xw_ready, 1)
                for t in range(TILES):
                    n = TILES * hg + t
                    if n >= 2:
                        finished(pool, JOB[f"y{(n - 2) // TILES}_{(n - 2) % TILES}"])
                    for dr in range(2):
                        h = dr * 32 + 4 * hg
                        pool.tensor_tensor(
                            xdt[:, n % 2, dr, :].rearrange("p (h d) -> p h d", h=4),
                            xtok[:, hg % 2, t, :].rearrange("p (h d) -> p h d", h=4),
                            dt3[:, t, h:h + 4].unsqueeze(2).to_broadcast([P, 4, 64]), ALU.mult).then_inc(xdt_ready, 1)
                    if t:
                        for dr in range(2):
                            i = (hg * 2 + t - 1) * 2 + dr
                            pool.wait_ge(row_exp, i + 1)
                            e4 = ce[:, n % 2, dr, :].rearrange("p (h l) -> p h l", h=4)
                            pool.tensor_tensor(
                                e4, e4, bc[:, 4 + hg // 2, t * P:(t + 1) * P].unsqueeze(1).to_broadcast([P, 4, P]),
                                ALU.mult).then_inc(ce_ready, 1)
            for q in range(first_so + SPL, SPLIT_NO["a0_1_0"]):
                low_part(q)
            moe(1)

        @block.scalar
        def _(act):
            def split(q, it=None, ahead=0):
                pos = AT[SPLITS[q]]
                per = 0 if it is None else BODY_LEN[ahead] // RAW
                act.wait_ge(raw_in[pos % RAW], counted(16 * (pos // RAW + 1), it, 16 * per))
                if q >= SPL:
                    finished(act, LAST_JOB[SPLITS[q - SPL]] if it is None or q - SPL >= SPLIT_NO[f"a0_{ahead}_0"]
                             else JOB[f"body{ahead}"] - 1 - (SPLIT_NO[f"a0_{ahead}_0"] - 1 - (q - SPL)) * 2, it)
                act.copy(whi[:, q % SPL, :], raw[:, pos % RAW, :]).then_inc(hi_done, 1)

            nsplit = [0]

            def split_to(name):
                while nsplit[0] <= SPLIT_NO[name]:
                    split(nsplit[0])
                    nsplit[0] += 1

            def mod_rows(s):
                act.wait_ge(mod_used, MOD_PIECES * (s + 1))
                if s:
                    act.wait_ge(mod_turned, s)
                act.copy(modrow[0:96, :], bank[MOD_BANK][0:96, :]).then_inc(modrow_ready, 1)

            def norm(phase, x_jobs):
                for kc in range(KC):
                    if x_jobs is not None:
                        taken(act, x_jobs + kc)
                    if kc >= 2:
                        act.wait_ge(sq_used, (KC - 1) * phase + kc - 1)
                    act.activation(squares[phase][:, kc % 2, :], x[:, kc, :], ACT.Square).then_inc(sq_ready, 1)
                n = JOB[f"norm{phase}"]
                finished(act, n)
                took(act.activation(rstd[:, :], bk(n)[:, 0:NTOK], ACT.Sqrt, bias=k("eps"), scale=1.0 / D), n)

            def norm_hi(phase):
                for kc in range(KC):
                    act.wait_ge(h32_ready, KC * phase + kc + 1)
                    act.copy(hhi[:, kc, :], h32[:, kc % 2, :]).then_inc(hhi_ready, 1)

            def out_of(job, *pairs):
                finished(act, JOB[job])
                for dst, src in pairs[:-1]:
                    act.copy(dst, src)
                took(act.copy(*pairs[-1]), JOB[job])

            act.dma_start(vec[:, :], inp["vec"]).then_inc(tables_in, 16)
            act.dma_start(kon[:, :], inp["kon"]).then_inc(tables_in, 16)
            act.dma_start(modb[:, :, :, :], inp["modb"]).then_inc(tables_in, 16)
            act.dma_start(x[:, :, :], inp["xT"]).then_inc(x_in, 16)
            act.dma_start(asq[:, 2, 0:256], inp["lam"]).then_inc(lam_in, 16)
            act.wait_ge(tables_in, 48)
            act.wait_ge(silc_zero, 1)
            act.activation(silc[:, :, 0:2], v("c").rearrange("p (k c) -> p k c", c=2), ACT.Silu).then_inc(silc_ready, 1)
            act.wait_ge(x_in, 16)
            norm(0, None)
            act.wait_ge(lam_prod, 2)
            act.activation(lam[:, 2:4], lam[:, 0:2], ACT.Exp).then_inc(lam_exp, 1)
            mod_rows(0)
            split_to("bqc01")
            mod_rows(1)
            split_to("bqc2kr")
            norm_hi(0)
            act.wait_ge(hlo_ready, KC)
            act.dma_start(katt[:, :], inp["katt"]).then_inc(katt_in, 16)
            act.dma_start(k_a[:, :, PAST], inp["cache_ak"]).then_inc(cache_in, 16)
            act.dma_start(v_a[:, 1, :], inp["cache_av"]).then_inc(cache_in, 16)
            act.dma_start(ckv[:, :, PAST], inp["cache_ckv"]).then_inc(cache_in, 16)
            act.dma_start(kr[:, PAST], inp["cache_kr"]).then_inc(cache_in, 16)

            def b(job, w=NTOK):
                return bk(JOB[job])[:, 0:w]

            def to_keys(dst, job):
                return ((dst[:, 0:NPROMPT], b(job)[:, 0:NPROMPT]), (dst[:, 2 * P:KEYS], b(job)[:, NPROMPT:NTOK]))

            rms_no = [0]

            def root(job, width, feats):
                i = rms_no[0]
                rms_no[0] += 1
                if i >= 3:
                    act.wait_ge(rms_ready, i - 2)
                finished(act, JOB[job])
                took(act.activation(ars[:, i % 3, 0:width], b(job, width), ACT.Sqrt, bias=k("eps"), scale=1.0 / feats),
                     JOB[job])

            split_to("kv01")
            out_of("bqc0", (bqc[:, 0, :], b("bqc0")))
            out_of("bqc1", (bqc[:, 1, :], b("bqc1")))
            split_to("aq01")
            out_of("bqc2", (bqc[:, 2, :], b("bqc2")))
            out_of("bkr", *to_keys(kr, "bkr"))
            split_to("aq23")
            out_of("kv0", *to_keys(ckv[:, 0, :], "kv0"))
            out_of("kv1", *to_keys(ckv[:, 1, :], "kv1"))
            out_of("aq0", (q_a[:, 0, :], b("aq0")))
            out_of("aq1", (q_a[:, 1, :], b("aq1")))
            root("N_bqc", NTOK, 384)
            out_of("aq2", (q_a[:, 2, :], b("aq2")))
            out_of("aq3", (q_a[:, 3, :], b("aq3")))
            root("N_kv", NTOK, 256)
            mod_rows(2)
            for j in range(4):
                out_of(f"wq{j}", (q_b[:, j, :], b(f"wq{j}")))
            for j in range(2):
                out_of(f"wq{4 + j}", (q_br[:, j, :], b(f"wq{4 + j}")))
            for h in range(HEADS):
                out_of(f"kn{h}", (k_b[:, h, :], b(f"kn{h}", KEYS)))
            split_to("ak01")
            for s in range(4):
                out_of(f"vb{s}", (v_b[:, s, :], b(f"vb{s}", KEYS)))
            split_to("ak23")
            split_to("va_lo")
            for h in range(2):
                out_of(f"ak{h}", *to_keys(k_a[:, h, :], f"ak{h}"))
            split_to("va_hi")
            for h in range(2, 4):
                out_of(f"ak{h}", *to_keys(k_a[:, h, :], f"ak{h}"))
            for name in RMS_ORDER[:8]:
                root("N_" + name, NTOK, DQK if name[0] == "a" else B_DQK)
            for t, slot in enumerate((0, 2, 3)):
                out_of(f"va{t}", (v_a[:, slot, :], b(f"va{t}", HEADS * P)))
            mod_rows(3)
            split_to("wo2")
            for name in RMS_ORDER[8:]:
                root("N_" + name, NTOK if name[0] == "a" else KEYS, DQK if name[0] == "a" else B_DQK)
            act.wait_ge(rms_ready, 2 + len(RMS_ORDER))
            taken(act, JOB["va2"])
            act.dma_start(out["new_ak"], k_a[:, :, 0:NPROMPT]).then_inc(stores, 16)
            act.dma_start(out["new_av"], v_a[:, 0, :]).then_inc(stores, 16)
            act.dma_start(out["new_ckv"], ckv[:, :, 0:NPROMPT]).then_inc(stores, 16)
            act.dma_start(out["new_kr"], kr[0:64, 0:NPROMPT]).then_inc(stores, 16)
            act.wait_ge(stores, 64)

            for u in range(len(UNITS) + 1):
                if u < len(UNITS):
                    kind, h, t = UNITS[u]
                    nk = NPROMPT if t == 0 else NTOK
                    act.wait_ge(nmax_ready, u + 1)
                    if u >= 2:
                        act.wait_ge(w_ready, u - 1)
                    for i in range(2 if kind == "A" else 1):
                        job = JOB[f"S{u}_{i}"]
                        took(act.activation(e_sb[:, u % 2, i, 0:nk], bk(job)[:, 0:nk], ACT.Exp,
                                            bias=stat[:, u % 2, i:i + 1], scale=1.0,
                                            accum_out=stat[:, u % 2, 2 + i:3 + i]), job)
                if u >= 1:
                    kind, h, t = UNITS[u - 1]
                    nk = NPROMPT if t == 0 else NTOK
                    job = JOB[f"W{u - 1}"]
                    finished(act, job)
                    took(act.copy(wt_sb[:, (u - 1) % 2, 0:nk], bk(job)[:, 0:nk]), job)
                    e = (u - 1) // TILES
                    if (u - 1) % TILES == 1 and e >= 1:
                        act.wait_ge(o_done, e)
                        act.copy(o_sb[:, e - 1, :], bank[6 + (e - 1) % 2][:, 0:NTOK]).then_inc(o_taken, 1)
            e = 2 * HEADS
            act.wait_ge(o_done, e)
            act.copy(o_sb[:, e - 1, :], bank[6 + (e - 1) % 2][:, 0:NTOK]).then_inc(o_taken, 1)
            for h in range(HEADS):
                act.wait_ge(o_taken, HEADS + h + 1)
                act.copy(hhi[:, HEADS + h, :], o_sb[:, HEADS + h, :]).then_inc(ohi_ready, 1)
            for h in range(HEADS):
                i = rms_no[0]
                rms_no[0] += 1
                if h >= 3:
                    act.wait_ge(o_normed, h - 2)
                n = JOB[f"N_o{h}"]
                finished(act, n)
                took(act.activation(ars[:, i % 3, 0:NTOK], bk(n)[:, 0:NTOK], ACT.Sqrt, bias=k("eps"), scale=1.0 / P), n)
            for h in range(HEADS):
                act.wait_ge(o_normed, h + 1)
                act.copy(hhi[:, h, :], o_sb[:, h, :]).then_inc(ohi_ready, 1)

            def moe(layer, x_jobs):
                phase = 2 * layer + 1
                split_to(f"sb{layer}")
                norm(phase, x_jobs)
                act.copy(rhi[:, :, :], v("router").rearrange("p (k e) -> p k e", e=NEXP)).then_inc(rhi_ready, 1)
                norm_hi(phase)
                n = JOB[f"router{layer}"]
                finished(act, n)
                took(act.activation(rt[:, 0, :], bk(n)[:, 0:TILES * NEXP], ACT.Sigmoid), n)
                split_to(f"sd{layer}")

                def gate_half(job, i, it):
                    finished(act, job, it)
                    taken(act, job - 3, it)
                    took(act.activation(sg[:, i % 2, :], bk(job)[:, 0:NTOK], ACT.Silu), job)

                def hid_hi(c, count, it=None):
                    act.wait_ge(p2_ready, counted(count, it, 2 * EXP_PER_BODY))
                    act.copy(hidhi[:, c, :], p2[:, c % 2, :]).then_inc(hid_hi_ready, 1)

                for c in range(2):
                    n = JOB[f"shu{layer}_{2 * c}"]
                    finished(act, n)
                    took(act.activation(sg[:, c % 2, :], bk(n)[:, 0:NTOK], ACT.Silu), n)
                for c in range(2):
                    taken(act, JOB[f"shu{layer}_{2 * c + 1}"])
                    act.copy(hidhi[:, c, :], p2[:, c, :]).then_inc(hid_hi_ready, 1)
                n = JOB[f"gt{layer}"]
                finished(act, n)
                took(act.copy(gt_sb[0:NEXP, :], bk(n)[0:NEXP, 0:NTOK]), n)
                taken(act, n)
                act.dma_start(gates_dram[layer], gt_sb[0:NEXP, :]).then_inc(gates_out, 16)
                act.wait_ge(gates_out, 16 * (layer + 1))
                for e in range(0, NEXP, 4):
                    act.dma_start(gbc[:, e:e + 4, :], gates_dram[layer, e:e + 4, :].partition_broadcast(P)).then_inc(
                        gates_in, 16)
                n0, q0 = JOB[f"body{layer}"], SPLIT_NO[f"a0_{layer}_0"]
                with act.Fori(0, BODIES) as it:
                    split(q0, it, layer)
                    split(q0 + 1, it, layer)
                    for i in range(BODY_SPLITS):
                        if i + 2 < BODY_SPLITS:
                            split(q0 + i + 2, it, layer)
                        if i < 2 * EXP_PER_BODY:
                            gate_half(n0 + 2 * i, i, it)
                            if i >= 1:
                                hid_hi(i - 1, layer * 2 * NEXP + i, it)
                        if i == 2 * EXP_PER_BODY:
                            hid_hi(i - 1, layer * 2 * NEXP + i, it)
                    if layer == 0:
                        act.wait_ge(mod_used, it * MOD_PIECES + MOD_PIECES * (MOD_SETS + 1))
                        act.wait_ge(mod_turned, it + MOD_SETS)
                        act.copy(modrow[0:96, :], bank[MOD_BANK][0:96, :]).then_inc(modrow_ready, 1)
                nsplit[0] = q0 + BODIES * BODY_SPLITS

            split_to("wo3")
            moe(0, JOB["wo0"])

            split_to("bc23")
            norm(2, JOB["body0"] + BODIES * BODY_JOBS - KC)
            act.dma_start(kssd[:, :], inp["kssd"]).then_inc(kssd_in, 16)
            act.dma_start(kcum[:, :, :], inp["kcum"]).then_inc(kssd_in, 16)
            norm_hi(2)
            split_to("bc01")
            act.activation(dts[:, 7, 0:64], v("a_log"), ACT.Exp).then_inc(dt_exp, 1)

            def conv_in(job, i):
                if i >= 2:
                    act.wait_ge(conv_ready, i - 1)
                finished(act, job)
                act.copy(cv[:, i % 2, 1:1 + NPROMPT], bk(job)[:, 0:NPROMPT])
                took(act.copy(cv[:, i % 2, 2 + NPROMPT:2 + NTOK], bk(job)[:, NPROMPT:NTOK]), job)

            def conv_silu(i, dst, c):
                act.wait_ge(conv_ready, i + 1)
                bias = v("conv_b", c, 1)
                act.activation(dst[:, 0:NPROMPT], ct[:, i % 2, 0:NPROMPT], ACT.Silu, bias=bias)
                act.activation(dst[:, NPROMPT:NTOK], ct[:, i % 2, NPROMPT + 1:NTOK + 1], ACT.Silu,
                               bias=bias).then_inc(conv_out, 1)

            act.wait_ge(pads_ready, 1)
            chunk = [(JOB[f"bc{i}"], bc[:, i, :], XCH + i) for i in range(8)]
            chunk += [(JOB[f"xs{i}"], xf[:, i, :], i) for i in range(XCH)]

            def conv_step(i):
                if i < len(chunk):
                    conv_in(chunk[i][0], i)
                if 1 <= i:
                    conv_silu(i - 1, chunk[i - 1][1], chunk[i - 1][2])

            act.wait_ge(dt_biased, 1)
            act.activation(dts[:, 2, :], dts[:, 1, :], ACT.Exp, scale=-1.0).then_inc(dt_exp, 1)
            act.wait_ge(dt_biased, 2)
            act.activation(dts[:, 5, :], dts[:, 3, :], ACT.Ln).then_inc(dt_ln, 1)
            split_to("bc23")
            conv_step(0)
            conv_step(1)
            split_to("bc45")
            conv_step(2)
            conv_step(3)
            split_to("bc67")
            n = JOB["cs0"]
            finished(act, n)
            act.activation(dts[:, 6, :], bk(n)[:, 192:384], ACT.Exp)
            took(act.copy(dts[:, 5, :], bk(n)[:, 0:192]), n)
            n = JOB["cs1"]
            finished(act, n)
            took(act.activation(dts[:, 3, :], bk(n)[:, 0:192], ACT.Exp), n)
            conv_step(4)
            conv_step(5)
            split_to("xsw0")
            n = JOB["csT"]
            finished(act, n)
            took(act.copy(acsT[0:64, :], bk(n)[0:64, 0:NTOK]), n)
            taken(act, n)
            act.dma_start(acs_dram, acsT[0:64, :]).then_inc(acs_out, 16)
            conv_step(6)
            conv_step(7)
            for i in range(8):
                split_to(f"xsw{i + 1}" if i < 7 else "zw0")
                conv_step(8 + 2 * i)
                conv_step(9 + 2 * i)
            conv_step(24)
            for i in range(8):
                split_to(f"zw{i + 1}" if i < 7 else "sow0")
                for c in (2 * i, 2 * i + 1):
                    n = JOB[f"z{c}"]
                    finished(act, n)
                    took(act.activation(z[:, c, :], bk(n)[:, 0:NTOK], ACT.Silu), n)
            split_to("sow2")

            def fetch_rows(n):
                hg, t = n // TILES, n % TILES
                if n >= 2:
                    act.wait_ge(seg_ready, 2 * (n - 1))
                for dr in range(2):
                    h = dr * 32 + 4 * hg
                    act.dma_start(rowb[:, n % 2, dr, :].rearrange("p (h l) -> p h l", h=4),
                                  acs_dram[h:h + 4, t * P:(t + 1) * P].partition_broadcast(P)).then_inc(
                        rowb_in[n % 2], 16)

            def fetch_state(hg):
                if hg >= 2:
                    finished(act, JOB[f"y{hg - 2}_2"])
                    act.wait_ge(s0_decayed, 2 * (hg - 1))
                act.dma_start(s0[:, hg % 2, :].rearrange("p (r c) -> p r c", r=2),
                              inp["s0T"][:, :, hg * 256:(hg + 1) * 256]).then_inc(s0_in[hg % 2], 16)

            act.wait_ge(acs_out, 16)
            taken(act, JOB["z15"])
            fetch_state(0)
            fetch_rows(0)
            fetch_rows(1)
            nexp = 0
            for g in range(SSD_G):
                out_of(f"bt{g}", (btok[:, :, :], bk(JOB[f"bt{g}"])[:, 0:NTOK].rearrange("p (t n) -> p t n", t=TILES)))
                for hg in (2 * g, 2 * g + 1):
                    out_of(f"xt{hg}_0", (xtok[:, hg % 2, 0:2, :],
                                         bk(JOB[f"xt{hg}_0"])[:, 0:512].rearrange("p (t c) -> p t c", t=2)))
                    out_of(f"xt{hg}_1", (xtok[:, hg % 2, 2, :], bk(JOB[f"xt{hg}_1"])[:, 0:256]))
                    if hg + 1 < 2 * SSD_G:
                        fetch_state(hg + 1)
                    if hg:
                        act.wait_ge(pf_out, 32 * hg)
                    out_of(f"st{hg}_0", (pf[:, :], bk(JOB[f"st{hg}_0"])[:, 0:512]))
                    taken(act, JOB[f"st{hg}_0"])
                    for dr in range(2):
                        act.dma_start(out["new_s"][:, dr, hg * 256:(hg + 1) * 256],
                                      pf[:, dr * 256:(dr + 1) * 256]).then_inc(pf_out, 16)
                    for t in range(TILES):
                        n = TILES * hg + t
                        if t:
                            for dr in range(2):
                                act.wait_ge(seg_ready, 2 * n + dr + 1)
                                act.activation(ce[:, n % 2, dr, :], rowb[:, n % 2, dr, :], ACT.Exp).then_inc(row_exp, 1)
                                nexp += 1
                        for dr in range(2):
                            act.wait_ge(seg_ready, 2 * n + dr + 1)
                            act.activation(seg[:, n % 2, dr, :], seg[:, n % 2, dr, :], ACT.Exp).then_inc(seg_exp, 1)
                        if t:
                            act.wait_ge(row_exp, nexp)
                        if n + 2 < 6 * SSD_G:
                            fetch_rows(n + 2)
            act.wait_ge(y_ready, 2 * SSD_G * TILES)
            for g in range(SSD_G):
                for c in range(4 * g, 4 * g + 4):
                    if c >= 2 and (c - 2) % 4 == 3:
                        finished(act, JOB[f"N_y{(c - 2) // 4}"])
                    elif c >= 2:
                        act.wait_ge(ysq_used, 3 * ((c - 2) // 4) + (c - 2) % 4 + 1)
                    act.activation(ysq[:, c % 2, :], xf[:, c, :], ACT.Square).then_inc(ysq_ready, 1)
                n = JOB[f"N_y{g}"]
                finished(act, n)
                if g:
                    act.wait_ge(yn_ready, 4 * g)
                took(act.activation(yrs[:, :], bk(n)[:, 0:NTOK], ACT.Sqrt, bias=k("eps"), scale=1.0 / 512), n)
                for c in range(4 * g, 4 * g + 4):
                    act.wait_ge(yn_ready, c + 1)
                    act.copy(yhi[:, c, :], xf[:, c, :]).then_inc(yhi_ready, 1)
            for i in range(3, KC):
                split_to(f"sow{i}")
            split_to("sa1")
            act.wait_ge(pf_out, 32 * 2 * SSD_G)
            moe(1, JOB["so0"])

        @block.vector
        def _(dve):
            steps = [0]

            def step(ins):
                ins.then_inc(dve_step, 1)
                steps[0] += 1

            def settle():
                dve.wait_ge(dve_step, steps[0])

            def add_mod(layer, s, it=None):
                turned = bank[TURN_BANK][:, 0:384].rearrange("p (q g c) -> p g q c", q=4, g=3)[:, :, :, 0:2]
                which = s if it is None else it
                dst = mod[:, layer, which, :].rearrange("p (g q c) -> p g q c", g=3, q=4)
                add = modb[:, layer, which, :].rearrange("p (g q c) -> p g q c", g=3, q=4)
                dve.wait_ge(mod_turned, counted(layer * MOD_SETS + s + 1, it, 1))
                dve.tensor_tensor(dst, turned, add, ALU.add).then_inc(mod_ready, 1)

            def gains(phase):
                layer, which = divmod(phase, 2)
                for half in range(2):
                    j = ((3 * which + 1) * KC * 2 + half * KC)
                    step(dve.scalar_tensor_tensor(
                        gain[:, phase, half * KC:(half + 1) * KC], mod[:, layer, j // 24, j % 24:j % 24 + KC], 1.0,
                        v("norm_g", phase * 2 * KC + half * KC, KC), ALU.add, ALU.mult))
                settle()

            def norm(phase):
                layer, which = divmod(phase, 2)
                taken(dve, JOB[f"norm{phase}"])
                step(dve.reciprocal(rstd[:, :], rstd[:, :]))
                settle()
                for kc in range(KC + 1):
                    if kc < KC:
                        step(dve.tensor_tensor(xr[:, kc % 2, :], x[:, kc, :], rstd[:, :], ALU.mult))
                        settle()
                        for cls, (a, e) in enumerate(CLASSES):
                            ins = dve.tensor_scalar(h32[:, kc % 2, a:e], xr[:, kc % 2, a:e],
                                                    gain[:, phase, 2 * kc + cls:2 * kc + cls + 1],
                                                    modcol(layer, 3 * which, kc, cls), ALU.mult, ALU.add)
                        ins.then_inc(h32_ready, 1)
                    if kc >= 1:
                        dve.wait_ge(hhi_ready, KC * phase + kc)
                        dve.tensor_tensor(hlo[:, kc - 1, :], h32[:, (kc - 1) % 2, :], hhi[:, kc - 1, :].bitcast(F32),
                                          ALU.subtract).then_inc(hlo_ready, 1)

            dve.memset(silc[:, :, :], 0.0).then_inc(silc_zero, 1)
            dve.wait_ge(tables_in, 48)
            dve.wait_ge(lam_in, 16)
            lam4 = asq[:, 2, 0:256].rearrange("p (a d) -> p a d", a=4)
            for i in range(2):
                step(dve.tensor_tensor(asq[:, i, 0:64], lam4[:, 2 * i, :], lam4[:, 2 * i + 1, :],
                                       ALU.mult))
            settle()
            for i in range(2):
                dve.tensor_reduce(lam[:, i:i + 1], asq[:, i, 0:64], AX.X, ALU.add).then_inc(
                    lam_prod, 1)
            for i, (name, f) in enumerate((("gq_a", A_SCALE), ("gq_bn", B_SCALE), ("gq_br", B_SCALE),
                                           ("sub_g", 1.0 - LAM_INIT))):
                step(dve.tensor_scalar(gq[:, i:i + 1], v(name), f, None, ALU.mult))
            dve.wait_ge(lam_exp, 1)
            step(dve.tensor_tensor(lam[:, 4:5], lam[:, 2:3], lam[:, 3:4], ALU.subtract))
            settle()
            step(dve.tensor_scalar(lam[:, 5:6], lam[:, 4:5], LAM_INIT, None, ALU.add))
            add_mod(0, 0)
            add_mod(0, 1)
            dve.wait_ge(mod_ready, 2)
            gains(0)
            norm(0)

            releases = []

            def square(src, w, norm_job, dst=None):
                i = len(releases)
                if dst is None:
                    if i >= 6:
                        finished(dve, JOB[releases[i - 6]])
                    releases.append(norm_job)
                    dst = asq[:, i % 6, 0:w]
                dve.tensor_tensor(dst, src, src, ALU.mult).then_inc(asq_ready, 1)

            roots = [0]

            def scaled(job, width, items):
                i = roots[0]
                roots[0] += 1
                taken(dve, JOB[job])
                r = ars[:, i % 3, 0:width]
                step(dve.reciprocal(r, r))
                settle()
                for j, (dst, src, g, r0, c0, c1) in enumerate(items):
                    ins = dve.scalar_tensor_tensor(dst, src, g, ars[r0:r0 + dst.shape[0], i % 3, c0:c1],
                                                   ALU.mult, ALU.mult)
                    if j == len(items) - 1:
                        ins.then_inc(rms_ready, 1)

            for c in range(3):
                taken(dve, JOB[f"bqc{c}"])
                square(bqc[:, c, :], NTOK, "N_bqc")
            dve.wait_ge(cache_in, 64)
            taken(dve, JOB["bkr"])
            square(kr[:, :], KEYS, None, krsq[:, :])
            for c in range(2):
                taken(dve, JOB[f"kv{c}"])
                i = len(releases)
                releases.append("N_kv")
                dve.tensor_tensor(asq[:, i % 6, 0:NPROMPT], ckv[:, c, 0:NPROMPT], ckv[:, c, 0:NPROMPT], ALU.mult)
                dve.tensor_tensor(asq[:, i % 6, NPROMPT:NTOK], ckv[:, c, 2 * P:KEYS], ckv[:, c, 2 * P:KEYS],
                                  ALU.mult).then_inc(asq_ready, 1)
            for h in range(2):
                taken(dve, JOB[f"aq{h}"])
                square(q_a[:, h, :], NTOK, f"N_aq{h}")
            scaled("N_bqc", NTOK, [(bqc[:, c, :], bqc[:, c, :], v("bqa_g", c, 1), 0, 0, NTOK) for c in range(3)])
            for h in range(2, 4):
                taken(dve, JOB[f"aq{h}"])
                square(q_a[:, h, :], NTOK, f"N_aq{h}")
            scaled("N_kv", NTOK, [(ckv[:, c, ka_:kb_], ckv[:, c, ka_:kb_], v("bkva_g", c, 1), 0, ra, rb)
                                  for c in range(2) for ka_, kb_, ra, rb in ((0, 128, 0, 128), (256, 512, 128, 384))])
            add_mod(0, 2)
            for j in range(4):
                taken(dve, JOB[f"wq{j}"])
                square(q_b[:, j, :], NTOK, f"N_bq{j}")
            for j in range(2):
                taken(dve, JOB[f"wq{4 + j}"])
                square(q_br[:, j, :], NTOK, f"N_bq{2 * j + 1}")
            for h in range(HEADS):
                scaled(f"N_aq{h}", NTOK, [(q_a[:, h, :], q_a[:, h, :], gq[:, 0:1], 0, 0, NTOK)])
            for h in range(HEADS):
                taken(dve, JOB[f"kn{h}"])
                square(k_b[:, h, :], KEYS, f"N_bk{h}")
            for h in range(HEADS):
                a, e = 64 * (h % 2), 64 * (h % 2) + 64
                scaled(f"N_bq{h}", NTOK, [
                    (q_b[:, h, :], q_b[:, h, :], gq[:, 1:2], 0, 0, NTOK),
                    (q_br[a:e, h // 2, :], q_br[a:e, h // 2, :], gq[a:e, 2:3], a, 0, NTOK)])
            dve.wait_ge(cache_in, 64)
            for h in range(HEADS):
                taken(dve, JOB[f"ak{h}"])
                i = len(releases)
                finished(dve, JOB[releases[i - 6]])
                releases.append(f"N_ak{h}")
                dve.tensor_tensor(asq[:, i % 6, 0:NPROMPT], k_a[:, h, 0:NPROMPT], k_a[:, h, 0:NPROMPT], ALU.mult)
                dve.tensor_tensor(asq[:, i % 6, NPROMPT:NTOK], k_a[:, h, 2 * P:KEYS], k_a[:, h, 2 * P:KEYS],
                                  ALU.mult).then_inc(asq_ready, 1)
            for h in range(HEADS):
                a, e = 64 * (h % 2), 64 * (h % 2) + 64
                scaled(f"N_bk{h}", KEYS, [
                    (k_b[:, h, :], k_b[:, h, :], v("gk_bn"), 0, 0, KEYS),
                    (k_br[a:e, h // 2, :], kr[a:e, :], v("gk_br")[a:e, :], a, 0, KEYS)])
            for h in range(HEADS):
                scaled(f"N_ak{h}", NTOK, [(k_a[:, h, ka_:kb_], k_a[:, h, ka_:kb_], v("gk_a"), 0, ra, rb)
                                          for ka_, kb_, ra, rb in ((0, 128, 0, 128), (256, 512, 128, 384))])
            add_mod(0, 3)
            dve.wait_ge(katt_in, 16)
            cos2 = ka("cos").unsqueeze(1).to_broadcast([P, 2, NLAT])
            sin2 = ka("sin").unsqueeze(1).to_broadcast([P, 2, NLAT])
            dve.wait_ge(rms_ready, 2 + len(RMS_ORDER))
            for i, tgt in enumerate(rope_targets(q_a, k_a, q_br, k_br)):
                n = JOB[f"rope{i}"]
                finished(dve, n)
                tmp = asq[:, i % 2, :].rearrange("p (a l) -> p a l", a=2)
                took(dve.tensor_tensor(tmp, bk(n)[:, :].rearrange("p (a l) -> p a l", a=2), sin2, ALU.mult), n)
                step(dve.tensor_tensor(tgt, tgt, cos2, ALU.mult))
                settle()
                taken(dve, n)
                dve.tensor_tensor(tgt, tgt, tmp, ALU.add).then_inc(roped, 1)

            dve.wait_ge(stores, 64)
            dve.wait_ge(roped, 6)
            for u in range(len(UNITS) + 1):
                if u < len(UNITS):
                    kind, h, t = UNITS[u]
                    nk = NPROMPT if t == 0 else NTOK
                    maps = 2 if kind == "A" else 1
                    for i in range(maps):
                        job = JOB[f"S{u}_{i}"]
                        finished(dve, job)
                        ins = dve.tensor_reduce(stat[:, u % 2, i:i + 1], bk(job)[:, 0:nk], AX.X, ALU.max, negate=True)
                    ins.then_inc(nmax_ready, 1)
                if u >= 1:
                    w = u - 1
                    kind, h, t = UNITS[w]
                    nk = NPROMPT if t == 0 else NTOK
                    maps = 2 if kind == "A" else 1
                    st = stat[:, w % 2, :]
                    for i in range(maps):
                        taken(dve, JOB[f"S{w}_{i}"])
                    step(dve.reciprocal(st[:, 4:4 + maps], st[:, 2:2 + maps]))
                    settle()
                    if w >= 2:
                        finished(dve, JOB[f"W{w - 2}"])
                    if kind == "A":
                        step(dve.tensor_tensor(st[:, 6:7], st[:, 5:6], lam[:, 5:6], ALU.mult))
                        settle()
                        step(dve.tensor_scalar(e_sb[:, w % 2, 1, 0:nk], e_sb[:, w % 2, 1, 0:nk], st[:, 6:7], None,
                                               ALU.mult))
                        settle()
                        dve.scalar_tensor_tensor(w_sb[:, w % 2, 0:nk], e_sb[:, w % 2, 0, 0:nk], st[:, 4:5],
                                                 e_sb[:, w % 2, 1, 0:nk], ALU.mult, ALU.subtract).then_inc(w_ready, 1)
                    else:
                        dve.tensor_scalar(w_sb[:, w % 2, 0:nk], e_sb[:, w % 2, 0, 0:nk], st[:, 4:5], None,
                                          ALU.mult).then_inc(w_ready, 1)
            for h in range(HEADS):
                dve.wait_ge(o_taken, h + 1)
                if h >= 2:
                    finished(dve, JOB[f"N_o{h - 2}"])
                dve.tensor_tensor(osq[:, h % 2, :], o_sb[:, h, :], o_sb[:, h, :], ALU.mult).then_inc(osq_ready, 1)
            for h in range(HEADS):
                i = roots[0]
                roots[0] += 1
                taken(dve, JOB[f"N_o{h}"])
                r = ars[:, i % 3, 0:NTOK]
                step(dve.reciprocal(r, r))
                settle()
                dve.scalar_tensor_tensor(o_sb[:, h, :], o_sb[:, h, :], gq[:, 3:4], r, ALU.mult, ALU.mult).then_inc(
                    o_normed, 1)
            for i, h in enumerate([4, 5, 6, 7, 0, 1, 2, 3]):
                dve.wait_ge(ohi_ready, i + 1)
                dve.tensor_tensor(hlo[:, h, :], o_sb[:, h, :], hhi[:, h, :].bitcast(F32), ALU.subtract).then_inc(
                    olo_ready, 1)

            def residual(job, layer, section, kc, it=None):
                finished(dve, job, it)
                for cls, (a, e) in enumerate(CLASSES):
                    ins = dve.scalar_tensor_tensor(x[:, kc, a:e], bk(job)[:, a:e], modcol(layer, section, kc, cls),
                                                   x[:, kc, a:e], ALU.mult, ALU.add)
                took(ins, job)

            def top_experts(layer):
                E = TILES * NEXP
                G = TILES * NGRP

                def col(i, w=E):
                    return rt[:, i, 0:w]

                def e3(i):
                    return rt[:, i, :].rearrange("p (t e) -> p t e", e=NEXP)

                def g3(i):
                    return rt[:, i, :].rearrange("p (g e) -> p g e", e=NGRP)

                def do(ins):
                    step(ins)
                    settle()

                taken(dve, JOB[f"router{layer}"])
                do(dve.tensor_tensor(e3(1), e3(0), v("rbias").unsqueeze(1).to_broadcast([P, TILES, NEXP]), ALU.add))
                s = g3(1)
                pairs = s.rearrange("p g (a b) -> p g a b", a=2)
                hi4 = col(2, 2 * G).rearrange("p (g a) -> p g a", a=2)
                lo4 = col(3, 2 * G).rearrange("p (g a) -> p g a", a=2)
                do(dve.tensor_tensor(hi4, pairs[:, :, :, 0], pairs[:, :, :, 1], ALU.max))
                do(dve.tensor_tensor(lo4, pairs[:, :, :, 0], pairs[:, :, :, 1], ALU.min))
                best, m2, m3 = col(4, G), col(5, G), col(6, G)
                do(dve.tensor_tensor(best, hi4[:, :, 0], hi4[:, :, 1], ALU.max))
                do(dve.tensor_tensor(m2, hi4[:, :, 0], hi4[:, :, 1], ALU.min))
                do(dve.tensor_tensor(m3, lo4[:, :, 0], lo4[:, :, 1], ALU.max))
                do(dve.tensor_tensor(m2, m2, m3, ALU.max))
                do(dve.tensor_tensor(best, best, m2, ALU.add))
                b3 = best.rearrange("p (t g) -> p t g", t=TILES)
                gm = col(5, TILES)
                do(dve.tensor_reduce(gm, b3, AX.X, ALU.max))
                key = col(6, G).rearrange("p (t g) -> p t g", t=TILES)
                do(dve.tensor_tensor(key, b3, gm.unsqueeze(2).to_broadcast([P, TILES, NGRP]), ALU.is_equal))
                do(dve.tensor_tensor(key, key, k("rank4").unsqueeze(1).to_broadcast([P, TILES, NGRP]), ALU.mult))
                do(dve.tensor_reduce(gm, key, AX.X, ALU.max))
                do(dve.tensor_tensor(key, key, gm.unsqueeze(2).to_broadcast([P, TILES, NGRP]), ALU.is_equal))
                do(dve.tensor_tensor(g3(7), s, col(6, G).unsqueeze(2).to_broadcast([P, G, NGRP]), ALU.mult))
                do(dve.tensor_scalar(key, key, -1.0, BIG, ALU.add, ALU.mult))
                do(dve.tensor_tensor(g3(7), g3(7), col(6, G).unsqueeze(2).to_broadcast([P, G, NGRP]), ALU.add))
                for one in (8, 9):
                    do(dve.tensor_reduce(gm, e3(7), AX.X, ALU.max))
                    do(dve.tensor_tensor(e3(one), e3(7), gm.unsqueeze(2).to_broadcast([P, TILES, NEXP]), ALU.is_equal))
                    do(dve.tensor_tensor(e3(one), e3(one), k("rank16").unsqueeze(1).to_broadcast([P, TILES, NEXP]),
                                         ALU.mult))
                    do(dve.tensor_reduce(gm, e3(one), AX.X, ALU.max))
                    do(dve.tensor_tensor(e3(one), e3(one), gm.unsqueeze(2).to_broadcast([P, TILES, NEXP]),
                                         ALU.is_equal))
                    if one == 8:
                        do(dve.scalar_tensor_tensor(col(7), col(8), -3.0 * BIG, col(7), ALU.mult, ALU.add))
                do(dve.tensor_tensor(col(8), col(8), col(9), ALU.add))
                do(dve.tensor_tensor(col(8), col(8), col(0), ALU.mult))
                do(dve.tensor_reduce(gm, e3(8), AX.X, ALU.add))
                do(dve.reciprocal(gm, gm))
                dve.tensor_tensor(e3(10), e3(8), gm.unsqueeze(2).to_broadcast([P, TILES, NEXP]), ALU.mult).then_inc(
                    gates_ready, 1)

            def moe(layer):
                phase = 2 * layer + 1
                gains(phase)
                dve.wait_ge(rhi_ready, layer + 1)
                norm(phase)
                dve.tensor_tensor(rlo[:, :, :], v("router").rearrange("p (k e) -> p k e", e=NEXP),
                                  rhi[:, :, :].bitcast(F32), ALU.subtract).then_inc(rlo_ready, 1)
                top_experts(layer)
                pre = layer * (2 + 2 * NEXP)
                for c in range(2):
                    n = JOB[f"shu{layer}_{2 * c + 1}"]
                    taken(dve, n - 1)
                    finished(dve, n)
                    took(dve.tensor_tensor(p2[:, c, :], sg[:, c, :], bk(n)[:, 0:NTOK], ALU.mult), n)
                for c in range(2):
                    dve.wait_ge(hid_hi_ready, pre + c + 1)
                    dve.tensor_tensor(hidlo[:, c, :], p2[:, c, :], hidhi[:, c, :].bitcast(F32),
                                      ALU.subtract).then_inc(hid_lo_ready, 1)
                for kc in range(KC):
                    residual(JOB[f"shd{layer}_{kc}"], layer, 5, kc)
                dve.wait_ge(gates_in, 64 * (layer + 1))
                n0 = JOB[f"body{layer}"]
                with dve.Fori(0, BODIES) as it:
                    for c in range(2 * EXP_PER_BODY + 1):
                        if c < 2 * EXP_PER_BODY:
                            n = n0 + 2 * c + 1
                            taken(dve, n - 1, it)
                            finished(dve, n, it)
                            took(dve.tensor_tensor(p1[:, c % 2, :], sg[:, c % 2, :], bk(n)[:, 0:NTOK], ALU.mult), n)
                            taken(dve, n, it)
                            dve.tensor_tensor(p2[:, c % 2, :], p1[:, c % 2, :],
                                              gbc[:, it * EXP_PER_BODY + c // 2, :], ALU.mult).then_inc(p2_ready, 1)
                        if c >= 1:
                            dve.wait_ge(hid_hi_ready, it * 2 * EXP_PER_BODY + pre + 2 + c)
                            dve.tensor_tensor(hidlo[:, c - 1, :], p2[:, (c - 1) % 2, :],
                                              hidhi[:, c - 1, :].bitcast(F32), ALU.subtract).then_inc(hid_lo_ready, 1)
                    for kc in range(KC):
                        residual(n0 + 4 * EXP_PER_BODY + kc, layer, 5, kc, it)
                    if layer == 0:
                        add_mod(1, 0, it)

            dve.wait_ge(mod_ready, 4)
            for kc in range(KC):
                residual(JOB[f"wo{kc}"], 0, 2, kc)
            moe(0)

            dve.wait_ge(mod_ready, 8)
            gains(2)
            norm(2)
            for i in range(2):
                for c in (0, 1 + NPROMPT, 2 + NTOK):
                    ins = dve.memset(cv[:, i, c:c + 1], 0.0)
            ins.then_inc(pads_ready, 1)
            n = JOB["dt"]
            finished(dve, n)
            took(dve.tensor_tensor(dts[:, 0, :].rearrange("p (t d) -> p t d", t=TILES),
                                   bk(n)[:, 0:192].rearrange("p (t d) -> p t d", t=TILES),
                                   v("dt_bias").unsqueeze(1).to_broadcast([P, TILES, 64]), ALU.add), n)
            taken(dve, n)
            dve.scalar_tensor_tensor(dts[:, 1, :], dts[:, 0, :], -1.0, dts[:, 0, :], ALU.mult, ALU.max).then_inc(
                dt_biased, 1)
            dve.wait_ge(dt_exp, 2)
            dve.tensor_scalar(dts[:, 3, :], dts[:, 2, :], 1.0, None, ALU.add).then_inc(dt_biased, 1)
            dve.wait_ge(dt_biased, 2)
            step(dve.tensor_scalar(dts[:, 4, :], dts[:, 3, :], -1.0, None, ALU.add))
            settle()
            step(dve.tensor_scalar(dts[:, 1, :], dts[:, 4, :], 0.0, None, ALU.is_equal))
            settle()
            step(dve.tensor_tensor(dts[:, 4, :], dts[:, 4, :], dts[:, 1, :], ALU.add))
            settle()
            step(dve.reciprocal(dts[:, 4, :], dts[:, 4, :]))
            dve.wait_ge(dt_ln, 1)
            step(dve.tensor_tensor(dts[:, 5, :], dts[:, 5, :], dts[:, 1, :], ALU.add))
            settle()
            step(dve.tensor_tensor(dts[:, 5, :], dts[:, 5, :], dts[:, 4, :], ALU.mult))
            settle()
            step(dve.tensor_tensor(dts[:, 5, :], dts[:, 5, :], dts[:, 2, :], ALU.mult))
            settle()
            step(dve.scalar_tensor_tensor(dts[:, 0, :], dts[:, 0, :], 0.0, dts[:, 5, :], ALU.max, ALU.add))
            settle()
            step(dve.tensor_scalar(dts[:, 7, 0:64], dts[:, 7, 0:64], -1.0, None, ALU.mult))
            settle()
            dve.tensor_tensor(dts[:, 1, :].rearrange("p (t d) -> p t d", t=TILES),
                              dts[:, 0, :].rearrange("p (t d) -> p t d", t=TILES),
                              dts[:, 7, 0:64].unsqueeze(1).to_broadcast([P, TILES, 64]), ALU.mult).then_inc(dt_ready, 1)

            def conv(i):
                job, c = (JOB[f"bc{i}"], XCH + i) if i < 8 else (JOB[f"xs{i - 8}"], i - 8)
                taken(dve, job)
                if i >= 2:
                    dve.wait_ge(conv_out, i - 1)
                w = NTOK + 1
                t = ct[:, i % 2, 0:w]
                step(dve.tensor_scalar(t, cv[:, i % 2, 0:w], v("conv_w", c, 1), None, ALU.mult))
                settle()
                step(dve.scalar_tensor_tensor(t, cv[:, i % 2, 1:1 + w], v("conv_w", 24 + c, 1), t, ALU.mult, ALU.add))
                settle()
                dve.scalar_tensor_tensor(t, cv[:, i % 2, 2:2 + w], v("conv_w", 48 + c, 1), t, ALU.mult,
                                         ALU.add).then_inc(conv_ready, 1)

            for i in range(4):
                conv(i)
            taken(dve, JOB["cs1"])
            dve.tensor_tensor(dts[:, 4, :], dts[:, 3, :], dts[:, 0, :], ALU.mult).then_inc(wdt_ready, 1)
            for i in range(4, 24):
                conv(i)

            def gated(hg, t):
                n = JOB[f"y{hg}_{t}"]
                ts = slice(t * P, (t + 1) * P)
                finished(dve, n)
                for c in range(2):
                    ins = dve.scalar_tensor_tensor(xf[:, 2 * hg + c, ts], xf[:, 2 * hg + c, ts],
                                                   v("ssd_d", 2 * hg + c, 1), bk(n)[:, c * P:(c + 1) * P],
                                                   ALU.mult, ALU.add)
                took(ins, n)
                taken(dve, n)
                both = slice(2 * hg, 2 * hg + 2)
                dve.tensor_tensor(xf[:, both, ts], xf[:, both, ts], z[:, both, ts], ALU.mult).then_inc(y_ready, 1)

            acs3 = dts[:, 5, :].rearrange("p (t d) -> p t d", t=TILES)
            dec3 = dts[:, 6, :].rearrange("p (t d) -> p t d", t=TILES)
            dve.wait_ge(kssd_in, 32)
            for g in range(SSD_G):
                n = JOB[f"cb{g}"]
                finished(dve, n)
                if g:
                    dve.wait_ge(seg_masked, 12 * g)
                c3 = bk(n)[:, 0:NTOK].rearrange("p (t l) -> p t l", t=TILES)
                dve.tensor_tensor(cbm[:, 0, :, :], c3, ks("upto").unsqueeze(1).to_broadcast([P, TILES, P]), ALU.mult)
                took(dve.tensor_tensor(cbm[:, 1, :, :], c3, ks("since").unsqueeze(1).to_broadcast([P, TILES, P]),
                                       ALU.mult), n)
                taken(dve, n)
                for hg in (2 * g, 2 * g + 1):
                    dve.wait_ge(s0_in[hg % 2], 16 * (hg // 2 + 1))
                    if hg:
                        finished(dve, JOB[f"y{hg - 1}_2"])
                    for dr, t in ((0, 1), (1, 2)):
                        h = dr * 32 + 4 * hg
                        ins = dve.tensor_tensor(
                            s1[:, dr * 256:(dr + 1) * 256].rearrange("p (h d) -> p h d", h=4),
                            s0[:, hg % 2, dr * 256:(dr + 1) * 256].rearrange("p (h d) -> p h d", h=4),
                            dec3[:, t, h:h + 4].unsqueeze(2).to_broadcast([P, 4, 64]), ALU.mult)
                        ins.then_inc(s0_decayed, 1)
                    n = JOB[f"st{hg}_1"]
                    finished(dve, n)
                    dve.wait_ge(s0_decayed, 2 * (hg + 1))
                    took(dve.tensor_tensor(s1[:, :], s1[:, :], bk(n)[:, 0:512], ALU.add), n)
                    for t in range(TILES + 1):
                        n = TILES * hg + t
                        if t < TILES:
                            dve.wait_ge(rowb_in[n % 2], 32 * (n // 2 + 1))
                            if n >= 2:
                                finished(dve, JOB[f"y{(n - 2) // TILES}_{(n - 2) % TILES}"])
                            for dr in range(2):
                                for i in range(4):
                                    h = dr * 32 + 4 * hg + i
                                    ins = dve.tensor_scalar(seg[:, n % 2, dr, i * P:(i + 1) * P],
                                                            rowb[:, n % 2, dr, i * P:(i + 1) * P],
                                                            acs3[:, t, h:h + 1], 0.0, ALU.subtract, ALU.min)
                                ins.then_inc(seg_ready, 1)
                        if t >= 1:
                            gated(hg, t - 1)
                        if t < TILES:
                            for dr in range(2):
                                dve.wait_ge(seg_exp, 2 * n + dr + 1)
                                s4 = seg[:, n % 2, dr, :].rearrange("p (h l) -> p h l", h=4)
                                dve.tensor_tensor(s4, s4, cbm[:, dr, t, :].unsqueeze(1).to_broadcast([P, 4, P]),
                                                  ALU.mult).then_inc(seg_masked, 1)
            for g in range(SSD_G):
                taken(dve, JOB[f"N_y{g}"])
                step(dve.reciprocal(yrs[:, :], yrs[:, :]))
                settle()
                for c in range(4 * g, 4 * g + 4):
                    dve.scalar_tensor_tensor(xf[:, c, :], xf[:, c, :], v("ssd_g", c, 1), yrs[:, :], ALU.mult,
                                             ALU.mult).then_inc(yn_ready, 1)
                for c in range(4 * g, 4 * g + 4):
                    dve.wait_ge(yhi_ready, c + 1)
                    dve.tensor_tensor(ylo[:, c, :], xf[:, c, :], yhi[:, c, :].bitcast(F32),
                                      ALU.subtract).then_inc(ylo_ready, 1)
            for kc in range(KC):
                residual(JOB[f"so{kc}"], 1, 2, kc)
            moe(1)

        @block.tensor
        def _(pe):
            def opened(job, it=None):
                if job >= JOB_BANKS:
                    pe.wait_ge(bank_taken[job % JOB_BANKS],
                               counted(job // JOB_BANKS, it, BODY_JOBS // JOB_BANKS))
                return bk(job)

            def mm3(dst, whi_, wlo_, xhi_, xlo_, first, last):
                pe.matmul(dst, whi_, xhi_, start=first, stop=False)
                pe.matmul(dst, whi_, xlo_, start=False, stop=False)
                return pe.matmul(dst, wlo_, xhi_, start=False, stop=last)

            def split_in(name, it=None):
                pe.wait_ge(lo_done, counted(SPLIT_NO[name] + 1, it, BODY_SPLITS))

            def mod_piece(name, it=None):
                layer, s, m_ = name
                pos = AT[name]
                pe.wait_ge(raw_in[pos % RAW], counted(16 * (pos // RAW + 1), it, 16 * (BODY_LEN[0] // RAW)))
                if m_ == 0:
                    if name == (0, 0, 0):
                        pe.wait_ge(silc_ready, 1)
                    else:
                        pe.wait_ge(modrow_ready, counted(layer * MOD_SETS + s, it, 1))
                for j in range(4):
                    kc, grp = divmod(4 * m_ + j, 3)
                    ins = pe.matmul(bank[MOD_BANK][32 * grp:32 * grp + 32, :], silc[:, kc, :],
                                    raw[:, pos % RAW, j * 512:(j + 1) * 512], start=kc == 0, stop=kc == KC - 1,
                                    skip_group_check=True)
                ins.then_inc(mod_used, 1)

            def turn_mod(layer, s, it=None):
                n = layer * MOD_SETS + s
                pe.wait_ge(modrow_ready, counted(n + 1, it, 1))
                if n:
                    pe.wait_ge(mod_ready, counted(n, it, 1))
                for q in range(4):
                    ins = pe.transpose(bank[TURN_BANK][:, q * 96:(q + 1) * 96], modrow[0:96, q * P:(q + 1) * P],
                                       k("ident")[0:96, 0:96])
                ins.then_inc(mod_turned, 1)

            def norm(phase):
                n = JOB[f"norm{phase}"]
                dst = opened(n)[:, 0:NTOK]
                for kc in range(KC):
                    pe.wait_ge(sq_ready, KC * phase + kc + 1)
                    ins = pe.matmul(dst, k("ones"), squares[phase][:, kc % 2, :], start=kc == 0, stop=kc == KC - 1)
                    ins.then_inc(sq_used if kc < KC - 1 else jobs_done, 1)

            def pair(name, jobs, rhi_, rlo_, kcs=KC, it=None):
                wh = piece(whi, name).rearrange("p (c k f) -> p c k f", k=kcs, f=P)
                wl = piece(wlo, name).rearrange("p (c k f) -> p c k f", k=kcs, f=P)
                split_in(name, it)
                for c, job in enumerate(jobs):
                    dst = opened(job, it)[:, 0:NTOK]
                    for kc in range(kcs):
                        ins = mm3(dst, wh[:, c, kc, :], wl[:, c, kc, :], rhi_[:, kc, :], rlo_[:, kc, :],
                                  kc == 0, kc == kcs - 1)
                    ins.then_inc(jobs_done, 1)

            def group(job, width, parts):
                dst = opened(JOB[job])[:, 0:width]
                for i, (lhs, rhs) in enumerate(parts):
                    ins = pe.matmul(dst, lhs, rhs, start=i == 0, stop=i == len(parts) - 1)
                ins.then_inc(jobs_done, 1)

            pe.wait_ge(tables_in, 48)
            norm(0)
            for s in range(2):
                for m_ in range(MOD_PIECES):
                    mod_piece((0, s, m_))
                turn_mod(0, s)
            pe.wait_ge(hlo_ready, KC)
            late = [(0, 2 + i // MOD_PIECES, i % MOD_PIECES) for i in range(2 * MOD_PIECES)]
            pair("bqc01", [JOB["bqc0"], JOB["bqc1"]], hhi, hlo)
            mod_piece(late[0])
            pair("bqc2kr", [JOB["bqc2"], JOB["bkr"]], hhi, hlo)
            mod_piece(late[1])
            pair("kv01", [JOB["kv0"], JOB["kv1"]], hhi, hlo)
            mod_piece(late[2])
            pair("aq01", [JOB["aq0"], JOB["aq1"]], hhi, hlo)
            mod_piece(late[3])
            ones = k("ones")
            pe.wait_ge(asq_ready, 3)
            group("N_bqc", NTOK, [(ones, asq[:, i, 0:NTOK]) for i in range(3)])
            pair("aq23", [JOB["aq2"], JOB["aq3"]], hhi, hlo)
            mod_piece(late[4])
            pe.wait_ge(asq_ready, 6)
            group("N_kv", NTOK, [(ones, asq[:, i, 0:NTOK]) for i in (3, 4)])
            pe.wait_ge(rms_ready, 1)
            for i, name in enumerate(("wq012", "wq345")):
                pos = AT[name]
                pe.wait_ge(raw_in[pos % RAW], 16 * (pos // RAW + 1))
                w = raw[:, pos % RAW, 0:3 * 3 * P].rearrange("p (c k f) -> p c k f", c=3, k=3)
                for c in range(3):
                    n = JOB[f"wq{3 * i + c}"]
                    dst = opened(n)[:, 0:NTOK]
                    for kc in range(3):
                        ins = pe.matmul(dst, w[:, c, kc, :], bqc[:, kc, :], start=kc == 0, stop=kc == 2)
                    ins.then_inc(jobs_done, 1)
                mod_piece(late[5 + i])
                if i == 0:
                    turn_mod(0, 2)
            pe.wait_ge(rms_ready, 2)
            pe.wait_ge(cache_in, 64)
            pos = AT["wkv"]
            pe.wait_ge(raw_in[pos % RAW], 16 * (pos // RAW + 1))
            wk = raw[:, pos % RAW, 0:1024].rearrange("p (c k f) -> p c k f", c=4, k=2)
            wv = raw[:, pos % RAW, 1024:2048].rearrange("p (k f) -> p k f", k=2)
            for h in range(HEADS):
                dst = opened(JOB[f"kn{h}"])[:, :]
                for kc in range(2):
                    ins = pe.matmul(dst, wk[:, h, kc, :], ckv[:, kc, :], start=kc == 0, stop=kc == 1)
                ins.then_inc(jobs_done, 1)
            for s in range(4):
                dst = opened(JOB[f"vb{s}"])[:, :]
                for kc in range(2):
                    ins = pe.matmul(dst, ckv[:, kc, s * P:(s + 1) * P], wv[:, kc, :], start=kc == 0, stop=kc == 1)
                ins.then_inc(jobs_done, 1)
            mod_piece(late[7])
            pair("ak01", [JOB["ak0"], JOB["ak1"]], hhi, hlo)
            mod_piece(late[8])
            pair("ak23", [JOB["ak2"], JOB["ak3"]], hhi, hlo)
            mod_piece(late[9])
            pe.wait_ge(katt_in, 16)
            block_ones = ka("block")
            for h in range(HEADS):
                pe.wait_ge(asq_ready, 7 + h)
                group(f"N_aq{h}", NTOK, [(block_ones, asq[:, (5 + h) % 6, 0:NTOK])])
            for h in range(HEADS):
                pe.wait_ge(asq_ready, 16 if h > 1 else 15)
                a = 64 * (h % 2)
                group(f"N_bq{h}", NTOK, [(ones, asq[:, (9 + h) % 6, 0:NTOK]),
                                         (ones[a:a + 64, :], asq[a:a + 64, (13 + h // 2) % 6, 0:NTOK])])
            split_in("va_lo")
            split_in("va_hi")
            for t in range(TILES):
                dst = opened(JOB[f"va{t}"])[:, :]
                for kc in range(KC):
                    name = "va_lo" if kc < 4 else "va_hi"
                    wh = piece(whi, name).rearrange("p (k f) -> p k f", k=4)[:, kc % 4, :]
                    wl = piece(wlo, name).rearrange("p (k f) -> p k f", k=4)[:, kc % 4, :]
                    ins = mm3(dst, hhi[:, kc, t * P:(t + 1) * P], hlo[:, kc, t * P:(t + 1) * P], wh, wl,
                              kc == 0, kc == KC - 1)
                ins.then_inc(jobs_done, 1)
            mod_piece(late[10])
            mod_piece(late[11])
            turn_mod(0, 3)
            for h in range(HEADS):
                pe.wait_ge(asq_ready, 17 + h)
                group(f"N_bk{h}", KEYS, [(ones, asq[:, (15 + h) % 6, :]), (ones[0:64, :], krsq[0:64, :])])
            for h in range(HEADS):
                pe.wait_ge(asq_ready, 21 + h)
                group(f"N_ak{h}", NTOK, [(block_ones, asq[:, (19 + h) % 6, 0:NTOK])])
            for i, tgt in enumerate(rope_targets(q_a, k_a, q_br, k_br)):
                pe.wait_ge(rms_ready, 2 + (4, 4, 16, 16, 8, 12)[i])
                n = JOB[f"rope{i}"]
                dst = opened(n)[:, :].rearrange("p (a l) -> p a l", a=2)
                pe.matmul(dst, ka("rot"), tgt, start=True, stop=True).then_inc(jobs_done, 1)

            pe.wait_ge(roped, 6)
            pe.wait_ge(mod_ready, 4)
            for u in range(len(UNITS) + 2):
                if u < len(UNITS):
                    kind, h, t = UNITS[u]
                    k0, k1 = (0, NPROMPT) if t == 0 else (NPROMPT, KEYS)
                    qs = slice(t * P, (t + 1) * P)
                    if kind == "A":
                        for i in range(2):
                            n = JOB[f"S{u}_{i}"]
                            r = slice(64 * i, 64 * i + 64)
                            pe.matmul(opened(n)[:, 0:k1 - k0], q_a[r, h, qs], k_a[r, h, k0:k1], start=True,
                                      stop=True).then_inc(jobs_done, 1)
                    else:
                        n = JOB[f"S{u}_0"]
                        r = slice(64 * (h % 2), 64 * (h % 2) + 64)
                        dst = opened(n)[:, 0:k1 - k0]
                        pe.matmul(dst, q_b[:, h, qs], k_b[:, h, k0:k1], start=True, stop=False)
                        pe.matmul(dst, q_br[r, h // 2, qs], k_br[r, h // 2, k0:k1], start=False,
                                  stop=True).then_inc(jobs_done, 1)
                if 1 <= u <= len(UNITS):
                    kind, h, t = UNITS[u - 1]
                    n = JOB[f"W{u - 1}"]
                    dst = opened(n)
                    pe.wait_ge(w_ready, u)
                    for j in range(1 if t == 0 else TILES):
                        ins = pe.transpose(dst[:, j * P:(j + 1) * P], w_sb[:, (u - 1) % 2, j * P:(j + 1) * P],
                                           k("ident"))
                    ins.then_inc(jobs_done, 1)
                if u >= 2:
                    kind, h, t = UNITS[u - 2]
                    e = (u - 2) // TILES
                    taken(pe, JOB[f"W{u - 2}"])
                    if t == 0 and e >= 2:
                        pe.wait_ge(o_taken, e - 1)
                    vals = v_a if kind == "A" else v_b
                    slots = [0] if t == 0 else [1, 2, 3]
                    for j, s in enumerate(slots):
                        ins = pe.matmul(bank[6 + e % 2][:, t * P:(t + 1) * P], vals[:, s, h * P:(h + 1) * P],
                                        wt_sb[:, (u - 2) % 2, j * P:(j + 1) * P], start=j == 0, stop=j == len(slots) - 1)
                    if t == TILES - 1:
                        ins.then_inc(o_done, 1)
            for h in range(HEADS):
                pe.wait_ge(osq_ready, h + 1)
                group(f"N_o{h}", NTOK, [(ones, osq[:, h % 2, :])])
            pe.wait_ge(olo_ready, KC)
            for i in range(4):
                pair(f"wo{i}", [JOB[f"wo{2 * i}"], JOB[f"wo{2 * i + 1}"]], hhi, hlo)

            def moe(layer):
                phase = 2 * layer + 1
                norm(phase)
                n = JOB[f"router{layer}"]
                dst = opened(n)
                pe.wait_ge(hlo_ready, KC * (phase + 1))
                pe.wait_ge(rlo_ready, layer + 1)
                for t in range(TILES):
                    for kc in range(KC):
                        ts = slice(t * P, (t + 1) * P)
                        ins = mm3(dst[:, t * NEXP:(t + 1) * NEXP], hhi[:, kc, ts], hlo[:, kc, ts], rhi[:, kc, :],
                                  rlo[:, kc, :], kc == 0, kc == KC - 1)
                ins.then_inc(jobs_done, 1)
                pair(f"sa{layer}", [JOB[f"shu{layer}_0"], JOB[f"shu{layer}_1"]], hhi, hlo)
                pair(f"sb{layer}", [JOB[f"shu{layer}_2"], JOB[f"shu{layer}_3"]], hhi, hlo)
                n = JOB[f"gt{layer}"]
                dst = opened(n)
                pe.wait_ge(gates_ready, layer + 1)
                for t in range(TILES):
                    ins = pe.transpose(dst[0:NEXP, t * P:(t + 1) * P], rt[:, 10, t * NEXP:(t + 1) * NEXP], k("ident"))
                ins.then_inc(jobs_done, 1)
                pre = layer * (2 + 2 * NEXP)
                pe.wait_ge(hid_lo_ready, pre + 2)
                pair(f"sd{layer}", [JOB[f"shd{layer}_{i}"] for i in range(KC)], hidhi, hidlo, kcs=2)
                n0 = JOB[f"body{layer}"]
                with pe.Fori(0, BODIES) as it:
                    names = [n_ for kind, n_ in STREAM[LOOP_AT[layer]:LOOP_AT[layer] + BODY_LEN[layer]]]
                    for name in names:
                        if isinstance(name, tuple):
                            mod_piece(name, it)
                            continue
                        i = int(name[1])
                        if name[0] in "ab":
                            j = 4 * i + 2 * (name[0] == "b")
                            pair(name, [n0 + j, n0 + j + 1], hhi, hlo, it=it)
                        else:
                            wh = piece(whi, name).rearrange("p (c k f) -> p c k f", k=KC, f=P)
                            wl = piece(wlo, name).rearrange("p (c k f) -> p c k f", k=KC, f=P)
                            split_in(name, it)
                            for c in range(2):
                                n = n0 + 4 * EXP_PER_BODY + 2 * i + c
                                dst = opened(n, it)[:, 0:NTOK]
                                for kc in range(KC):
                                    if i == 0 and c == 0:
                                        pe.wait_ge(hid_lo_ready, it * KC + pre + 2 + kc + 1)
                                    ins = mm3(dst, wh[:, c, kc, :], wl[:, c, kc, :], hidhi[:, kc, :], hidlo[:, kc, :],
                                              kc == 0, kc == KC - 1)
                                ins.then_inc(jobs_done, 1)
                    if layer == 0:
                        turn_mod(1, 0, it)

            moe(0)

            norm(2)
            n = JOB["dt"]
            dst = opened(n)
            split_in("dtw")
            pe.wait_ge(hlo_ready, 3 * KC)
            wh = piece(whi, "dtw")[:, 0:512].rearrange("p (k f) -> p k f", k=KC)
            wl = piece(wlo, "dtw")[:, 0:512].rearrange("p (k f) -> p k f", k=KC)
            for t in range(TILES):
                for kc in range(KC):
                    ts = slice(t * P, (t + 1) * P)
                    ins = mm3(dst[:, t * 64:(t + 1) * 64], hhi[:, kc, ts], hlo[:, kc, ts], wh[:, kc, :], wl[:, kc, :],
                              kc == 0, kc == KC - 1)
            ins.then_inc(jobs_done, 1)
            pair("bc01", [JOB["bc0"], JOB["bc1"]], hhi, hlo)
            pair("bc23", [JOB["bc2"], JOB["bc3"]], hhi, hlo)
            pe.wait_ge(dt_ready, 1)
            pe.wait_ge(kssd_in, 32)
            dta = dts[:, 1, :].rearrange("p (t d) -> p t d", t=TILES)
            n = JOB["cs0"]
            dst = opened(n)[:, 0:384].rearrange("p (w t d) -> p w t d", w=2, t=TILES)
            for dr, name in enumerate(("upto", "since")):
                r = slice(32 * dr, 32 * dr + 32)
                pe.matmul(dst[:, 0, :, r], ks(name), dta[:, :, r], start=True, stop=True)
            pe.matmul(dst[:, 1, :, :], ones, dta, start=True, stop=True).then_inc(jobs_done, 1)
            n = JOB["cs1"]
            dst = opened(n)[:, 0:192].rearrange("p (t d) -> p t d", t=TILES)
            for dr in range(2):
                r = slice(32 * dr, 32 * dr + 32)
                ins = pe.matmul(dst[:, :, r], kcum[:, dr, :], dta[:, :, r], start=True, stop=True)
            ins.then_inc(jobs_done, 1)
            pair("bc45", [JOB["bc4"], JOB["bc5"]], hhi, hlo)
            n = JOB["csT"]
            dst = opened(n)
            taken(pe, JOB["cs0"])
            for t in range(TILES):
                ins = pe.transpose(dst[0:64, t * P:(t + 1) * P], dts[:, 5, t * 64:(t + 1) * 64], k("ident"))
            ins.then_inc(jobs_done, 1)
            pair("bc67", [JOB["bc6"], JOB["bc7"]], hhi, hlo)
            for i in range(8):
                pair(f"xsw{i}", [JOB[f"xs{2 * i}"], JOB[f"xs{2 * i + 1}"]], hhi, hlo)
            for i in range(8):
                pair(f"zw{i}", [JOB[f"z{2 * i}"], JOB[f"z{2 * i + 1}"]], hhi, hlo)

            pe.wait_ge(conv_out, 24)
            for g in range(SSD_G):
                dst = opened(JOB[f"bt{g}"])
                for t in range(TILES):
                    ins = pe.transpose(dst[:, t * P:(t + 1) * P], bc[:, g, t * P:(t + 1) * P], k("ident"))
                ins.then_inc(jobs_done, 1)
                dst = opened(JOB[f"cb{g}"])
                for t in range(TILES):
                    ts = slice(t * P, (t + 1) * P)
                    ins = pe.matmul(dst[:, ts], bc[:, g, ts], bc[:, 4 + g, ts], start=True, stop=True)
                ins.then_inc(jobs_done, 1)
                for hg in (2 * g, 2 * g + 1):
                    for j, tiles in enumerate(((0, 1), (2,))):
                        dst = opened(JOB[f"xt{hg}_{j}"])
                        for a, t in enumerate(tiles):
                            for c in range(2):
                                ins = pe.transpose(dst[:, (2 * a + c) * P:(2 * a + c + 1) * P],
                                                   xf[:, 2 * hg + c, t * P:(t + 1) * P], k("ident"))
                        ins.then_inc(jobs_done, 1)
                    taken(pe, JOB[f"bt{g}"])
                    pe.wait_ge(xw_ready, 4 * hg + 4)
                    for j in range(2):
                        dst = opened(JOB[f"st{hg}_{j}"])
                        for a in range(2):
                            t = 0 if j == 0 else 1 + a
                            ins = pe.matmul(dst[:, a * 256:(a + 1) * 256], btok[:, t, :], xw[:, 2 * j + a, :],
                                            start=True, stop=True)
                        ins.then_inc(jobs_done, 1)
                    for t in range(TILES):
                        n = TILES * hg + t
                        ts = slice(t * P, (t + 1) * P)
                        dst = opened(JOB[f"y{hg}_{t}"])
                        pe.wait_ge(seg_masked, 2 * n + 2)
                        pe.wait_ge(xdt_ready, 2 * n + 2)
                        if t:
                            pe.wait_ge(ce_ready, 4 * hg + 2 * t)
                            taken(pe, JOB[f"st{hg}_1"])
                        for c in range(2):
                            terms = []
                            for dr in range(2):
                                for p_ in range(2):
                                    i = 2 * c + p_
                                    terms.append((p_, xdt[:, n % 2, dr, i * 64:(i + 1) * 64],
                                                  seg[:, n % 2, dr, i * P:(i + 1) * P]))
                            if t:
                                for dr in range(2):
                                    first_chunk = (t == 1) if dr == 0 else (t == 2)
                                    st = s0[:, hg % 2, :] if first_chunk else s1[:, :]
                                    for p_ in range(2):
                                        i = 2 * c + p_
                                        o = dr * 256 + i * 64
                                        terms.append((p_, st[:, o:o + 64], ce[:, n % 2, dr, i * P:(i + 1) * P]))
                            for j, (p_, lhs, rhs) in enumerate(terms):
                                ins = pe.matmul(dst[64 * p_:64 * p_ + 64, c * P:(c + 1) * P], lhs, rhs,
                                                start=j < 2, stop=j >= len(terms) - 2, skip_group_check=True)
                        ins.then_inc(jobs_done, 1)
            for g in range(SSD_G):
                dst = opened(JOB[f"N_y{g}"])[:, 0:NTOK]
                for c in range(4 * g, 4 * g + 4):
                    pe.wait_ge(ysq_ready, c + 1)
                    ins = pe.matmul(dst, ones, ysq[:, c % 2, :], start=c % 4 == 0, stop=c % 4 == 3)
                    if c % 4 < 3:
                        ins.then_inc(ysq_used, 1)
                ins.then_inc(jobs_done, 1)
            pe.wait_ge(ylo_ready, XCH)
            for i in range(KC):
                name = f"sow{i}"
                wh = piece(whi, name).rearrange("p (k f) -> p k f", k=XCH)
                wl = piece(wlo, name).rearrange("p (k f) -> p k f", k=XCH)
                split_in(name)
                dst = opened(JOB[f"so{i}"])[:, 0:NTOK]
                for kc in range(XCH):
                    ins = mm3(dst, wh[:, kc, :], wl[:, kc, :], yhi[:, kc, :], ylo[:, kc, :], kc == 0, kc == XCH - 1)
                ins.then_inc(jobs_done, 1)
            moe(1)


_OUTS = {"yT": (P, KC, NTOK), "new_ak": (P, HEADS, NPROMPT), "new_av": (P, HEADS * P), "new_ckv": (P, 2, NPROMPT),
         "new_kr": (64, NPROMPT), "new_s": (P, 2, SSD_H * SSD_P)}


def chunks_of(w, starts):
    k = w.shape[0] // P
    return np.stack([w[:, s:s + P].reshape(k, P, P).transpose(1, 0, 2) for s in starts], axis=1)


def lay_stream(a):
    stream = np.zeros((len(STREAM), P, PIECE), np.float32)
    w_in, wq, wkv = a["attn_w_in"][0], a["b_wq_up"][0], a["b_wkv_up"][0]
    ssd_in, ssd_out, attn_out = a["ssd_w_in"][0], a["ssd_w_out"][0], a["attn_w_out"][0]
    c_kr = 2176
    w_kr = np.concatenate([w_in[:, c_kr:], w_in[:, c_kr:]], axis=1)
    wq_cols = np.concatenate([wq[:, h * B_DQK:h * B_DQK + P] for h in range(HEADS)] +
                             [wq[:, h * B_DQK + P:(h + 1) * B_DQK] for h in range(HEADS)], axis=1)
    kv4 = wkv.reshape(2 * P, HEADS, 2 * P)
    fixed = {
        "bqc01": chunks_of(w_in, (1536, 1664)), "kv01": chunks_of(w_in, (1920, 2048)),
        "bqc2kr": np.concatenate([chunks_of(w_in, (1792,)), chunks_of(w_kr, (0,))], axis=1),
        "aq01": chunks_of(w_in, (0, 128)), "aq23": chunks_of(w_in, (256, 384)),
        "ak01": chunks_of(w_in, (512, 640)), "ak23": chunks_of(w_in, (768, 896)),
        "wq012": chunks_of(wq_cols, (0, 128, 256)), "wq345": chunks_of(wq_cols, (384, 512, 640)),
        "wkv": np.concatenate([
            chunks_of(kv4[:, :, :P].reshape(2 * P, HEADS * P), range(0, HEADS * P, P)).reshape(P, -1),
            kv4[:, :, P:].reshape(2, P, HEADS * P).transpose(1, 0, 2).reshape(P, -1)], axis=1),
        "dtw": ssd_in[:, 5120:].reshape(KC, P, 64).transpose(1, 0, 2),
    }
    values = w_in[:, 1024:1536].reshape(KC, P, HEADS * P).transpose(1, 0, 2)
    fixed["va_lo"], fixed["va_hi"] = values[:, :4], values[:, 4:]
    for i in range(4):
        fixed[f"wo{i}"] = chunks_of(attn_out, (256 * i, 256 * i + P))
        fixed[f"bc{2 * i}{2 * i + 1}"] = chunks_of(ssd_in, (4096 + 256 * i, 4096 + 256 * i + P))
    for i in range(8):
        fixed[f"xsw{i}"] = chunks_of(ssd_in, (2048 + 256 * i, 2048 + 256 * i + P))
        fixed[f"zw{i}"] = chunks_of(ssd_in, (256 * i, 256 * i + P))
        fixed[f"sow{i}"] = chunks_of(ssd_out, (P * i,))
    for layer in range(DEPTH):
        sh_in, sh_out = a["shared_w_in"][layer], a["shared_w_out"][layer]
        fixed[f"sa{layer}"] = chunks_of(sh_in, (0, 256))
        fixed[f"sb{layer}"] = chunks_of(sh_in, (128, 384))
        fixed[f"sd{layer}"] = chunks_of(sh_out, range(0, D, P))
    for n, (kind, name) in enumerate(STREAM):
        if kind == "mod":
            layer, s, m = name
            for j in range(4):
                kc, grp = divmod(4 * m + j, 3)
                col = s * MOD_COLS + grp * 512
                stream[n, :, j * 512:(j + 1) * 512] = a["mod_w"][layer, kc * P:(kc + 1) * P, col:col + 512]
            continue
        if name in fixed:
            w = fixed[name]
        else:
            what, layer, it = name.split("_")
            layer, it, i = int(layer), int(it), int(what[1])
            e = EXP_PER_BODY * it
            if what[0] == "a":
                w = chunks_of(a["moe_w_in"][layer, e + i], (0, 256))
            elif what[0] == "b":
                w = chunks_of(a["moe_w_in"][layer, e + i], (128, 384))
            else:
                down = a["moe_w_out"][layer, e:e + EXP_PER_BODY].reshape(-1, D)
                w = chunks_of(down, (256 * i, 256 * i + P))
        w = w.reshape(P, -1)
        stream[n, :, :w.shape[1]] = w
    return stream


def column(x, n=1):
    return x.reshape(n, P).T


def rows(x):
    return np.broadcast_to(x.reshape(1, -1), (P, x.size))


def lay_vectors(a):
    def twice(x):
        return np.concatenate([x, x])

    norm_g = np.stack([a["norm1_g"], a["norm2_g"]], axis=1).reshape(2 * DEPTH * KC, P)
    cols = {
        "c": np.stack([column(a["c_ctx"], KC), column(a["c"][0], KC)], axis=2).reshape(P, -1),
        "norm_g": np.repeat(norm_g.T, 2, axis=1),
        "gq_a": column(twice(a["a_qk_g"][0, 0])), "gk_a": column(twice(a["a_qk_g"][0, 1])),
        "sub_g": column(a["a_sub_g"][0]), "bqa_g": column(a["b_qa_g"][0], 3), "bkva_g": column(a["b_kva_g"][0], 2),
        "gq_bn": column(a["b_qk_g"][0, 0, :P]), "gq_br": column(twice(a["b_qk_g"][0, 0, P:])),
        "gk_bn": column(a["b_qk_g"][0, 1, :P]), "gk_br": column(twice(a["b_qk_g"][0, 1, P:])),
        "rbias": rows(a["router_bias"]),
        "conv_w": column(a["ssd_conv_w"][0], 72), "conv_b": column(a["ssd_conv_b"][0], 24),
        "ssd_d": column(np.repeat(a["ssd_d"][0], SSD_P), XCH), "ssd_g": column(a["ssd_norm_g"][0], XCH),
        "dt_bias": rows(a["ssd_dt_bias"][0]), "a_log": rows(a["ssd_a_log"][0]),
        "router": a["router_w"].reshape(KC, P, NEXP).transpose(1, 0, 2).reshape(P, -1),
    }
    return np.ascontiguousarray(np.concatenate([cols[n] for n, _ in _VEC], axis=1))


def constants():
    f = np.float32
    i = np.arange(P)
    eye = np.eye(P, dtype=f)
    kon = np.concatenate([eye, np.ones((P, P), f), np.full((P, 1), EPS, f), np.ones((P, 1), f),
                          rows(np.arange(NEXP, 0, -1).astype(f)), rows(np.arange(NGRP, 0, -1).astype(f))], axis=1)
    rot = np.zeros((P, P), f)
    for m in range(P):
        if m % 64 < 32:
            rot[m + 32, m] = -1.0
        else:
            rot[m - 32, m] = 1.0
    tok = np.arange(NLAT)
    inv = (f(ROPE_BASE) ** (f(-2.0) * np.arange(16, dtype=f) / f(32))).astype(f)
    ang = np.concatenate([(tok // GRID_W).astype(f)[:, None] * inv, (tok % GRID_W).astype(f)[:, None] * inv], axis=1)
    ang = ang.T[i % 32]
    katt = np.concatenate([(i[:, None] // 64 == i[None] // 64).astype(f), rot, np.cos(ang), np.sin(ang)], axis=1)
    r, c = i[:, None], i[None]
    kssd = np.concatenate([r <= c, r >= c], axis=1).astype(f)
    kcum = np.stack([r > c, r < c], axis=1).astype(f)
    return kon, katt.astype(f), kssd, kcum


def kernel(**inputs):
    import concourse.bacc as bacc
    from concourse.bass_utils import run_bass_kernel_spmd

    a = {n: np.asarray(x) for n, x in inputs.items()}
    kon, katt, kssd, kcum = constants()
    x = np.concatenate([a["x_prompt"][0], a["x_sample"][0]], axis=0)
    kr = a["cache_b_krope"][0, 0].T
    mod_b = a["mod_b"].reshape(DEPTH, 6 * KC, P).transpose(2, 0, 1)
    arrays = {
        "stream": lay_stream(a), "vec": lay_vectors(a), "kon": kon, "katt": katt, "kssd": kssd, "kcum": kcum,
        "lam": rows(a["a_lambda"][0]),
        "modb": np.repeat(mod_b, 2, axis=2).reshape(P, DEPTH, MOD_SETS, 24),
        "xT": x.T.reshape(KC, P, NTOK).transpose(1, 0, 2),
        "cache_ak": a["cache_a_k"][0, 0].transpose(2, 3, 1, 0).reshape(P, HEADS, P),
        "cache_av": a["cache_a_v"][0, 0].reshape(P, HEADS * P),
        "cache_ckv": a["cache_b_ckv"][0, 0].T.reshape(2, P, P).transpose(1, 0, 2),
        "cache_kr": np.concatenate([kr, kr], axis=0),
        "s0T": a["state_ssd"][0, 0].transpose(3, 0, 1, 2).reshape(P, 2, SSD_H * SSD_P),
    }
    nc = bacc.Bacc("TRN2", target_bir_lowering=False, num_devices=1)
    inp, out = {}, {}
    for n in list(arrays):
        arrays[n] = np.ascontiguousarray(arrays[n])
        inp[n] = nc.dram_tensor(n, arrays[n].shape, mybir.dt.from_np(arrays[n].dtype), kind="ExternalInput").ap()
    for n, shape in _OUTS.items():
        out[n] = nc.dram_tensor(n, shape, F32, kind="ExternalOutput").ap()
    build(nc, inp, out)
    r = run_bass_kernel_spmd(nc, [arrays], core_ids=[0]).results[0]
    y = r["yT"].transpose(1, 0, 2).reshape(D, NTOK).T
    new_ak = r["new_ak"].reshape(2, DQK, HEADS, NPROMPT).transpose(3, 2, 0, 1)
    new_ckv = r["new_ckv"].transpose(1, 0, 2).reshape(2 * P, NPROMPT).T
    new_s = r["new_s"].transpose(1, 2, 0).reshape(2, SSD_H, SSD_P, P)
    return (y[None, :NPROMPT], y[None, NPROMPT:], new_ak[None, None], r["new_av"].reshape(1, 1, NPROMPT, HEADS, P),
            new_ckv[None, None], r["new_kr"].T[None, None], new_s[None, None])
```

```python
from contextlib import ExitStack

import numpy as np
import concourse.bass as bass
from concourse import mybir

F32 = mybir.dt.float32
F32R = mybir.dt.float32r
ALU = mybir.AluOpType
ACT = mybir.ActivationFunctionType
AX = mybir.AxisListType

P = 128
D = 1024
KC = D // P
NPROMPT = 128
NLAT = 256
NTOK = NPROMPT + NLAT
TILES = NTOK // P
CLASSES = ((0, NPROMPT), (NPROMPT, NTOK))
DEPTH = 2
GRID_W = 64
ROPE_BASE = 10000.0
EPS = 1e-6
LAM_INIT = 0.8 - 0.6 * 1.0
HEADS = 4
DQK = 64
B_DQK = 192
A_SCALE = 64 ** -0.5
B_SCALE = B_DQK ** -0.5
KEYS = 512
PAST = slice(128, 256)
NEXP = 16
NGRP = 4
SSD_H = 32
SSD_P = 64
SSD_G = 4
XCH = 16
PIECE = 2048
RAW = 3
SPL = 3
JOB_BANKS = 6
CORE_BANKS = 5
O_BANK = 5
MOD_BANK = 7
TURN_BANK = 6
MOD_SETS = 6 * D // PIECE
MOD_PIECES = KC
MOD_GROUPS = PIECE // 512
MOD_W = 2 * PIECE // P
D_EXP = 256
PER_GRP = NEXP // NGRP
MAX_BLOCKS = (NTOK - NGRP) // P + NGRP
MIN_BLOCKS = NTOK // P
BLOCK_COLS = MAX_BLOCKS + 1
UNIT = PIECE // 2
UP_PARTS, DOWN_PARTS = KC * 2 * D_EXP // UNIT, 2 * D // UNIT


def expert_order():
    def up(i):
        return [f"u{i}_{part}" for part in range(UP_PARTS)]

    def down(i):
        return [f"d{i}_{part}" for part in range(DOWN_PARTS)]

    return up(0) + up(1) + up(2) + down(0) + up(3) + down(1) + down(2) + down(3)


EXPERT_ORDER = expert_order()
GRP_UNITS = len(EXPERT_ORDER)
SLOTS = 2 * RAW
SLOT_USES = GRP_UNITS // SLOTS
U_BANK, T_BANK, PERM_BANK, Y_BANK = 0, 2, 4, 6
BIG = 1e30

_VEC = [("c", 16), ("norm_g", 64), ("gq_a", 1), ("gk_a", 1), ("sub_g", 1), ("bqa_g", 3), ("bkva_g", 2),
        ("gq_bn", 1), ("gq_br", 1), ("gk_bn", 1), ("gk_br", 1), ("rbias", 16), 
        ("conv_w", 72), ("conv_b", 24), ("ssd_d", 16), ("ssd_g", 16), ("dt_bias", 64), ("a_log", 64),
        ("router", 128)]
_KONST = [("ident", 128), ("ones", 128), ("eps", 1), ("one", 1), ("rank16", 16), ("rank4", 4)]
_KATT = [("block", 128), ("rot", 128), ("cos", 256), ("sin", 256)]
_KMOE = [("slots", BLOCK_COLS * P), ("before", 128), ("blocks", 8)]
_KSSD = [("upto", 128), ("since", 128)]


def offsets(table):
    out, at = {}, 0
    for name, w in table:
        out[name] = (at, at + w)
        at += w
    return out, at


VEC, VEC_W = offsets(_VEC)
KONST, KONST_W = offsets(_KONST)
KATT, KATT_W = offsets(_KATT)
KMOE, KMOE_W = offsets(_KMOE)
KSSD, KSSD_W = offsets(_KSSD)

UNITS = [("A", h, t) for h in range(HEADS) for t in range(TILES)] + \
        [("B", h, t) for h in range(HEADS) for t in range(TILES)]
LATE_EARLY = 5
CORE_SETS = [(0, 2), (1, 0), (1, 1), (1, 2)]
TURN_EVERY = 5
PIECES_AT = [[CORE_SETS[p // MOD_PIECES] + (p % MOD_PIECES,) for p in range(len(CORE_SETS) * MOD_PIECES)
              if p * TURN_EVERY // MOD_PIECES == u] for u in range(len(UNITS))]
SQUARE_AT, SUM_AT, ROOT_AT, SCALE_AT, HI_AT, LO_AT = 15, 16, 17, 18, 19, 20
WO_SPLIT_AT = 20


def turned_at(u):
    i = u // TURN_EVERY - 1
    return i if u and u % TURN_EVERY == 0 and i < len(CORE_SETS) else None


RMS_ORDER = ["aq0", "aq1", "aq2", "aq3", "bq0", "bq1", "bq2", "bq3", "bk0", "bk1", "bk2", "bk3",
             "ak0", "ak1", "ak2", "ak3"]


def numbered(prefix, n):
    return [f"{prefix}{i}" for i in range(n)]


def plan_jobs():
    names = ["norm0"] + numbered("bqc", 3) + ["bkr", "kv0", "kv1", "aq0", "aq1", "N_bqc", "aq2", "aq3", "N_kv"]
    names += numbered("N_aq", 4) + numbered("wq", 6) + numbered("kn", 4) + numbered("vb", 4)
    names += numbered("N_bq", 4) + numbered("ak", 4) + numbered("N_bk", 4) + numbered("N_ak", 4) + numbered("va", 3)
    names += numbered("rope", 6)
    for u in range(len(UNITS) + 2):
        if u < len(UNITS):
            names += [f"S{u}_0", f"S{u}_1"] if UNITS[u][0] == "A" else [f"S{u}_0"]
        if turned_at(u) is not None:
            names.append(f"turn{turned_at(u)}")
        if u >= 2:
            names.append(f"W{u - 2}")
        if 0 <= u - SUM_AT < HEADS:
            names.append(f"N_o{u - SUM_AT}")
    names += numbered("wo", KC)
    job, at = {}, 0

    def add(more):
        nonlocal at
        for n in more:
            job[n] = at
            at += 1

    def moe(layer):
        tok = numbered(f"tok{layer}_", 2 * TILES)
        add([f"norm{2 * layer + 1}", f"router{layer}"] + tok[:2] + [f"scores{layer}"] + tok[2:] +
            numbered(f"shu{layer}_", 4) + [f"rank{layer}"] + numbered(f"shd{layer}_", KC) + [f"gate{layer}"] +
            numbered(f"back{layer}_", MAX_BLOCKS) + numbered(f"comb{layer}_", KC))

    add(names)
    moe(0)
    add(["norm2", "dt", "bc0", "bc1", "dtT", "bc2", "bc3", "cs0", "cs1"] + ["bc4", "bc5", "csT", "bc6", "bc7"])
    add(numbered("xs", XCH) + numbered("z", XCH))

    def turned(hg):
        return ([f"bt{hg // 2}", f"cb{hg // 2}"] if hg % 2 == 0 else []) + [f"xt{hg}_0", f"xt{hg}_1"]

    def states(hg):
        return [f"st{hg}_0", f"st{hg}_1"]

    add(turned(0) + states(0))
    for hg in range(2 * SSD_G):
        more = hg + 1 < 2 * SSD_G
        add([f"y{hg}_0"] + (turned(hg + 1) if more else []) + [f"y{hg}_1", f"y{hg}_2"] +
            (states(hg + 1) if more else []))
    add(numbered("N_y", SSD_G) + numbered("so", KC))
    moe(1)
    core = range(job["S0_0"], job["wo0"])
    where, uses = [], [0] * JOB_BANKS
    turn = 0
    for n in range(at):
        b = turn % (CORE_BANKS if n in core else JOB_BANKS)
        where.append((b, uses[b]))
        uses[b] += 1
        turn = b + 1
    return job, where


JOB, BANK_OF = plan_jobs()


def plan_stream():
    last = {}
    stream = [("mod", (0, s, m)) for s in range(1) for m in range(MOD_PIECES)]
    early = [("split", "bqc01", "bqc1"), ("split", "bqc2kr", "bkr"), ("split", "kv01", "kv1"),
             ("split", "aq01", "aq1"), ("split", "aq23", "aq3"), ("plain", "wq012", "wq2"),
             ("plain", "wq345", "wq5"), ("plain", "wkv", "vb3"), ("split", "ak01", "ak1"),
             ("split", "ak23", "ak3"), ("split", "va_lo", "va2"), ("split", "va_hi", "va2")]
    for i, (kind, name, job) in enumerate(early):
        stream.append((kind, name))
        if i < LATE_EARLY:
            stream.append(("mod", (0, 1, i)))
        last[name] = JOB[job]
    stream += [("mod", (0, 1, i)) for i in range(LATE_EARLY, MOD_PIECES)]
    stream += [("mod", piece) for pieces in PIECES_AT for piece in pieces]
    for i in range(4):
        stream.append(("split", f"wo{i}"))
        last[f"wo{i}"] = JOB[f"wo{2 * i + 1}"]
    loops = {}

    def moe(layer):
        for name, job in (("sa", f"shu{layer}_1"), ("sb", f"shu{layer}_3"), ("sd", f"shd{layer}_7")):
            stream.append(("split", f"{name}{layer}"))
            last[f"{name}{layer}"] = JOB[job]
        loops[layer] = len(stream)

    moe(0)
    ssd = [("dtw", "dt"), ("bc01", "bc1"), ("bc23", "bc3"), ("bc45", "bc5"), ("bc67", "bc7")]
    ssd += [(f"xsw{i}", f"xs{2 * i + 1}") for i in range(8)] + [(f"zw{i}", f"z{2 * i + 1}") for i in range(8)]
    ssd += [(f"sow{i}", f"so{i}") for i in range(KC)]
    for name, job in ssd:
        stream.append(("split", name))
        last[name] = JOB[job]
    moe(1)
    return stream, last, loops


STREAM, LAST_JOB, LOOP_AT = plan_stream()
SPLITS = [name for kind, name in STREAM if kind == "split"]
SPLIT_NO = {name: i for i, name in enumerate(SPLITS)}
AT = {name: i for i, (kind, name) in enumerate(STREAM)}
MODS = [name for kind, name in STREAM if kind == "mod"]
MOD_NO = {name: i for i, name in enumerate(MODS)}


def rope_targets(q_a, k_a, q_br, k_br):
    q, ke = slice(NPROMPT, NTOK), slice(2 * P, KEYS)
    return [q_a[:, 0:2, q], q_a[:, 2:4, q], k_a[:, 0:2, ke], k_a[:, 2:4, ke], q_br[:, :, q], k_br[:, :, ke]]


def build(nc, inp, out):
    ctx = ExitStack()
    with ctx:
        base = 16512

        class Map:

            def __init__(self, at, end=229344):
                self.at, self.end = at, end

            def put(self, name, shape, dt=F32):
                t = nc.alloc_sbuf_tensor_at(name, [P] + shape, dt, offset=self.at)
                self.at += (int(np.prod(shape)) * 4 + 31) // 32 * 32
                assert self.at <= self.end, (name, self.at)
                return t

        m = Map(base)
        raw = m.put("raw", [RAW, PIECE])
        whi = m.put("whi", [SPL, PIECE], F32R)
        wlo = m.put("wlo", [SPL, PIECE], F32R)
        x = m.put("x", [KC, NTOK])
        vec = m.put("vec", [VEC_W])
        kon = m.put("kon", [KONST_W])
        modb = m.put("modb", [DEPTH, MOD_SETS, MOD_W])
        mod = m.put("mod", [DEPTH, MOD_SETS, MOD_W])
        gain = m.put("gain", [2 * DEPTH, 2 * KC])
        gq = m.put("gq", [4])
        lam = m.put("lamv", [8])
        low = m.at
        hhi = m.put("hhi", [KC, NTOK], F32R)
        hlo = m.put("hlo", [KC, NTOK], F32R)
        free = m.at
        mn = Map(free)
        sq = mn.put("sq", [2, NTOK])
        rstd = mn.put("rstd", [NTOK])
        xr = mn.put("xr", [2, NTOK])
        h32 = mn.put("h32", [2, NTOK])
        norm_end = mn.at

        ms = Map(229344 - (8 * 32 + 512) * 4 - 64)
        silc = ms.put("silc", [KC, 32])
        modrow = ms.put("modrow", [512])
        top = 229344 - (8 * 32 + 512) * 4 - 64
        ma = Map(free, top)
        katt = ma.put("katt", [KATT_W])
        q_a = ma.put("q_a", [HEADS, NTOK])
        k_a = ma.put("k_a", [HEADS, KEYS])
        v_a = ma.put("v_a", [4, HEADS * P])
        q_b = ma.put("q_b", [HEADS, NTOK])
        q_br = ma.put("q_br", [2, NTOK])
        k_b = ma.put("k_b", [HEADS, KEYS])
        k_br = ma.put("k_br", [2, KEYS])
        v_b = ma.put("v_b", [4, HEADS * P])
        ars = ma.put("ars", [3, KEYS])
        mi = Map(ma.at, top)
        ckv = mi.put("ckv", [2, KEYS])
        kr = mi.put("kr", [KEYS])
        krsq = mi.put("krsq", [KEYS])
        bqc = mi.put("bqc", [3, NTOK])
        asq = mi.put("asq", [6, KEYS])
        mc = Map(ma.at, top)
        stat = mc.put("stat", [2, 8])
        e_sb = mc.put("e_sb", [2, 2, NTOK])
        w_sb = mc.put("w_sb", [2, NTOK])
        wt_sb = mc.put("wt_sb", [2, NTOK])
        o_sb = mc.put("o_sb", [2 * HEADS, NTOK])
        osq = mc.put("osq", [2, NTOK])

        my = Map(low)
        yhi_e = my.put("yhi_e", [MAX_BLOCKS, D], F32R)
        assert my.at <= free
        my = Map(free)
        ylo_e = my.put("ylo_e", [MAX_BLOCKS, D], F32R)
        mm = Map(norm_end)
        h_moe = mm.put("h_moe", [KC, NTOK])
        mm = Map(max(my.at, mm.at))
        rhi = mm.put("rhi", [KC, NEXP], F32R)
        rlo = mm.put("rlo", [KC, NEXP], F32R)
        rt = mm.put("rt", [14, TILES * NEXP])
        kmoe = mm.put("kmoe", [KMOE_W])
        place = mm.put("place", [TILES, BLOCK_COLS * P])
        back = mm.put("back", [MAX_BLOCKS, NTOK], F32R)
        msq = Map(mm.at).put("msq", [2, NTOK])
        h_tok = mm.put("h_tok", [TILES, D])
        blk_hi = mm.put("blk_hi", [KC, P], F32R)
        blk_lo = mm.put("blk_lo", [KC, P], F32R)
        nums = mm.put("nums", [8, 16])
        blk_grp = mm.put("blk_grp", [16], mybir.dt.int32)
        gates = mm.put("gates", [BLOCK_COLS, PER_GRP])
        gate_now = mm.put("gate_now", [PER_GRP])
        score_rows = mm.put("score_rows", [NTOK])
        sg = mm.put("sg", [2, NTOK])
        p2 = mm.put("p2", [2, NTOK])
        hidhi = mm.put("hidhi", [2, NTOK], F32R)
        hidlo = mm.put("hidlo", [2, NTOK], F32R)
        sg_e = mm.put("sg_e", [2, D_EXP])
        hid_e = mm.put("hid_e", [2, D_EXP])
        ht_hi = mm.put("ht_hi", [2, 2, P], F32R)
        ht_lo = mm.put("ht_lo", [2, 2, P], F32R)

        mz = Map(free)
        z = mz.put("z", [XCH, NTOK])
        xf = mz.put("xf", [XCH, NTOK])
        mzz = Map(free)
        yhi = mzz.put("yhi", [XCH, NTOK], F32R)
        ylo = mzz.put("ylo", [XCH, NTOK], F32R)
        bc = mz.put("bc", [8, NTOK])
        kssd = mz.put("kssd", [KSSD_W])
        dts_at = mz.at
        dts = mz.put("dts", [8, TILES * 64])
        mw = Map(mz.at)
        kcum = mw.put("kcum", [2, P])
        acsT = mw.put("acsT", [NTOK])
        cv = mw.put("cv", [2, 388])
        ct = mw.put("ct", [2, 388])
        mk = Map(mz.at)
        s0 = mk.put("s0", [2, 512])
        s1a = mk.put("s1a", [512])
        s1b = nc.alloc_sbuf_tensor_at("s1b", [P, 512], F32, offset=dts_at + TILES * 64 * 4)
        s1 = (s1a, s1b)
        pf = mk.put("pf", [512])
        xw = mk.put("xw", [4, 256])
        rowb = mk.put("rowb", [2, 2, 512])
        seg = mk.put("seg", [2, 2, 512])
        mh = Map(low, free)
        ce = mh.put("ce", [2, 2, 512])
        xtok = mh.put("xtok", [2, TILES, 256])
        btok = mh.put("btok", [TILES, P])
        cbm = mh.put("cbm", [2, TILES, P])
        xdt = mh.put("xdt", [2, 2, 256])
        mg = Map(low, free)
        ysq = mg.put("ysq", [2, NTOK])
        yrs = mg.put("yrs", [2, NTOK])

        squares = [sq, sq, msq, ysq]

        bank = [ctx.enter_context(nc.psum_tensor(f"bank{i}", [P, 512], F32)) for i in range(8)]

        acs_dram = nc.dram_tensor("acs_rows", [64, NTOK], F32).ap()

        def sem(name):
            return ctx.enter_context(nc.semaphore(name))

        raw_in = [sem(f"raw_in{i}") for i in range(RAW)]
        hi_done, lo_done, mod_used = sem("hi_done"), sem("lo_done"), sem("mod_used")
        jobs_done = sem("jobs_done")
        bank_taken = [sem(f"bank_taken{i}") for i in range(JOB_BANKS)]
        tables_in, x_in, katt_in, cache_in, kssd_in = (
            sem("tables_in"), sem("x_in"), sem("katt_in"), sem("cache_in"), sem("kssd_in"))
        silc_zero, silc_ready = sem("silc_zero"), sem("silc_ready")
        modrow_ready, mod_turned, mod_ready = sem("modrow_ready"), sem("mod_turned"), sem("mod_ready")
        cos_done = sem("cos_done")
        rstd_ready, xr_ready = sem("rstd_ready"), sem("xr_ready")
        sq_ready, sq_used, h32_ready, hhi_ready, hlo_ready = (
            sem("sq_ready"), sem("sq_used"), sem("h32_ready"), sem("hhi_ready"), sem("hlo_ready"))
        dve_step = sem("dve_step")
        lam_in, lam_prod, lam_exp = sem("lam_in"), sem("lam_prod"), sem("lam_exp")
        asq_ready, rms_ready, roped = sem("asq_ready"), sem("rms_ready"), sem("roped")
        nmax_ready, w_ready = sem("nmax_ready"), sem("w_ready")
        o_done, o_taken, osq_ready, o_normed, ohi_ready, olo_ready = (
            sem("o_done"), sem("o_taken"), sem("osq_ready"), sem("o_normed"), sem("ohi_ready"), sem("olo_ready"))
        rhi_ready, rlo_ready, member_ready, groups_ready, place_ready, kmoe_in = (
            sem("rhi_ready"), sem("rlo_ready"), sem("member_ready"), sem("groups_ready"), sem("place_ready"),
            sem("kmoe_in"))
        hid_hi_ready, hid_lo_ready = sem("hid_hi_ready"), sem("hid_lo_ready")

        class LoopSems:

            def __init__(self, layer):
                def own(name):
                    return sem(f"{name}_{layer}")

                self.e_in = [own(f"e_in{i}") for i in range(SLOTS)]
                self.e_lo = [own(f"e_lo{i}") for i in range(SLOTS)]
                self.e_used = [own(f"e_used{i}") for i in range(SLOTS)]
                self.e_hi = own("e_hi")
                self.perm_done, self.blk_hi_ready, self.blk_lo_ready = (
                    own("perm_done"), own("blk_hi_ready"), own("blk_lo_ready"))
                self.gate_ready, self.silu_ready, self.hid_ready = (
                    own("gate_ready"), own("silu_ready"), own("hid_ready"))
                self.turned, self.ht_hi_ready, self.ht_lo_ready = (
                    own("turned"), own("ht_hi_ready"), own("ht_lo_ready"))
                self.y_hi_ready, self.y_lo_ready = own("y_hi_ready"), own("y_lo_ready")

        loop_sems = [LoopSems(layer) for layer in range(DEPTH)]
        y_zeroed = sem("y_zeroed")

        def block_count(eng):
            return eng.value_load(blk_grp[0:1, BLOCK_COLS:BLOCK_COLS + 1], min_val=MIN_BLOCKS, max_val=MAX_BLOCKS)

        def last_block(eng):
            return eng.value_load(blk_grp[0:1, BLOCK_COLS + 1:BLOCK_COLS + 2], min_val=MIN_BLOCKS - 1,
                                  max_val=MAX_BLOCKS - 1)
        dt_biased, dt_exp, dt_ln, dt_ready, acs_out, rowb_in = (
            sem("dt_biased"), sem("dt_exp"), sem("dt_ln"), sem("dt_ready"), sem("acs_out"),
            [sem("rowb_in0"), sem("rowb_in1")])
        pads_ready, conv_ready, conv_out = sem("pads_ready"), sem("conv_ready"), sem("conv_out")
        wdt_ready, xw_ready, cb_ready, s0_in, s0_decayed, s1_ready, pf_out = (
            sem("wdt_ready"), sem("xw_ready"), sem("cb_ready"), [sem("s0_in0"), sem("s0_in1")], sem("s0_decayed"), sem("s1_ready"),
            sem("pf_out"))
        seg_ready, seg_exp, seg_masked, row_exp, ce_ready, xdt_ready, y_ready = (
            sem("seg_ready"), sem("seg_exp"), sem("seg_masked"), sem("row_exp"), sem("ce_ready"),
            sem("xdt_ready"), sem("y_ready"))
        ysq_ready, ysq_used, yn_ready, yhi_ready, ylo_ready = (
            sem("ysq_ready"), sem("ysq_used"), sem("yn_ready"), sem("yhi_ready"), sem("ylo_ready"))
        stores = sem("stores")

        def v(name, i=0, n=None):
            a, b = VEC[name]
            return vec[:, a + i:(a + i + n if n else b)]

        def k(name, i=0, n=None):
            a, b = KONST[name]
            return kon[:, a + i:(a + i + n if n else b)]

        def ka(name):
            return katt[:, KATT[name][0]:KATT[name][1]]

        def km(name):
            return kmoe[:, KMOE[name][0]:KMOE[name][1]]

        def ks(name):
            return kssd[:, KSSD[name][0]:KSSD[name][1]]

        def modcol(layer, section, kc, cls):
            j = (section * KC + kc) * 2 + cls
            return mod[:, layer, j // MOD_W, j % MOD_W:j % MOD_W + 1]

        def finished(eng, job):
            eng.wait_ge(jobs_done, job + 1)

        def taken(eng, job):
            b, before = BANK_OF[job]
            eng.wait_ge(bank_taken[b], before + 1)

        def normed(phase, kc):
            return h_moe[:, kc, :] if phase % 2 else h32[:, kc % 2, :]

        def unit(t, j):
            slot = j % SLOTS
            return t[:, slot // 2, (slot % 2) * UNIT:(slot % 2 + 1) * UNIT]

        def by_pool(j):
            return j % 3 == 2

        def bk(job):
            return bank[BANK_OF[job][0]]

        def took(ins, job):
            ins.then_inc(bank_taken[BANK_OF[job][0]], 1)

        def piece(t, name):
            return t[:, SPLIT_NO[name] % SPL, :]

        block = ctx.enter_context(nc.Block())

        @block.sync
        def _(sp):
            def load(pos):
                if pos >= RAW:
                    kind, name = STREAM[pos - RAW]
                    if kind == "mod":
                        sp.wait_ge(mod_used, MOD_NO[name] + 1)
                    elif kind == "split":
                        sp.wait_ge(lo_done, SPLIT_NO[name] + 1)
                    else:
                        finished(sp, LAST_JOB[name])
                sp.dma_start(raw[:, pos % RAW, :], inp["stream"][pos]).then_inc(raw_in[pos % RAW], 16)

            def moe(layer):
                ls = loop_sems[layer]
                sp.wait_ge(groups_ready, layer + 1)
                sp.wait_ge(lo_done, SPLIT_NO[f"sd{layer}"] + 1)
                for slot in range(SLOTS):
                    sp.sem_inc(ls.e_lo[slot], 1)
                count = block_count(sp)
                with sp.Fori(0, count) as it:
                    grp = sp.value_load(blk_grp[0:1, bass.ds(it, 1)], min_val=0, max_val=NGRP - 1)
                    for j in range(GRP_UNITS):
                        sp.wait_ge(ls.e_lo[j % SLOTS], it * SLOT_USES + (1 + j // SLOTS))
                        sp.dma_start(unit(raw, j), inp["experts"][grp * GRP_UNITS + (layer * NGRP * GRP_UNITS + j)]
                                     ).then_inc(ls.e_in[j % SLOTS], 16)
                for slot in range(SLOTS):
                    sp.wait_ge(ls.e_lo[slot], count * SLOT_USES + 1)

            for pos in range(LOOP_AT[0]):
                load(pos)
            moe(0)
            for pos in range(LOOP_AT[0], LOOP_AT[1]):
                load(pos)
            moe(1)
            for kc in range(KC):
                taken(sp, JOB[f"comb1_{kc}"])
                sp.dma_start(out["yT"][:, kc, :], x[:, kc, :]).then_inc(stores, 16)
            sp.wait_ge(stores, 16 * (KC + 4))

        @block.gpsimd
        def _(pool):
            def low_part(q):
                pool.wait_ge(hi_done, q + 1)
                pos = AT[SPLITS[q]]
                pool.tensor_tensor(wlo[:, q % SPL, :], raw[:, pos % RAW, :], whi[:, q % SPL, :].bitcast(F32),
                                   ALU.subtract).then_inc(lo_done, 1)

            def moe(layer):
                ls = loop_sems[layer]
                finished(pool, JOB[f"shu{layer}_3"])
                for t in (yhi_e, ylo_e):
                    pool.memset(t[:, MIN_BLOCKS:, :].bitcast(F32), 0.0).then_inc(y_zeroed, 1)
                pool.wait_ge(groups_ready, layer + 1)
                with pool.Fori(0, block_count(pool)) as it:
                    for j in range(GRP_UNITS):
                        if by_pool(j):
                            pool.wait_ge(ls.e_hi, it * GRP_UNITS + (j + 1))
                            pool.tensor_tensor(unit(wlo, j), unit(raw, j), unit(whi, j).bitcast(F32),
                                               ALU.subtract).then_inc(ls.e_lo[j % SLOTS], 1)

            nlow = [0]

            def low_to(name):
                while nlow[0] <= SPLIT_NO[name]:
                    low_part(nlow[0])
                    nlow[0] += 1

            def scaled_x(phase):
                pool.wait_ge(rstd_ready, phase + 1)
                for kc in range(KC):
                    if kc >= 2:
                        pool.wait_ge(h32_ready, KC * phase + kc - 1)
                    pool.tensor_tensor(xr[:, kc % 2, :], x[:, kc, :], rstd[:, :], ALU.mult).then_inc(xr_ready, 1)

            low_to("bqc2kr")
            scaled_x(0)
            low_to("va_hi")
            cos2 = ka("cos").unsqueeze(1).to_broadcast([P, 2, NLAT])
            pool.wait_ge(katt_in, 16)
            for i, tgt in enumerate(rope_targets(q_a, k_a, q_br, k_br)):
                finished(pool, JOB[f"rope{i}"])
                pool.tensor_tensor(tgt, tgt, cos2, ALU.mult).then_inc(cos_done, 1)
            low_to("sb0")
            scaled_x(1)
            low_to("sd0")
            moe(0)
            low_to("bc23")
            scaled_x(2)
            low_to("zw7")

            dt3 = dts[:, 0, :].rearrange("p (t d) -> p t d", t=TILES)
            pool.wait_ge(wdt_ready, 1)

            for hg in range(2 * SSD_G):
                for t in range(TILES):
                    n = TILES * hg + t
                    if t == 0:
                        taken(pool, JOB[f"xt{hg}_1"])
                    if n >= 2:
                        finished(pool, JOB[f"y{(n - 2) // TILES}_{(n - 2) % TILES}"])
                    for dr in range(2):
                        h = dr * 32 + 4 * hg
                        pool.tensor_tensor(
                            xdt[:, n % 2, dr, :].rearrange("p (h d) -> p h d", h=4),
                            xtok[:, hg % 2, t, :].rearrange("p (h d) -> p h d", h=4),
                            dt3[:, t, h:h + 4].unsqueeze(2).to_broadcast([P, 4, 64]), ALU.mult).then_inc(xdt_ready, 1)
                    if t == 0 and hg % 2 == 0 and hg:
                        low_to(f"sow{hg // 2 - 1}")
                    if t:
                        for dr in range(2):
                            i = (hg * 2 + t - 1) * 2 + dr
                            pool.wait_ge(row_exp, i + 1)
                            e4 = ce[:, n % 2, dr, :].rearrange("p (h l) -> p h l", h=4)
                            pool.tensor_tensor(
                                e4, e4, bc[:, 4 + hg // 2, t * P:(t + 1) * P].unsqueeze(1).to_broadcast([P, 4, P]),
                                ALU.mult).then_inc(ce_ready, 1)
            for c in range(XCH):
                pool.wait_ge(yhi_ready, c + 1)
                pool.tensor_tensor(ylo[:, c, :], xf[:, c, :], yhi[:, c, :].bitcast(F32),
                                   ALU.subtract).then_inc(ylo_ready, 1)
            low_to("sb1")
            scaled_x(3)
            low_to("sd1")
            moe(1)

        @block.scalar
        def _(act):
            def split(q):
                pos = AT[SPLITS[q]]
                act.wait_ge(raw_in[pos % RAW], 16 * (pos // RAW + 1))
                if q >= SPL:
                    finished(act, LAST_JOB[SPLITS[q - SPL]])
                act.copy(whi[:, q % SPL, :], raw[:, pos % RAW, :]).then_inc(hi_done, 1)

            nsplit = [0]

            def split_to(name):
                while nsplit[0] <= SPLIT_NO[name]:
                    split(nsplit[0])
                    nsplit[0] += 1

            def mod_rows(s):
                act.wait_ge(mod_used, MOD_PIECES * (s + 1))
                if s >= MOD_SETS:
                    finished(act, JOB[f"turn{s - MOD_SETS}"])
                elif s:
                    act.wait_ge(mod_turned, s)
                act.copy(modrow[:, :], bank[MOD_BANK][:, :]).then_inc(modrow_ready, 1)

            def norm(phase, x_jobs):
                for kc in range(KC):
                    if x_jobs is not None:
                        taken(act, x_jobs + kc)
                    if kc >= 2:
                        act.wait_ge(sq_used, (KC - 1) * phase + kc - 1)
                    act.activation(squares[phase][:, kc % 2, :], x[:, kc, :], ACT.Square).then_inc(sq_ready, 1)
                n = JOB[f"norm{phase}"]
                finished(act, n)
                took(act.activation(rstd[:, :], bk(n)[:, 0:NTOK], ACT.Sqrt, bias=k("eps"), scale=1.0 / D), n)

            def norm_hi(phase):
                for kc in range(KC):
                    act.wait_ge(h32_ready, KC * phase + kc + 1)
                    act.copy(hhi[:, kc, :], normed(phase, kc)).then_inc(hhi_ready, 1)

            def out_of(job, *pairs):
                finished(act, JOB[job])
                for dst, src in pairs[:-1]:
                    act.copy(dst, src)
                took(act.copy(*pairs[-1]), JOB[job])

            act.dma_start(vec[:, :], inp["vec"]).then_inc(tables_in, 16)
            act.dma_start(kon[:, :], inp["kon"]).then_inc(tables_in, 16)
            act.dma_start(modb[:, :, :, :], inp["modb"]).then_inc(tables_in, 16)
            act.dma_start(x[:, :, :], inp["xT"]).then_inc(x_in, 16)
            act.dma_start(asq[:, 2, 0:256], inp["lam"]).then_inc(lam_in, 16)
            act.wait_ge(tables_in, 48)
            act.wait_ge(silc_zero, 1)
            act.activation(silc[:, :, 0:2], v("c").rearrange("p (k c) -> p k c", c=2), ACT.Silu).then_inc(silc_ready, 1)
            act.wait_ge(x_in, 16)
            norm(0, None)
            act.wait_ge(lam_prod, 2)
            act.activation(lam[:, 2:4], lam[:, 0:2], ACT.Exp).then_inc(lam_exp, 1)
            mod_rows(0)
            split_to("bqc2kr")
            norm_hi(0)
            act.wait_ge(hlo_ready, KC)
            act.dma_start(katt[:, :], inp["katt"]).then_inc(katt_in, 16)
            act.dma_start(k_a[:, :, PAST], inp["cache_ak"]).then_inc(cache_in, 16)
            act.dma_start(v_a[:, 1, :], inp["cache_av"]).then_inc(cache_in, 16)
            act.dma_start(ckv[:, :, PAST], inp["cache_ckv"]).then_inc(cache_in, 16)
            act.dma_start(kr[:, PAST], inp["cache_kr"]).then_inc(cache_in, 16)

            def b(job, w=NTOK):
                return bk(JOB[job])[:, 0:w]

            def to_keys(dst, job):
                return ((dst[:, 0:NPROMPT], b(job)[:, 0:NPROMPT]), (dst[:, 2 * P:KEYS], b(job)[:, NPROMPT:NTOK]))

            rms_no = [0]

            def root(job, width, feats):
                i = rms_no[0]
                rms_no[0] += 1
                if i >= 3:
                    act.wait_ge(rms_ready, i - 2)
                finished(act, JOB[job])
                took(act.activation(ars[:, i % 3, 0:width], b(job, width), ACT.Sqrt, bias=k("eps"), scale=1.0 / feats),
                     JOB[job])

            split_to("kv01")
            out_of("bqc0", (bqc[:, 0, :], b("bqc0")))
            out_of("bqc1", (bqc[:, 1, :], b("bqc1")))
            split_to("aq01")
            out_of("bqc2", (bqc[:, 2, :], b("bqc2")))
            out_of("bkr", *to_keys(kr, "bkr"))
            split_to("aq23")
            out_of("kv0", *to_keys(ckv[:, 0, :], "kv0"))
            out_of("kv1", *to_keys(ckv[:, 1, :], "kv1"))
            out_of("aq0", (q_a[:, 0, :], b("aq0")))
            out_of("aq1", (q_a[:, 1, :], b("aq1")))
            root("N_bqc", NTOK, 384)
            out_of("aq2", (q_a[:, 2, :], b("aq2")))
            out_of("aq3", (q_a[:, 3, :], b("aq3")))
            root("N_kv", NTOK, 256)
            for h in range(HEADS):
                root(f"N_aq{h}", NTOK, DQK)
            for j in range(4):
                out_of(f"wq{j}", (q_b[:, j, :], b(f"wq{j}")))
            for j in range(2):
                out_of(f"wq{4 + j}", (q_br[:, j, :], b(f"wq{4 + j}")))
            for h in range(HEADS):
                out_of(f"kn{h}", (k_b[:, h, :], b(f"kn{h}", KEYS)))
            split_to("ak01")
            for s in range(4):
                out_of(f"vb{s}", (v_b[:, s, :], b(f"vb{s}", KEYS)))
            split_to("ak23")
            for h in range(HEADS):
                root(f"N_bq{h}", NTOK, B_DQK)
            split_to("va_lo")
            for h in range(2):
                out_of(f"ak{h}", *to_keys(k_a[:, h, :], f"ak{h}"))
            split_to("va_hi")
            for h in range(2, 4):
                out_of(f"ak{h}", *to_keys(k_a[:, h, :], f"ak{h}"))
            for h in range(HEADS):
                root(f"N_bk{h}", KEYS, B_DQK)
            for h in range(HEADS):
                root(f"N_ak{h}", NTOK, DQK)
            for t, slot in enumerate((0, 2, 3)):
                out_of(f"va{t}", (v_a[:, slot, :], b(f"va{t}", HEADS * P)))
            mod_rows(1)
            act.wait_ge(rms_ready, 2 + len(RMS_ORDER))
            taken(act, JOB["va2"])
            act.dma_start(out["new_ak"], k_a[:, :, 0:NPROMPT]).then_inc(stores, 16)
            act.dma_start(out["new_av"], v_a[:, 0, :]).then_inc(stores, 16)
            act.dma_start(out["new_ckv"], ckv[:, :, 0:NPROMPT]).then_inc(stores, 16)
            act.dma_start(out["new_kr"], kr[0:64, 0:NPROMPT]).then_inc(stores, 16)
            act.wait_ge(stores, 64)

            for u in range(len(UNITS) + 2):
                if u < len(UNITS):
                    kind, h, t = UNITS[u]
                    nk = NPROMPT if t == 0 else NTOK
                    act.wait_ge(nmax_ready, u + 1)
                    if u >= 2:
                        act.wait_ge(w_ready, u - 1)
                    for i in range(2 if kind == "A" else 1):
                        job = JOB[f"S{u}_{i}"]
                        took(act.activation(e_sb[:, u % 2, i, 0:nk], bk(job)[:, 0:nk], ACT.Exp,
                                            bias=stat[:, u % 2, i:i + 1], scale=1.0,
                                            accum_out=stat[:, u % 2, 2 + i:3 + i]), job)
                if turned_at(u) is not None:
                    mod_rows(MOD_SETS - 1 + turned_at(u))
                if u >= 2:
                    kind, h, t = UNITS[u - 2]
                    nk = NPROMPT if t == 0 else NTOK
                    job = JOB[f"W{u - 2}"]
                    finished(act, job)
                    took(act.copy(wt_sb[:, (u - 2) % 2, 0:nk], bk(job)[:, 0:nk]), job)
                    e = (u - 2) // TILES
                    if (u - 2) % TILES == 1 and e >= 1:
                        act.wait_ge(o_done, e)
                        act.copy(o_sb[:, e - 1, :], bank[O_BANK + (e - 1) % 2][:, 0:NTOK]).then_inc(o_taken, 1)
                if 0 <= u - ROOT_AT < HEADS:
                    h = u - ROOT_AT
                    i = rms_no[0]
                    rms_no[0] += 1
                    if h >= 3:
                        act.wait_ge(o_normed, h - 2)
                    n = JOB[f"N_o{h}"]
                    finished(act, n)
                    took(act.activation(ars[:, i % 3, 0:NTOK], bk(n)[:, 0:NTOK], ACT.Sqrt, bias=k("eps"),
                                        scale=1.0 / P), n)
                if 0 <= u - HI_AT < HEADS:
                    h = u - HI_AT
                    act.wait_ge(o_normed, h + 1)
                    act.copy(hhi[:, h, :], o_sb[:, h, :]).then_inc(ohi_ready, 1)
                if 0 <= u - WO_SPLIT_AT < SPL:
                    split_to(f"wo{u - WO_SPLIT_AT}")
            for h in range(HEADS, 2 * HEADS):
                if h == 2 * HEADS - 1:
                    act.wait_ge(o_done, 2 * HEADS)
                    act.copy(o_sb[:, h, :], bank[O_BANK + h % 2][:, 0:NTOK]).then_inc(o_taken, 1)
                act.wait_ge(o_taken, h + 1)
                act.copy(hhi[:, h, :], o_sb[:, h, :]).then_inc(ohi_ready, 1)

            def moe(layer, x_jobs):
                phase = 2 * layer + 1
                split_to(f"sb{layer}")
                norm(phase, x_jobs)
                act.copy(rhi[:, :, :], v("router").rearrange("p (k e) -> p k e", e=NEXP)).then_inc(rhi_ready, 1)
                norm_hi(phase)
                act.dma_start(kmoe[:, :], inp["kmoe"]).then_inc(kmoe_in, 16)
                n = JOB[f"router{layer}"]
                finished(act, n)
                took(act.activation(score_rows[0:NEXP, :], bk(n)[0:NEXP, 0:NTOK], ACT.Sigmoid), n)
                for i in range(2 * TILES):
                    if i == 2:
                        n = JOB[f"scores{layer}"]
                        finished(act, n)
                        took(act.copy(rt[:, 0, :], bk(n)[:, 0:TILES * NEXP]), n)
                    n = JOB[f"tok{layer}_{i}"]
                    finished(act, n)
                    took(act.copy(h_tok[:, i // 2, (i % 2) * 512:(i % 2 + 1) * 512], bk(n)[:, :]), n)
                split_to(f"sd{layer}")
                for c in range(2):
                    n = JOB[f"shu{layer}_{2 * c}"]
                    finished(act, n)
                    took(act.activation(sg[:, c % 2, :], bk(n)[:, 0:NTOK], ACT.Silu), n)
                for c in range(2):
                    taken(act, JOB[f"shu{layer}_{2 * c + 1}"])
                    act.copy(hidhi[:, c, :], p2[:, c, :]).then_inc(hid_hi_ready, 1)
                n = JOB[f"gate{layer}"]
                finished(act, n)
                took(act.copy(gates[:, :, :], bk(n)[:, 0:BLOCK_COLS * PER_GRP].rearrange("p (b i) -> p b i", b=BLOCK_COLS)), n)
                for b_ in range(MAX_BLOCKS):
                    n = JOB[f"back{layer}_{b_}"]
                    finished(act, n)
                    took(act.copy(back[:, b_, :], bk(n)[:, 0:NTOK]), n)
                ls = loop_sems[layer]

                def blk_part(it):
                    act.wait_ge(ls.perm_done, it * 2 + 2)
                    act.copy(blk_hi[:, 0:4, :], bank[PERM_BANK][:, :].rearrange("p (k f) -> p k f", k=4))
                    act.copy(blk_hi[:, 4:8, :], bank[PERM_BANK + 1][:, :].rearrange("p (k f) -> p k f", k=4)).then_inc(
                        ls.blk_hi_ready, 1)

                def split_e(it, j):
                    act.wait_ge(ls.e_in[j % SLOTS], it * (16 * SLOT_USES) + 16 * (j // SLOTS + 1))
                    act.wait_ge(ls.e_used[j % SLOTS], it * SLOT_USES + (1 + j // SLOTS))
                    act.copy(unit(whi, j), unit(raw, j)).then_inc(ls.e_hi, 1)

                def silu(it, i):
                    j = EXPERT_ORDER.index(f"u{i}_{UP_PARTS - 1}")
                    act.wait_ge(ls.e_used[j % SLOTS], it * SLOT_USES + (2 + j // SLOTS))
                    act.activation(sg_e[:, i % 2, :], bank[U_BANK + i % 2][:, 0:D_EXP], ACT.Silu).then_inc(
                        ls.silu_ready, 1)

                def turned_hi(it, i):
                    act.wait_ge(ls.turned, it * PER_GRP + (i + 1))
                    act.copy(ht_hi[:, i % 2, :, :], bank[T_BANK + i % 2][:, 0:2 * P].rearrange(
                        "p (c t) -> p c t", c=2)).then_inc(ls.ht_hi_ready, 1)

                def result_hi(it):
                    act.wait_ge(ls.e_used[(GRP_UNITS - 1) % SLOTS], it * SLOT_USES + (1 + SLOT_USES))
                    for half in range(2):
                        act.copy(yhi_e[:, bass.ds(it, 1), half * 512:(half + 1) * 512],
                                 bank[Y_BANK + half][:, :].unsqueeze(1)).then_inc(ls.y_hi_ready, 1)

                def one_block(it, last):
                    for j in range(SLOTS, 9):
                        split_e(it, j)
                    silu(it, 0)
                    for j in range(9, 13):
                        split_e(it, j)
                    silu(it, 1)
                    split_e(it, 13)
                    turned_hi(it, 0)
                    for j in range(14, 17):
                        split_e(it, j)
                    silu(it, 2)
                    for j in range(17, 20):
                        split_e(it, j)
                    turned_hi(it, 1)
                    for j in range(20, 23):
                        split_e(it, j)
                    silu(it, 3)
                    split_e(it, 23)
                    if not last:
                        split_e(it + 1, 0)
                    turned_hi(it, 2)
                    if not last:
                        split_e(it + 1, 1)
                        split_e(it + 1, 2)
                    turned_hi(it, 3)
                    if not last:
                        split_e(it + 1, 3)
                    blk_part(it + 1)
                    if not last:
                        split_e(it + 1, 4)
                        split_e(it + 1, 5)
                    result_hi(it)

                for slot in range(SLOTS):
                    act.sem_inc(ls.e_used[slot], 1)
                blk_part(0)
                act.wait_ge(y_zeroed, 2 * (layer + 1))
                act.wait_ge(groups_ready, layer + 1)
                last = last_block(act)
                for j in range(SLOTS):
                    split_e(0, j)
                with act.Fori(0, last) as it:
                    one_block(it, False)
                one_block(last, True)
                if layer < DEPTH - 1:
                    for slot in range(SLOTS):
                        act.wait_ge(ls.e_used[slot], last * SLOT_USES + (1 + SLOT_USES))

            split_to("wo3")
            moe(0, JOB["wo0"])

            split_to("bc23")
            norm(2, JOB["comb0_0"])
            act.dma_start(kssd[:, :], inp["kssd"]).then_inc(kssd_in, 16)
            act.dma_start(kcum[:, :, :], inp["kcum"]).then_inc(kssd_in, 16)
            norm_hi(2)
            split_to("bc01")
            n = JOB["dt"]
            finished(act, n)
            took(act.copy(acsT[0:64, :], bk(n)[0:64, 0:NTOK]), n)
            act.activation(dts[:, 7, 0:64], v("a_log"), ACT.Exp).then_inc(dt_exp, 1)

            def conv_in(job, i):
                if i >= 2:
                    act.wait_ge(conv_ready, i - 1)
                finished(act, job)
                act.copy(cv[:, i % 2, 1:1 + NPROMPT], bk(job)[:, 0:NPROMPT])
                took(act.copy(cv[:, i % 2, 2 + NPROMPT:2 + NTOK], bk(job)[:, NPROMPT:NTOK]), job)

            def conv_silu(i, dst, c):
                act.wait_ge(conv_ready, i + 1)
                bias = v("conv_b", c, 1)
                act.activation(dst[:, 0:NPROMPT], ct[:, i % 2, 0:NPROMPT], ACT.Silu, bias=bias)
                act.activation(dst[:, NPROMPT:NTOK], ct[:, i % 2, NPROMPT + 1:NTOK + 1], ACT.Silu,
                               bias=bias).then_inc(conv_out, 1)

            act.wait_ge(pads_ready, 1)
            chunk = [(JOB[f"bc{i}"], bc[:, i, :], XCH + i) for i in range(8)]
            chunk += [(JOB[f"xs{i}"], xf[:, i, :], i) for i in range(XCH)]

            def conv_step(i):
                if i < len(chunk):
                    conv_in(chunk[i][0], i)
                if 1 <= i:
                    conv_silu(i - 1, chunk[i - 1][1], chunk[i - 1][2])

            act.wait_ge(dt_biased, 1)
            act.activation(dts[:, 2, :], dts[:, 1, :], ACT.Exp, scale=-1.0).then_inc(dt_exp, 1)
            act.wait_ge(dt_biased, 2)
            act.activation(dts[:, 5, :], dts[:, 3, :], ACT.Ln).then_inc(dt_ln, 1)
            split_to("bc23")
            conv_step(0)
            conv_step(1)
            split_to("bc45")
            conv_step(2)
            conv_step(3)
            split_to("bc67")
            n = JOB["cs0"]
            finished(act, n)
            act.activation(dts[:, 6, :], bk(n)[:, 192:384], ACT.Exp)
            took(act.copy(dts[:, 5, :], bk(n)[:, 0:192]), n)
            n = JOB["cs1"]
            finished(act, n)
            took(act.activation(dts[:, 3, :], bk(n)[:, 0:192], ACT.Exp), n)
            conv_step(4)
            conv_step(5)
            split_to("xsw0")
            n = JOB["csT"]
            finished(act, n)
            took(act.copy(acsT[0:64, :], bk(n)[0:64, 0:NTOK]), n)
            taken(act, n)
            act.dma_start(acs_dram, acsT[0:64, :]).then_inc(acs_out, 16)
            conv_step(6)
            conv_step(7)
            for i in range(8):
                split_to(f"xsw{i + 1}" if i < 7 else "zw0")
                conv_step(8 + 2 * i)
                conv_step(9 + 2 * i)
            conv_step(24)
            for i in range(8):
                split_to(f"zw{i + 1}" if i < 7 else "sow0")
                for c in (2 * i, 2 * i + 1):
                    n = JOB[f"z{c}"]
                    finished(act, n)
                    took(act.activation(z[:, c, :], bk(n)[:, 0:NTOK], ACT.Silu), n)
            split_to("sow2")

            def fetch_rows(n):
                hg, t = n // TILES, n % TILES
                if n >= 2:
                    act.wait_ge(seg_ready, 2 * (n - 1))
                for dr in range(2):
                    h = dr * 32 + 4 * hg
                    act.dma_start(rowb[:, n % 2, dr, :].rearrange("p (h l) -> p h l", h=4),
                                  acs_dram[h:h + 4, t * P:(t + 1) * P].partition_broadcast(P)).then_inc(
                        rowb_in[n % 2], 16)

            def fetch_state(hg):
                if hg >= 2:
                    finished(act, JOB[f"y{hg - 2}_2"])
                    act.wait_ge(s0_decayed, 2 * (hg - 1))
                act.dma_start(s0[:, hg % 2, :].rearrange("p (r c) -> p r c", r=2),
                              inp["s0T"][:, :, hg * 256:(hg + 1) * 256]).then_inc(s0_in[hg % 2], 16)

            act.wait_ge(acs_out, 16)
            taken(act, JOB["z15"])
            fetch_state(0)
            fetch_rows(0)
            fetch_rows(1)
            def turned_out(hg):
                if hg % 2 == 0:
                    n = JOB[f"bt{hg // 2}"]
                    out_of(f"bt{hg // 2}", (btok[:, :, :], bk(n)[:, 0:NTOK].rearrange("p (t n) -> p t n", t=TILES)))
                if hg >= 2:
                    act.wait_ge(xw_ready, 4 * (hg - 1))
                    act.wait_ge(xdt_ready, 2 * TILES * (hg - 1))
                out_of(f"xt{hg}_0", (xtok[:, hg % 2, 0:2, :],
                                     bk(JOB[f"xt{hg}_0"])[:, 0:512].rearrange("p (t c) -> p t c", t=2)))
                out_of(f"xt{hg}_1", (xtok[:, hg % 2, 2, :], bk(JOB[f"xt{hg}_1"])[:, 0:256]))

            nexp = 0
            turned_out(0)
            for hg in range(2 * SSD_G):
                for t in range(TILES):
                    n = TILES * hg + t
                    if t:
                        act.wait_ge(rowb_in[n % 2], 32 * (n // 2 + 1))
                        if n >= 2:
                            finished(act, JOB[f"y{(n - 2) // TILES}_{(n - 2) % TILES}"])
                        for dr in range(2):
                            act.activation(ce[:, n % 2, dr, :], rowb[:, n % 2, dr, :], ACT.Exp).then_inc(row_exp, 1)
                            nexp += 1
                    for dr in range(2):
                        act.wait_ge(seg_ready, 2 * n + dr + 1)
                        act.activation(seg[:, n % 2, dr, :], seg[:, n % 2, dr, :], ACT.Exp).then_inc(seg_exp, 1)
                    if t:
                        act.wait_ge(row_exp, nexp)
                    if n + 2 < 6 * SSD_G:
                        fetch_rows(n + 2)
                    if t == 0:
                        if hg:
                            act.wait_ge(pf_out, 32 * hg)
                        out_of(f"st{hg}_0", (pf[:, :], bk(JOB[f"st{hg}_0"])[:, 0:512]))
                        taken(act, JOB[f"st{hg}_0"])
                        for dr in range(2):
                            act.dma_start(out["new_s"][:, dr, hg * 256:(hg + 1) * 256],
                                          pf[:, dr * 256:(dr + 1) * 256]).then_inc(pf_out, 16)
                    if t == 1 and hg + 1 < 2 * SSD_G:
                        turned_out(hg + 1)
                        fetch_state(hg + 1)
            act.wait_ge(y_ready, 2 * SSD_G * TILES)
            def group_squares(g):
                for c in range(4 * g, 4 * g + 4):
                    if c >= 2 and (c - 2) % 4 == 3:
                        finished(act, JOB[f"N_y{(c - 2) // 4}"])
                    elif c >= 2:
                        act.wait_ge(ysq_used, 3 * ((c - 2) // 4) + (c - 2) % 4 + 1)
                    act.activation(ysq[:, c % 2, :], xf[:, c, :], ACT.Square).then_inc(ysq_ready, 1)

            group_squares(0)
            for g in range(SSD_G):
                n = JOB[f"N_y{g}"]
                finished(act, n)
                if g >= 2:
                    act.wait_ge(yn_ready, 4 * (g - 1))
                took(act.activation(yrs[:, g % 2, :], bk(n)[:, 0:NTOK], ACT.Sqrt, bias=k("eps"), scale=1.0 / 512), n)
                if g + 1 < SSD_G:
                    group_squares(g + 1)
                for c in range(4 * g, 4 * g + 4):
                    act.wait_ge(yn_ready, c + 1)
                    act.copy(yhi[:, c, :], xf[:, c, :]).then_inc(yhi_ready, 1)
            for i in range(3, KC):
                split_to(f"sow{i}")
            split_to("sa1")
            act.wait_ge(pf_out, 32 * 2 * SSD_G)
            moe(1, JOB["so0"])

        @block.vector
        def _(dve):
            steps = [0]

            def step(ins):
                ins.then_inc(dve_step, 1)
                steps[0] += 1

            def settle():
                dve.wait_ge(dve_step, steps[0])

            def add_mod(layer, s):
                in_core = (layer, s) in CORE_SETS
                job = JOB[f"turn{CORE_SETS.index((layer, s))}"] if in_core else None
                from_bank = bk(job) if in_core else bank[TURN_BANK]
                turned = from_bank[:, :].rearrange("p (q g c) -> p g q c", q=4, g=MOD_GROUPS)[:, :, :, 0:2]
                dst = mod[:, layer, s, :].rearrange("p (g q c) -> p g q c", g=MOD_GROUPS, q=4)
                add = modb[:, layer, s, :].rearrange("p (g q c) -> p g q c", g=MOD_GROUPS, q=4)
                if in_core:
                    finished(dve, job)
                    took(dve.tensor_tensor(dst, turned, add, ALU.add), job)
                else:
                    dve.wait_ge(mod_turned, s + 1)
                    dve.tensor_tensor(dst, turned, add, ALU.add).then_inc(mod_ready, 1)

            def gains(phase):
                layer, which = divmod(phase, 2)
                for half in range(2):
                    j = ((3 * which + 1) * KC * 2 + half * KC)
                    step(dve.scalar_tensor_tensor(
                        gain[:, phase, half * KC:(half + 1) * KC], mod[:, layer, j // MOD_W, j % MOD_W:j % MOD_W + KC], 1.0,
                        v("norm_g", phase * 2 * KC + half * KC, KC), ALU.add, ALU.mult))
                settle()

            def inverse(phase):
                taken(dve, JOB[f"norm{phase}"])
                dve.reciprocal(rstd[:, :], rstd[:, :]).then_inc(rstd_ready, 1)

            def norm(phase):
                layer, which = divmod(phase, 2)
                for kc in range(KC + 1):
                    if kc < KC:
                        dve.wait_ge(xr_ready, KC * phase + kc + 1)
                        if kc >= 2 and phase % 2 == 0:
                            dve.wait_ge(hlo_ready, KC * phase + kc - 1)
                        for cls, (a, e) in enumerate(CLASSES):
                            ins = dve.tensor_scalar(normed(phase, kc)[:, a:e], xr[:, kc % 2, a:e],
                                                    gain[:, phase, 2 * kc + cls:2 * kc + cls + 1],
                                                    modcol(layer, 3 * which, kc, cls), ALU.mult, ALU.add)
                        ins.then_inc(h32_ready, 1)
                    if kc >= 1:
                        dve.wait_ge(hhi_ready, KC * phase + kc)
                        dve.tensor_tensor(hlo[:, kc - 1, :], normed(phase, kc - 1), hhi[:, kc - 1, :].bitcast(F32),
                                          ALU.subtract).then_inc(hlo_ready, 1)

            dve.memset(silc[:, :, :], 0.0).then_inc(silc_zero, 1)
            dve.wait_ge(tables_in, 48)
            dve.wait_ge(lam_in, 16)
            lam4 = asq[:, 2, 0:256].rearrange("p (a d) -> p a d", a=4)
            for i in range(2):
                step(dve.tensor_tensor(asq[:, i, 0:64], lam4[:, 2 * i, :], lam4[:, 2 * i + 1, :],
                                       ALU.mult))
            settle()
            for i in range(2):
                dve.tensor_reduce(lam[:, i:i + 1], asq[:, i, 0:64], AX.X, ALU.add).then_inc(
                    lam_prod, 1)
            for i, (name, f) in enumerate((("gq_a", A_SCALE), ("gq_bn", B_SCALE), ("gq_br", B_SCALE),
                                           ("sub_g", 1.0 - LAM_INIT))):
                step(dve.tensor_scalar(gq[:, i:i + 1], v(name), f, None, ALU.mult))
            dve.wait_ge(lam_exp, 1)
            step(dve.tensor_tensor(lam[:, 4:5], lam[:, 2:3], lam[:, 3:4], ALU.subtract))
            settle()
            step(dve.tensor_scalar(lam[:, 5:6], lam[:, 4:5], LAM_INIT, None, ALU.add))
            inverse(0)
            add_mod(0, 0)
            dve.wait_ge(mod_ready, 1)
            gains(0)
            norm(0)

            releases = []

            def square(src, w, norm_job, dst=None):
                i = len(releases)
                if dst is None:
                    if i >= 6:
                        finished(dve, JOB[releases[i - 6]])
                    releases.append(norm_job)
                    dst = asq[:, i % 6, 0:w]
                dve.tensor_tensor(dst, src, src, ALU.mult).then_inc(asq_ready, 1)

            roots = [0]

            def scaled(job, width, items):
                i = roots[0]
                roots[0] += 1
                taken(dve, JOB[job])
                r = ars[:, i % 3, 0:width]
                step(dve.reciprocal(r, r))
                settle()
                for j, (dst, src, g, r0, c0, c1) in enumerate(items):
                    ins = dve.scalar_tensor_tensor(dst, src, g, ars[r0:r0 + dst.shape[0], i % 3, c0:c1],
                                                   ALU.mult, ALU.mult)
                    if j == len(items) - 1:
                        ins.then_inc(rms_ready, 1)

            for c in range(3):
                taken(dve, JOB[f"bqc{c}"])
                square(bqc[:, c, :], NTOK, "N_bqc")
            dve.wait_ge(cache_in, 64)
            taken(dve, JOB["bkr"])
            square(kr[:, :], KEYS, None, krsq[:, :])
            for c in range(2):
                taken(dve, JOB[f"kv{c}"])
                i = len(releases)
                releases.append("N_kv")
                dve.tensor_tensor(asq[:, i % 6, 0:NPROMPT], ckv[:, c, 0:NPROMPT], ckv[:, c, 0:NPROMPT], ALU.mult)
                dve.tensor_tensor(asq[:, i % 6, NPROMPT:NTOK], ckv[:, c, 2 * P:KEYS], ckv[:, c, 2 * P:KEYS],
                                  ALU.mult).then_inc(asq_ready, 1)
            for h in range(2):
                taken(dve, JOB[f"aq{h}"])
                square(q_a[:, h, :], NTOK, f"N_aq{h}")
            scaled("N_bqc", NTOK, [(bqc[:, c, :], bqc[:, c, :], v("bqa_g", c, 1), 0, 0, NTOK) for c in range(3)])
            for h in range(2, 4):
                taken(dve, JOB[f"aq{h}"])
                square(q_a[:, h, :], NTOK, f"N_aq{h}")
            scaled("N_kv", NTOK, [(ckv[:, c, ka_:kb_], ckv[:, c, ka_:kb_], v("bkva_g", c, 1), 0, ra, rb)
                                  for c in range(2) for ka_, kb_, ra, rb in ((0, 128, 0, 128), (256, 512, 128, 384))])
            for h in range(HEADS):
                scaled(f"N_aq{h}", NTOK, [(q_a[:, h, :], q_a[:, h, :], gq[:, 0:1], 0, 0, NTOK)])
            for j in range(4):
                taken(dve, JOB[f"wq{j}"])
                square(q_b[:, j, :], NTOK, f"N_bq{j}")
            for j in range(2):
                taken(dve, JOB[f"wq{4 + j}"])
                square(q_br[:, j, :], NTOK, f"N_bq{2 * j + 1}")
            for h in range(HEADS):
                a, e = 64 * (h % 2), 64 * (h % 2) + 64
                scaled(f"N_bq{h}", NTOK, [
                    (q_b[:, h, :], q_b[:, h, :], gq[:, 1:2], 0, 0, NTOK),
                    (q_br[a:e, h // 2, :], q_br[a:e, h // 2, :], gq[a:e, 2:3], a, 0, NTOK)])
            for h in range(HEADS):
                taken(dve, JOB[f"kn{h}"])
                square(k_b[:, h, :], KEYS, f"N_bk{h}")
            dve.wait_ge(cache_in, 64)
            for h in range(HEADS):
                taken(dve, JOB[f"ak{h}"])
                i = len(releases)
                finished(dve, JOB[releases[i - 6]])
                releases.append(f"N_ak{h}")
                dve.tensor_tensor(asq[:, i % 6, 0:NPROMPT], k_a[:, h, 0:NPROMPT], k_a[:, h, 0:NPROMPT], ALU.mult)
                dve.tensor_tensor(asq[:, i % 6, NPROMPT:NTOK], k_a[:, h, 2 * P:KEYS], k_a[:, h, 2 * P:KEYS],
                                  ALU.mult).then_inc(asq_ready, 1)
            for h in range(HEADS):
                a, e = 64 * (h % 2), 64 * (h % 2) + 64
                scaled(f"N_bk{h}", KEYS, [
                    (k_b[:, h, :], k_b[:, h, :], v("gk_bn"), 0, 0, KEYS),
                    (k_br[a:e, h // 2, :], kr[a:e, :], v("gk_br")[a:e, :], a, 0, KEYS)])
            for h in range(HEADS):
                scaled(f"N_ak{h}", NTOK, [(k_a[:, h, ka_:kb_], k_a[:, h, ka_:kb_], v("gk_a"), 0, ra, rb)
                                          for ka_, kb_, ra, rb in ((0, 128, 0, 128), (256, 512, 128, 384))])
            add_mod(0, 1)
            dve.wait_ge(katt_in, 16)
            sin2 = ka("sin").unsqueeze(1).to_broadcast([P, 2, NLAT])
            dve.wait_ge(rms_ready, 2 + len(RMS_ORDER))
            for i, tgt in enumerate(rope_targets(q_a, k_a, q_br, k_br)):
                n = JOB[f"rope{i}"]
                finished(dve, n)
                tmp = asq[:, i % 2, :].rearrange("p (a l) -> p a l", a=2)
                took(dve.tensor_tensor(tmp, bk(n)[:, :].rearrange("p (a l) -> p a l", a=2), sin2, ALU.mult), n)
                taken(dve, n)
                dve.wait_ge(cos_done, i + 1)
                dve.tensor_tensor(tgt, tgt, tmp, ALU.add).then_inc(roped, 1)

            def out_lo(h):
                dve.wait_ge(ohi_ready, h + 1)
                dve.tensor_tensor(hlo[:, h, :], o_sb[:, h, :], hhi[:, h, :].bitcast(F32), ALU.subtract).then_inc(
                    olo_ready, 1)

            dve.wait_ge(stores, 64)
            dve.wait_ge(roped, 6)
            for u in range(len(UNITS) + 1):
                if u < len(UNITS):
                    kind, h, t = UNITS[u]
                    nk = NPROMPT if t == 0 else NTOK
                    maps = 2 if kind == "A" else 1
                    for i in range(maps):
                        job = JOB[f"S{u}_{i}"]
                        finished(dve, job)
                        ins = dve.tensor_reduce(stat[:, u % 2, i:i + 1], bk(job)[:, 0:nk], AX.X, ALU.max, negate=True)
                    ins.then_inc(nmax_ready, 1)
                if turned_at(u) is not None:
                    add_mod(*CORE_SETS[turned_at(u)])
                if u >= 1:
                    w = u - 1
                    kind, h, t = UNITS[w]
                    nk = NPROMPT if t == 0 else NTOK
                    maps = 2 if kind == "A" else 1
                    st = stat[:, w % 2, :]
                    for i in range(maps):
                        taken(dve, JOB[f"S{w}_{i}"])
                    step(dve.reciprocal(st[:, 4:4 + maps], st[:, 2:2 + maps]))
                    settle()
                    if w >= 2:
                        finished(dve, JOB[f"W{w - 2}"])
                    if kind == "A":
                        step(dve.tensor_tensor(st[:, 6:7], st[:, 5:6], lam[:, 5:6], ALU.mult))
                        settle()
                        step(dve.tensor_scalar(e_sb[:, w % 2, 1, 0:nk], e_sb[:, w % 2, 1, 0:nk], st[:, 6:7], None,
                                               ALU.mult))
                        settle()
                        dve.scalar_tensor_tensor(w_sb[:, w % 2, 0:nk], e_sb[:, w % 2, 0, 0:nk], st[:, 4:5],
                                                 e_sb[:, w % 2, 1, 0:nk], ALU.mult, ALU.subtract).then_inc(w_ready, 1)
                    else:
                        dve.tensor_scalar(w_sb[:, w % 2, 0:nk], e_sb[:, w % 2, 0, 0:nk], st[:, 4:5], None,
                                          ALU.mult).then_inc(w_ready, 1)
                if 0 <= u - SQUARE_AT < HEADS:
                    h = u - SQUARE_AT
                    dve.wait_ge(o_taken, h + 1)
                    if h >= 2:
                        finished(dve, JOB[f"N_o{h - 2}"])
                    dve.tensor_tensor(osq[:, h % 2, :], o_sb[:, h, :], o_sb[:, h, :], ALU.mult).then_inc(osq_ready, 1)
                if 0 <= u - SCALE_AT < HEADS:
                    h = u - SCALE_AT
                    i = roots[0]
                    roots[0] += 1
                    taken(dve, JOB[f"N_o{h}"])
                    r = ars[:, i % 3, 0:NTOK]
                    step(dve.reciprocal(r, r))
                    settle()
                    dve.scalar_tensor_tensor(o_sb[:, h, :], o_sb[:, h, :], gq[:, 3:4], r, ALU.mult, ALU.mult).then_inc(
                        o_normed, 1)
                if 0 <= u - LO_AT < HEADS:
                    out_lo(u - LO_AT)
            for h in range(HEADS, 2 * HEADS):
                out_lo(h)

            def residual(job, layer, section, kc):
                finished(dve, job)
                for cls, (a, e) in enumerate(CLASSES):
                    ins = dve.scalar_tensor_tensor(x[:, kc, a:e], bk(job)[:, a:e], modcol(layer, section, kc, cls),
                                                   x[:, kc, a:e], ALU.mult, ALU.add)
                took(ins, job)

            def top_experts(layer):
                E = TILES * NEXP
                G = TILES * NGRP

                def col(i, w=E):
                    return rt[:, i, 0:w]

                def e3(i):
                    return rt[:, i, :].rearrange("p (t e) -> p t e", e=NEXP)

                def g3(i):
                    return rt[:, i, :].rearrange("p (g e) -> p g e", e=NGRP)

                def do(ins):
                    step(ins)
                    settle()

                taken(dve, JOB[f"scores{layer}"])
                do(dve.tensor_tensor(e3(1), e3(0), v("rbias").unsqueeze(1).to_broadcast([P, TILES, NEXP]), ALU.add))
                s = g3(1)
                pairs = s.rearrange("p g (a b) -> p g a b", a=2)
                hi4 = col(2, 2 * G).rearrange("p (g a) -> p g a", a=2)
                lo4 = col(3, 2 * G).rearrange("p (g a) -> p g a", a=2)
                do(dve.tensor_tensor(hi4, pairs[:, :, :, 0], pairs[:, :, :, 1], ALU.max))
                do(dve.tensor_tensor(lo4, pairs[:, :, :, 0], pairs[:, :, :, 1], ALU.min))
                best, m2, m3 = col(4, G), col(5, G), col(6, G)
                do(dve.tensor_tensor(best, hi4[:, :, 0], hi4[:, :, 1], ALU.max))
                do(dve.tensor_tensor(m2, hi4[:, :, 0], hi4[:, :, 1], ALU.min))
                do(dve.tensor_tensor(m3, lo4[:, :, 0], lo4[:, :, 1], ALU.max))
                do(dve.tensor_tensor(m2, m2, m3, ALU.max))
                do(dve.tensor_tensor(best, best, m2, ALU.add))
                b3 = best.rearrange("p (t g) -> p t g", t=TILES)
                gm = col(5, TILES)
                do(dve.tensor_reduce(gm, b3, AX.X, ALU.max))
                key = col(6, G).rearrange("p (t g) -> p t g", t=TILES)
                do(dve.tensor_tensor(key, b3, gm.unsqueeze(2).to_broadcast([P, TILES, NGRP]), ALU.is_equal))
                do(dve.tensor_tensor(key, key, k("rank4").unsqueeze(1).to_broadcast([P, TILES, NGRP]), ALU.mult))
                do(dve.tensor_reduce(gm, key, AX.X, ALU.max))
                do(dve.tensor_tensor(key, key, gm.unsqueeze(2).to_broadcast([P, TILES, NGRP]), ALU.is_equal))
                dve.tensor_scalar(col(11, G), col(6, G), 1.0, None, ALU.mult).then_inc(member_ready, 1)
                do(dve.tensor_tensor(g3(7), s, col(6, G).unsqueeze(2).to_broadcast([P, G, NGRP]), ALU.mult))
                do(dve.tensor_scalar(key, key, -1.0, BIG, ALU.add, ALU.mult))
                do(dve.tensor_tensor(g3(7), g3(7), col(6, G).unsqueeze(2).to_broadcast([P, G, NGRP]), ALU.add))
                for one in (8, 9):
                    do(dve.tensor_reduce(gm, e3(7), AX.X, ALU.max))
                    do(dve.tensor_tensor(e3(one), e3(7), gm.unsqueeze(2).to_broadcast([P, TILES, NEXP]), ALU.is_equal))
                    do(dve.tensor_tensor(e3(one), e3(one), k("rank16").unsqueeze(1).to_broadcast([P, TILES, NEXP]),
                                         ALU.mult))
                    do(dve.tensor_reduce(gm, e3(one), AX.X, ALU.max))
                    do(dve.tensor_tensor(e3(one), e3(one), gm.unsqueeze(2).to_broadcast([P, TILES, NEXP]),
                                         ALU.is_equal))
                    if one == 8:
                        do(dve.scalar_tensor_tensor(col(7), col(8), -3.0 * BIG, col(7), ALU.mult, ALU.add))
                do(dve.tensor_tensor(col(8), col(8), col(9), ALU.add))
                do(dve.tensor_tensor(col(8), col(8), col(0), ALU.mult))
                do(dve.tensor_reduce(gm, e3(8), AX.X, ALU.add))
                do(dve.reciprocal(gm, gm))
                do(dve.tensor_tensor(e3(10), e3(8), gm.unsqueeze(2).to_broadcast([P, TILES, NEXP]), ALU.mult))
                do(dve.tensor_reduce(rt[:, 12, 0:TILES * PER_GRP].rearrange("p (t i) -> p t i", t=TILES),
                                     rt[:, 10, :].rearrange("p (t g i) -> p t i g", g=NGRP, i=PER_GRP), AX.X, ALU.add))

            def find_places(layer):
                def do(ins):
                    step(ins)
                    settle()

                n = JOB[f"rank{layer}"]
                finished(dve, n)
                took(dve.tensor_copy(nums[:, 0, :], bk(n)[:, 0:16]), n)
                taken(dve, n)
                count, blocks, start = nums[:, 0, 12:16], nums[:, 1, 0:NGRP], nums[:, 2, 0:NGRP]
                dve.wait_ge(kmoe_in, 16 * (layer + 1))
                do(dve.tensor_scalar(blocks, count, 0.0, None, ALU.is_gt))
                for full in range(1, TILES):
                    do(dve.scalar_tensor_tensor(blocks, count, float(full * P), blocks, ALU.is_gt, ALU.add))
                do(dve.tensor_scalar(nums[:, 2, 0:1], blocks[:, 0:1], 0.0, None, ALU.mult))
                for g in range(1, NGRP):
                    do(dve.tensor_tensor(start[:, g:g + 1], start[:, g - 1:g], blocks[:, g - 1:g], ALU.add))
                which = nums[:, 3, 0:8]
                do(dve.tensor_scalar(which, km("blocks"), start[:, 1:2], None, ALU.is_ge))
                for g in range(2, NGRP):
                    do(dve.scalar_tensor_tensor(which, km("blocks"), start[:, g:g + 1], which, ALU.is_ge, ALU.add))
                do(dve.tensor_tensor(nums[:, 3, BLOCK_COLS:BLOCK_COLS + 1], start[:, NGRP - 1:NGRP],
                                     blocks[:, NGRP - 1:NGRP], ALU.add))
                do(dve.tensor_scalar(nums[:, 3, BLOCK_COLS + 1:BLOCK_COLS + 2], nums[:, 3, BLOCK_COLS:BLOCK_COLS + 1],
                                     -1.0, None, ALU.add))
                dve.tensor_copy(blk_grp[:, 0:BLOCK_COLS + 2], nums[:, 3, 0:BLOCK_COLS + 2]).then_inc(groups_ready, 1)
                g3 = nums[:, 4, 0:TILES * NGRP].rearrange("p (t g) -> p t g", t=TILES)
                do(dve.scalar_tensor_tensor(g3, start.unsqueeze(1).to_broadcast([P, TILES, NGRP]), float(P),
                                            nums[:, 0, 0:TILES * NGRP].rearrange("p (t g) -> p t g", t=TILES),
                                            ALU.mult, ALU.add))
                do(dve.tensor_tensor(g3, g3, rt[:, 11, 0:TILES * NGRP].rearrange("p (t g) -> p t g", t=TILES), ALU.mult))
                do(dve.tensor_reduce(nums[:, 5, 0:TILES], g3, AX.X, ALU.add))
                for t in range(TILES):
                    dve.tensor_scalar(place[:, t, :], km("slots"), nums[:, 5, t:t + 1], None, ALU.is_equal).then_inc(
                        place_ready, 1)

            def moe(layer):
                phase = 2 * layer + 1
                gains(phase)
                dve.wait_ge(rhi_ready, layer + 1)
                dve.tensor_tensor(rlo[:, :, :], v("router").rearrange("p (k e) -> p k e", e=NEXP),
                                  rhi[:, :, :].bitcast(F32), ALU.subtract).then_inc(rlo_ready, 1)
                inverse(phase)
                norm(phase)
                top_experts(layer)
                for c in range(2):
                    n = JOB[f"shu{layer}_{2 * c + 1}"]
                    taken(dve, n - 1)
                    finished(dve, n)
                    took(dve.tensor_tensor(p2[:, c, :], sg[:, c, :], bk(n)[:, 0:NTOK], ALU.mult), n)
                for c in range(2):
                    dve.wait_ge(hid_hi_ready, 2 * layer + c + 1)
                    dve.tensor_tensor(hidlo[:, c, :], p2[:, c, :], hidhi[:, c, :].bitcast(F32),
                                      ALU.subtract).then_inc(hid_lo_ready, 1)
                find_places(layer)
                for kc in range(KC):
                    residual(JOB[f"shd{layer}_{kc}"], layer, 5, kc)
                ls = loop_sems[layer]

                def blk_part(it):
                    dve.wait_ge(ls.blk_hi_ready, it + 1)
                    for half in range(2):
                        ks_ = slice(4 * half, 4 * half + 4)
                        ins = dve.tensor_tensor(blk_lo[:, ks_, :],
                                                bank[PERM_BANK + half][:, :].rearrange("p (k f) -> p k f", k=4),
                                                blk_hi[:, ks_, :].bitcast(F32), ALU.subtract)
                    ins.then_inc(ls.blk_lo_ready, 1)

                def low_e(it, j):
                    if not by_pool(j):
                        dve.wait_ge(ls.e_hi, it * GRP_UNITS + (j + 1))
                        dve.tensor_tensor(unit(wlo, j), unit(raw, j), unit(whi, j).bitcast(F32),
                                          ALU.subtract).then_inc(ls.e_lo[j % SLOTS], 1)

                def hidden(it, i):
                    dve.wait_ge(ls.silu_ready, it * PER_GRP + (i + 1))
                    dve.scalar_tensor_tensor(hid_e[:, i % 2, :], bank[U_BANK + i % 2][:, D_EXP:2 * D_EXP],
                                             gate_now[:, i:i + 1], sg_e[:, i % 2, :], ALU.mult,
                                             ALU.mult).then_inc(ls.hid_ready, 1)

                def turned_lo(it, i):
                    dve.wait_ge(ls.ht_hi_ready, it * PER_GRP + (i + 1))
                    dve.tensor_tensor(ht_lo[:, i % 2, :, :], bank[T_BANK + i % 2][:, 0:2 * P].rearrange(
                        "p (c t) -> p c t", c=2), ht_hi[:, i % 2, :, :].bitcast(F32), ALU.subtract).then_inc(
                        ls.ht_lo_ready, 1)

                def result_lo(it):
                    for half in range(2):
                        part = (slice(None), bass.ds(it, 1), slice(half * 512, (half + 1) * 512))
                        dve.wait_ge(ls.y_hi_ready, it * 2 + (half + 1))
                        dve.tensor_tensor(ylo_e[part], bank[Y_BANK + half][:, :].unsqueeze(1), yhi_e[part].bitcast(F32),
                                          ALU.subtract).then_inc(ls.y_lo_ready, 1)

                def one_block(it, last):
                    dve.tensor_copy(gate_now[:, :].unsqueeze(1), gates[:, bass.ds(it, 1), :]).then_inc(ls.gate_ready, 1)
                    for j in range(SLOTS, 9):
                        low_e(it, j)
                    dve.wait_ge(ls.gate_ready, it + 1)
                    hidden(it, 0)
                    for j in range(9, 13):
                        low_e(it, j)
                    hidden(it, 1)
                    low_e(it, 13)
                    turned_lo(it, 0)
                    for j in range(14, 17):
                        low_e(it, j)
                    hidden(it, 2)
                    for j in range(17, 20):
                        low_e(it, j)
                    turned_lo(it, 1)
                    for j in range(20, 23):
                        low_e(it, j)
                    hidden(it, 3)
                    low_e(it, 23)
                    if not last:
                        low_e(it + 1, 0)
                    turned_lo(it, 2)
                    if not last:
                        low_e(it + 1, 1)
                        low_e(it + 1, 2)
                    turned_lo(it, 3)
                    if not last:
                        low_e(it + 1, 3)
                    blk_part(it + 1)
                    if not last:
                        low_e(it + 1, 4)
                        low_e(it + 1, 5)
                    result_lo(it)

                blk_part(0)
                dve.wait_ge(y_zeroed, 2 * (layer + 1))
                dve.wait_ge(groups_ready, layer + 1)
                last = last_block(dve)
                taken(dve, JOB[f"gate{layer}"])
                for j in range(SLOTS):
                    low_e(0, j)
                with dve.Fori(0, last) as it:
                    one_block(it, False)
                one_block(last, True)
                for kc in range(KC):
                    residual(JOB[f"comb{layer}_{kc}"], layer, 5, kc)

            dve.wait_ge(mod_ready, 2)
            taken(dve, JOB["turn0"])
            for kc in range(KC):
                residual(JOB[f"wo{kc}"], 0, 2, kc)
            moe(0)

            for i in range(1, len(CORE_SETS)):
                taken(dve, JOB[f"turn{i}"])
            gains(2)
            inverse(2)
            norm(2)
            for i in range(2):
                for c in (0, 1 + NPROMPT, 2 + NTOK):
                    ins = dve.memset(cv[:, i, c:c + 1], 0.0)
            ins.then_inc(pads_ready, 1)
            n = JOB["dtT"]
            finished(dve, n)
            took(dve.tensor_tensor(dts[:, 0, :].rearrange("p (t d) -> p t d", t=TILES),
                                   bk(n)[:, 0:192].rearrange("p (t d) -> p t d", t=TILES),
                                   v("dt_bias").unsqueeze(1).to_broadcast([P, TILES, 64]), ALU.add), n)
            taken(dve, n)
            dve.scalar_tensor_tensor(dts[:, 1, :], dts[:, 0, :], -1.0, dts[:, 0, :], ALU.mult, ALU.max).then_inc(
                dt_biased, 1)
            dve.wait_ge(dt_exp, 2)
            dve.tensor_scalar(dts[:, 3, :], dts[:, 2, :], 1.0, None, ALU.add).then_inc(dt_biased, 1)
            dve.wait_ge(dt_biased, 2)
            step(dve.tensor_scalar(dts[:, 4, :], dts[:, 3, :], -1.0, None, ALU.add))
            settle()
            step(dve.tensor_scalar(dts[:, 1, :], dts[:, 4, :], 0.0, None, ALU.is_equal))
            settle()
            step(dve.tensor_tensor(dts[:, 4, :], dts[:, 4, :], dts[:, 1, :], ALU.add))
            settle()
            step(dve.reciprocal(dts[:, 4, :], dts[:, 4, :]))
            dve.wait_ge(dt_ln, 1)
            step(dve.tensor_tensor(dts[:, 5, :], dts[:, 5, :], dts[:, 1, :], ALU.add))
            settle()
            step(dve.tensor_tensor(dts[:, 5, :], dts[:, 5, :], dts[:, 4, :], ALU.mult))
            settle()
            step(dve.tensor_tensor(dts[:, 5, :], dts[:, 5, :], dts[:, 2, :], ALU.mult))
            settle()
            step(dve.scalar_tensor_tensor(dts[:, 0, :], dts[:, 0, :], 0.0, dts[:, 5, :], ALU.max, ALU.add))
            settle()
            step(dve.tensor_scalar(dts[:, 7, 0:64], dts[:, 7, 0:64], -1.0, None, ALU.mult))
            settle()
            dve.tensor_tensor(dts[:, 1, :].rearrange("p (t d) -> p t d", t=TILES),
                              dts[:, 0, :].rearrange("p (t d) -> p t d", t=TILES),
                              dts[:, 7, 0:64].unsqueeze(1).to_broadcast([P, TILES, 64]), ALU.mult).then_inc(dt_ready, 1)

            def conv(i):
                job, c = (JOB[f"bc{i}"], XCH + i) if i < 8 else (JOB[f"xs{i - 8}"], i - 8)
                taken(dve, job)
                if i >= 2:
                    dve.wait_ge(conv_out, i - 1)
                w = NTOK + 1
                t = ct[:, i % 2, 0:w]
                step(dve.tensor_scalar(t, cv[:, i % 2, 0:w], v("conv_w", c, 1), None, ALU.mult))
                settle()
                step(dve.scalar_tensor_tensor(t, cv[:, i % 2, 1:1 + w], v("conv_w", 24 + c, 1), t, ALU.mult, ALU.add))
                settle()
                dve.scalar_tensor_tensor(t, cv[:, i % 2, 2:2 + w], v("conv_w", 48 + c, 1), t, ALU.mult,
                                         ALU.add).then_inc(conv_ready, 1)

            for i in range(4):
                conv(i)
            taken(dve, JOB["cs1"])
            dve.tensor_tensor(dts[:, 4, :], dts[:, 3, :], dts[:, 0, :], ALU.mult).then_inc(wdt_ready, 1)
            for i in range(4, 24):
                conv(i)

            def gated(hg, t):
                n = JOB[f"y{hg}_{t}"]
                ts = slice(t * P, (t + 1) * P)
                finished(dve, n)
                for c in range(2):
                    ins = dve.scalar_tensor_tensor(xf[:, 2 * hg + c, ts], xf[:, 2 * hg + c, ts],
                                                   v("ssd_d", 2 * hg + c, 1), bk(n)[:, c * P:(c + 1) * P],
                                                   ALU.mult, ALU.add)
                took(ins, n)
                taken(dve, n)
                both = slice(2 * hg, 2 * hg + 2)
                dve.tensor_tensor(xf[:, both, ts], xf[:, both, ts], z[:, both, ts], ALU.mult).then_inc(y_ready, 1)

            acs3 = dts[:, 5, :].rearrange("p (t d) -> p t d", t=TILES)
            dec3 = dts[:, 6, :].rearrange("p (t d) -> p t d", t=TILES)
            dve.wait_ge(kssd_in, 32)

            def masked_cb(g):
                n = JOB[f"cb{g}"]
                finished(dve, n)
                if g:
                    dve.wait_ge(seg_masked, 12 * g)
                c3 = bk(n)[:, 0:NTOK].rearrange("p (t l) -> p t l", t=TILES)
                dve.tensor_tensor(cbm[:, 0, :, :], c3, ks("upto").unsqueeze(1).to_broadcast([P, TILES, P]), ALU.mult)
                took(dve.tensor_tensor(cbm[:, 1, :, :], c3, ks("since").unsqueeze(1).to_broadcast([P, TILES, P]),
                                       ALU.mult), n)
                taken(dve, n)

            def next_state(hg):
                dve.wait_ge(s0_in[hg % 2], 16 * (hg // 2 + 1))
                for dr, t in ((0, 1), (1, 2)):
                    h = dr * 32 + 4 * hg
                    dve.tensor_tensor(
                        s1[hg % 2][:, dr * 256:(dr + 1) * 256].rearrange("p (h d) -> p h d", h=4),
                        s0[:, hg % 2, dr * 256:(dr + 1) * 256].rearrange("p (h d) -> p h d", h=4),
                        dec3[:, t, h:h + 4].unsqueeze(2).to_broadcast([P, 4, 64]), ALU.mult).then_inc(s0_decayed, 1)
                n = JOB[f"st{hg}_1"]
                finished(dve, n)
                dve.wait_ge(s0_decayed, 2 * (hg + 1))
                took(dve.tensor_tensor(s1[hg % 2][:, :], s1[hg % 2][:, :], bk(n)[:, 0:512], ALU.add), n)

            def segments(n):
                hg, t = divmod(n, TILES)
                dve.wait_ge(rowb_in[n % 2], 32 * (n // 2 + 1))
                if n >= 2:
                    finished(dve, JOB[f"y{(n - 2) // TILES}_{(n - 2) % TILES}"])
                for dr in range(2):
                    for i in range(4):
                        h = dr * 32 + 4 * hg + i
                        ins = dve.tensor_scalar(seg[:, n % 2, dr, i * P:(i + 1) * P],
                                                rowb[:, n % 2, dr, i * P:(i + 1) * P],
                                                acs3[:, t, h:h + 1], 0.0, ALU.subtract, ALU.min)
                    ins.then_inc(seg_ready, 1)

            def weighted_x(hg):
                taken(dve, JOB[f"xt{hg}_1"])
                if hg:
                    finished(dve, JOB[f"st{hg - 1}_1"])
                for i, (t, dr) in enumerate(((0, 0), (0, 1), (1, 0), (2, 1))):
                    h = dr * 32 + 4 * hg
                    dve.tensor_tensor(
                        xw[:, i, :].rearrange("p (h d) -> p h d", h=4),
                        xtok[:, hg % 2, t, :].rearrange("p (h d) -> p h d", h=4),
                        wdt3[:, t, h:h + 4].unsqueeze(2).to_broadcast([P, 4, 64]), ALU.mult).then_inc(xw_ready, 1)

            wdt3 = dts[:, 4, :].rearrange("p (t d) -> p t d", t=TILES)
            weighted_x(0)
            masked_cb(0)
            segments(0)
            for n in range(TILES * 2 * SSD_G):
                hg, t = divmod(n, TILES)
                for dr in range(2):
                    dve.wait_ge(seg_exp, 2 * n + dr + 1)
                    s4 = seg[:, n % 2, dr, :].rearrange("p (h l) -> p h l", h=4)
                    dve.tensor_tensor(s4, s4, cbm[:, dr, t, :].unsqueeze(1).to_broadcast([P, 4, P]),
                                      ALU.mult).then_inc(seg_masked, 1)
                if n % 6 == 5 and hg + 1 < 2 * SSD_G:
                    masked_cb(n // 6 + 1)
                if n + 1 < TILES * 2 * SSD_G:
                    segments(n + 1)
                if t == 2 and hg + 1 < 2 * SSD_G:
                    weighted_x(hg + 1)
                if n:
                    gated((n - 1) // TILES, (n - 1) % TILES)
                if t == 0:
                    next_state(hg)
            gated(2 * SSD_G - 1, TILES - 1)
            for g in range(SSD_G):
                taken(dve, JOB[f"N_y{g}"])
                r = yrs[:, g % 2, :]
                step(dve.reciprocal(r, r))
                settle()
                for c in range(4 * g, 4 * g + 4):
                    dve.scalar_tensor_tensor(xf[:, c, :], xf[:, c, :], v("ssd_g", c, 1), r, ALU.mult,
                                             ALU.mult).then_inc(yn_ready, 1)
            for kc in range(KC):
                residual(JOB[f"so{kc}"], 1, 2, kc)
            moe(1)

        @block.tensor
        def _(pe):
            def opened(job):
                b, before = BANK_OF[job]
                if before:
                    pe.wait_ge(bank_taken[b], before)
                return bk(job)

            def mm3(dst, whi_, wlo_, xhi_, xlo_, first, last):
                pe.matmul(dst, whi_, xhi_, start=first, stop=False)
                pe.matmul(dst, whi_, xlo_, start=False, stop=False)
                return pe.matmul(dst, wlo_, xhi_, start=False, stop=last)

            def split_in(name):
                pe.wait_ge(lo_done, SPLIT_NO[name] + 1)

            def mod_piece(name):
                layer, s, m_ = name
                pos = AT[name]
                pe.wait_ge(raw_in[pos % RAW], 16 * (pos // RAW + 1))
                if m_ == 0:
                    if name == (0, 0, 0):
                        pe.wait_ge(silc_ready, 1)
                    else:
                        pe.wait_ge(modrow_ready, layer * MOD_SETS + s)
                for grp in range(MOD_GROUPS):
                    ins = pe.matmul(bank[MOD_BANK][32 * grp:32 * grp + 32, :], silc[:, m_, :],
                                    raw[:, pos % RAW, grp * 512:(grp + 1) * 512], start=m_ == 0, stop=m_ == KC - 1,
                                    skip_group_check=True)
                ins.then_inc(mod_used, 1)

            def turn_mod(layer, s):
                in_core = (layer, s) in CORE_SETS
                dst = opened(JOB[f"turn{CORE_SETS.index((layer, s))}"]) if in_core else bank[TURN_BANK]
                pe.wait_ge(modrow_ready, layer * MOD_SETS + s + 1)
                if s and not in_core:
                    pe.wait_ge(mod_ready, s)
                for q in range(4):
                    ins = pe.transpose(dst[:, q * P:(q + 1) * P], modrow[:, q * P:(q + 1) * P], k("ident"))
                ins.then_inc(jobs_done if in_core else mod_turned, 1)

            def norm(phase):
                n = JOB[f"norm{phase}"]
                dst = opened(n)[:, 0:NTOK]
                for kc in range(KC):
                    pe.wait_ge(sq_ready, KC * phase + kc + 1)
                    ins = pe.matmul(dst, k("ones"), squares[phase][:, kc % 2, :], start=kc == 0, stop=kc == KC - 1)
                    ins.then_inc(sq_used if kc < KC - 1 else jobs_done, 1)

            def pair(name, jobs, rhi_, rlo_, kcs=KC, as_normed=False):
                wh = piece(whi, name).rearrange("p (c k f) -> p c k f", k=kcs, f=P)
                wl = piece(wlo, name).rearrange("p (c k f) -> p c k f", k=kcs, f=P)
                split_in(name)
                for c, job in enumerate(jobs):
                    dst = opened(job)[:, 0:NTOK]
                    for kc in range(kcs):
                        if as_normed and c == 0:
                            pe.wait_ge(hlo_ready, kc + 1)
                        ins = mm3(dst, wh[:, c, kc, :], wl[:, c, kc, :], rhi_[:, kc, :], rlo_[:, kc, :],
                                  kc == 0, kc == kcs - 1)
                    ins.then_inc(jobs_done, 1)

            def group(job, width, parts):
                dst = opened(JOB[job])[:, 0:width]
                for i, (lhs, rhs) in enumerate(parts):
                    ins = pe.matmul(dst, lhs, rhs, start=i == 0, stop=i == len(parts) - 1)
                ins.then_inc(jobs_done, 1)

            pe.wait_ge(tables_in, 48)
            for m_ in range(MOD_PIECES):
                mod_piece((0, 0, m_))
                if m_ == 3:
                    norm(0)
            turn_mod(0, 0)
            late = [(0, 1, i) for i in range(MOD_PIECES)]
            mod_piece(late[0])
            mod_piece(late[1])
            pair("bqc01", [JOB["bqc0"], JOB["bqc1"]], hhi, hlo, as_normed=True)
            pair("bqc2kr", [JOB["bqc2"], JOB["bkr"]], hhi, hlo)
            pair("kv01", [JOB["kv0"], JOB["kv1"]], hhi, hlo)
            mod_piece(late[2])
            pair("aq01", [JOB["aq0"], JOB["aq1"]], hhi, hlo)
            mod_piece(late[3])
            ones = k("ones")
            pe.wait_ge(asq_ready, 3)
            group("N_bqc", NTOK, [(ones, asq[:, i, 0:NTOK]) for i in range(3)])
            pair("aq23", [JOB["aq2"], JOB["aq3"]], hhi, hlo)
            mod_piece(late[4])
            pe.wait_ge(asq_ready, 6)
            group("N_kv", NTOK, [(ones, asq[:, i, 0:NTOK]) for i in (3, 4)])
            pe.wait_ge(katt_in, 16)
            block_ones = ka("block")
            for h in range(HEADS):
                pe.wait_ge(asq_ready, 7 + h)
                group(f"N_aq{h}", NTOK, [(block_ones, asq[:, (5 + h) % 6, 0:NTOK])])
            pe.wait_ge(rms_ready, 1)
            for i, name in enumerate(("wq012", "wq345")):
                pos = AT[name]
                pe.wait_ge(raw_in[pos % RAW], 16 * (pos // RAW + 1))
                w = raw[:, pos % RAW, 0:3 * 3 * P].rearrange("p (c k f) -> p c k f", c=3, k=3)
                for c in range(3):
                    n = JOB[f"wq{3 * i + c}"]
                    dst = opened(n)[:, 0:NTOK]
                    for kc in range(3):
                        ins = pe.matmul(dst, w[:, c, kc, :], bqc[:, kc, :], start=kc == 0, stop=kc == 2)
                    ins.then_inc(jobs_done, 1)
            pe.wait_ge(rms_ready, 2)
            pe.wait_ge(cache_in, 64)
            pos = AT["wkv"]
            pe.wait_ge(raw_in[pos % RAW], 16 * (pos // RAW + 1))
            wk = raw[:, pos % RAW, 0:1024].rearrange("p (c k f) -> p c k f", c=4, k=2)
            wv = raw[:, pos % RAW, 1024:2048].rearrange("p (k f) -> p k f", k=2)
            for h in range(HEADS):
                dst = opened(JOB[f"kn{h}"])[:, :]
                for kc in range(2):
                    ins = pe.matmul(dst, wk[:, h, kc, :], ckv[:, kc, :], start=kc == 0, stop=kc == 1)
                ins.then_inc(jobs_done, 1)
            for s in range(4):
                dst = opened(JOB[f"vb{s}"])[:, :]
                for kc in range(2):
                    ins = pe.matmul(dst, ckv[:, kc, s * P:(s + 1) * P], wv[:, kc, :], start=kc == 0, stop=kc == 1)
                ins.then_inc(jobs_done, 1)
            for h in range(HEADS):
                pe.wait_ge(asq_ready, 16 if h > 1 else 15)
                a = 64 * (h % 2)
                group(f"N_bq{h}", NTOK, [(ones, asq[:, (9 + h) % 6, 0:NTOK]),
                                         (ones[a:a + 64, :], asq[a:a + 64, (13 + h // 2) % 6, 0:NTOK])])
            pair("ak01", [JOB["ak0"], JOB["ak1"]], hhi, hlo)
            pair("ak23", [JOB["ak2"], JOB["ak3"]], hhi, hlo)
            for h in range(HEADS):
                pe.wait_ge(asq_ready, 17 + h)
                group(f"N_bk{h}", KEYS, [(ones, asq[:, (15 + h) % 6, :]), (ones[0:64, :], krsq[0:64, :])])
            for h in range(HEADS):
                pe.wait_ge(asq_ready, 21 + h)
                group(f"N_ak{h}", NTOK, [(block_ones, asq[:, (19 + h) % 6, 0:NTOK])])
            split_in("va_lo")
            split_in("va_hi")
            for t in range(TILES):
                dst = opened(JOB[f"va{t}"])[:, :]
                for kc in range(KC):
                    name = "va_lo" if kc < 4 else "va_hi"
                    wh = piece(whi, name).rearrange("p (k f) -> p k f", k=4)[:, kc % 4, :]
                    wl = piece(wlo, name).rearrange("p (k f) -> p k f", k=4)[:, kc % 4, :]
                    ins = mm3(dst, hhi[:, kc, t * P:(t + 1) * P], hlo[:, kc, t * P:(t + 1) * P], wh, wl,
                              kc == 0, kc == KC - 1)
                ins.then_inc(jobs_done, 1)
            for i in range(LATE_EARLY, MOD_PIECES):
                mod_piece(late[i])
            turn_mod(0, 1)
            for i, tgt in enumerate(rope_targets(q_a, k_a, q_br, k_br)):
                pe.wait_ge(rms_ready, 2 + (4, 4, 16, 16, 8, 12)[i])
                n = JOB[f"rope{i}"]
                dst = opened(n)[:, :].rearrange("p (a l) -> p a l", a=2)
                pe.matmul(dst, ka("rot"), tgt, start=True, stop=True).then_inc(jobs_done, 1)

            pe.wait_ge(roped, 6)
            pe.wait_ge(mod_ready, 2)
            for i in range(JOB_BANKS):
                taken(pe, JOB["S0_0"] - 1 - i)
            for u in range(len(UNITS) + 3):
                if u < len(UNITS):
                    kind, h, t = UNITS[u]
                    k0, k1 = (0, NPROMPT) if t == 0 else (NPROMPT, KEYS)
                    qs = slice(t * P, (t + 1) * P)
                    if kind == "A":
                        for i in range(2):
                            n = JOB[f"S{u}_{i}"]
                            r = slice(64 * i, 64 * i + 64)
                            pe.matmul(opened(n)[:, 0:k1 - k0], q_a[r, h, qs], k_a[r, h, k0:k1], start=True,
                                      stop=True).then_inc(jobs_done, 1)
                    else:
                        n = JOB[f"S{u}_0"]
                        r = slice(64 * (h % 2), 64 * (h % 2) + 64)
                        dst = opened(n)[:, 0:k1 - k0]
                        pe.matmul(dst, q_b[:, h, qs], k_b[:, h, k0:k1], start=True, stop=False)
                        pe.matmul(dst, q_br[r, h // 2, qs], k_br[r, h // 2, k0:k1], start=False,
                                  stop=True).then_inc(jobs_done, 1)
                if turned_at(u) is not None:
                    turn_mod(*CORE_SETS[turned_at(u)])
                if 2 <= u <= len(UNITS) + 1:
                    kind, h, t = UNITS[u - 2]
                    n = JOB[f"W{u - 2}"]
                    dst = opened(n)
                    pe.wait_ge(w_ready, u - 1)
                    for j in range(1 if t == 0 else TILES):
                        ins = pe.transpose(dst[:, j * P:(j + 1) * P], w_sb[:, (u - 2) % 2, j * P:(j + 1) * P],
                                           k("ident"))
                    ins.then_inc(jobs_done, 1)
                if 0 <= u - SUM_AT < HEADS:
                    h = u - SUM_AT
                    pe.wait_ge(osq_ready, h + 1)
                    group(f"N_o{h}", NTOK, [(ones, osq[:, h % 2, :])])
                if u >= 3:
                    kind, h, t = UNITS[u - 3]
                    e = (u - 3) // TILES
                    taken(pe, JOB[f"W{u - 3}"])
                    if t == 0 and e >= 2:
                        pe.wait_ge(o_taken, e - 1)
                    vals = v_a if kind == "A" else v_b
                    slots = [0] if t == 0 else [1, 2, 3]
                    for j, s in enumerate(slots):
                        ins = pe.matmul(bank[O_BANK + e % 2][:, t * P:(t + 1) * P], vals[:, s, h * P:(h + 1) * P],
                                        wt_sb[:, (u - 3) % 2, j * P:(j + 1) * P], start=j == 0, stop=j == len(slots) - 1)
                    if t == TILES - 1:
                        ins.then_inc(o_done, 1)
                if u < len(UNITS):
                    for name in PIECES_AT[u]:
                        mod_piece(name)
            pe.wait_ge(olo_ready, KC)
            for i in range(4):
                pair(f"wo{i}", [JOB[f"wo{2 * i}"], JOB[f"wo{2 * i + 1}"]], hhi, hlo)

            def moe(layer):
                phase = 2 * layer + 1
                norm(phase)
                n = JOB[f"router{layer}"]
                dst = opened(n)
                pe.wait_ge(rlo_ready, layer + 1)
                for kc in range(KC):
                    pe.wait_ge(hlo_ready, KC * phase + kc + 1)
                    ins = mm3(dst[0:NEXP, 0:NTOK], rhi[:, kc, :], rlo[:, kc, :], hhi[:, kc, :], hlo[:, kc, :],
                              kc == 0, kc == KC - 1)
                ins.then_inc(jobs_done, 1)
                for i in range(2 * TILES):
                    if i == 2:
                        n = JOB[f"scores{layer}"]
                        dst = opened(n)
                        taken(pe, JOB[f"router{layer}"])
                        for t in range(TILES):
                            ins = pe.transpose(dst[:, t * NEXP:(t + 1) * NEXP], score_rows[0:NEXP, t * P:(t + 1) * P],
                                               k("ident")[0:NEXP, 0:NEXP])
                        ins.then_inc(jobs_done, 1)
                    dst = opened(JOB[f"tok{layer}_{i}"])
                    for q in range(4):
                        ins = pe.transpose(dst[:, q * P:(q + 1) * P],
                                           h_moe[:, 4 * (i % 2) + q, (i // 2) * P:(i // 2 + 1) * P], k("ident"))
                    ins.then_inc(jobs_done, 1)
                pair(f"sa{layer}", [JOB[f"shu{layer}_0"], JOB[f"shu{layer}_1"]], hhi, hlo)
                pair(f"sb{layer}", [JOB[f"shu{layer}_2"], JOB[f"shu{layer}_3"]], hhi, hlo)
                n = JOB[f"rank{layer}"]
                dst = opened(n)
                pe.wait_ge(member_ready, layer + 1)
                pe.wait_ge(kmoe_in, 16 * (layer + 1))
                member = [rt[:, 11, t * NGRP:(t + 1) * NGRP] for t in range(TILES)]
                for t in range(TILES + 1):
                    for t2 in range(min(t + 1, TILES)):
                        last_one = t2 == min(t, TILES - 1)
                        ins = pe.matmul(dst[:, t * NGRP:(t + 1) * NGRP], km("before") if t2 == t else ones, member[t2],
                                        start=t2 == 0, stop=last_one)
                ins.then_inc(jobs_done, 1)
                pe.wait_ge(hid_lo_ready, 2 * layer + 2)
                pair(f"sd{layer}", [JOB[f"shd{layer}_{i}"] for i in range(KC)], hidhi, hidlo, kcs=2)
                n = JOB[f"gate{layer}"]
                dst = opened(n)
                pe.wait_ge(place_ready, TILES * (layer + 1))
                for b_ in range(BLOCK_COLS):
                    for t in range(TILES):
                        ins = pe.matmul(dst[:, b_ * PER_GRP:(b_ + 1) * PER_GRP], place[:, t, b_ * P:(b_ + 1) * P],
                                        rt[:, 12, t * PER_GRP:(t + 1) * PER_GRP], start=t == 0, stop=t == TILES - 1)
                ins.then_inc(jobs_done, 1)
                for b_ in range(MAX_BLOCKS):
                    dst = opened(JOB[f"back{layer}_{b_}"])
                    for t in range(TILES):
                        ins = pe.transpose(dst[:, t * P:(t + 1) * P], place[:, t, b_ * P:(b_ + 1) * P], k("ident"))
                    ins.then_inc(jobs_done, 1)
                for i in range(JOB_BANKS):
                    taken(pe, JOB[f"back{layer}_{MAX_BLOCKS - 1}"] - i)
                ls = loop_sems[layer]

                def permute(it, half):
                    for kc in range(4 * half, 4 * half + 4):
                        for t in range(TILES):
                            ins = pe.matmul(bank[PERM_BANK + kc // 4][:, (kc % 4) * P:(kc % 4 + 1) * P],
                                            h_tok[:, t, kc * P:(kc + 1) * P], place[:, t, bass.ds(it * P, P)],
                                            start=t == 0, stop=t == TILES - 1)
                    ins.then_inc(ls.perm_done, 1)

                permute(0, 0)
                permute(0, 1)
                pe.wait_ge(groups_ready, layer + 1)
                count = block_count(pe)
                with pe.Fori(0, count) as it:
                    def e_split_in(j):
                        pe.wait_ge(ls.e_lo[j % SLOTS], it * SLOT_USES + (2 + j // SLOTS))

                    def up(i):
                        for part in range(UP_PARTS):
                            j = EXPERT_ORDER.index(f"u{i}_{part}")
                            wh = unit(whi, j).rearrange("p (k f) -> p k f", k=2)
                            wl = unit(wlo, j).rearrange("p (k f) -> p k f", k=2)
                            e_split_in(j)
                            for q in range(2):
                                kc = 2 * part + q
                                ins = mm3(bank[U_BANK + i % 2][:, :], blk_hi[:, kc, :], blk_lo[:, kc, :], wh[:, q, :],
                                          wl[:, q, :], kc == 0, kc == KC - 1)
                            ins.then_inc(ls.e_used[j % SLOTS], 1)

                    def turn(i):
                        pe.wait_ge(ls.hid_ready, it * PER_GRP + i + 1)
                        for c in range(2):
                            ins = pe.transpose(bank[T_BANK + i % 2][:, c * P:(c + 1) * P],
                                               hid_e[:, i % 2, c * P:(c + 1) * P], k("ident"))
                        ins.then_inc(ls.turned, 1)

                    def down(i):
                        pe.wait_ge(ls.ht_lo_ready, it * PER_GRP + (i + 1))
                        for c in range(DOWN_PARTS):
                            j = EXPERT_ORDER.index(f"d{i}_{c}")
                            e_split_in(j)
                            for half in range(2):
                                hs = slice(half * 512, (half + 1) * 512)
                                ins = mm3(bank[Y_BANK + half][:, :], ht_hi[:, i % 2, c, :], ht_lo[:, i % 2, c, :],
                                          unit(whi, j)[:, hs], unit(wlo, j)[:, hs], i == 0 and c == 0,
                                          i == PER_GRP - 1 and c == 1)
                            ins.then_inc(ls.e_used[j % SLOTS], 1)

                    pe.wait_ge(ls.blk_lo_ready, it + 1)
                    up(0)
                    up(1)
                    turn(0)
                    up(2)
                    down(0)
                    turn(1)
                    up(3)
                    down(1)
                    turn(2)
                    permute(it + 1, 0)
                    down(2)
                    turn(3)
                    permute(it + 1, 1)
                    down(3)
                pe.wait_ge(ls.blk_lo_ready, count + 1)
                pe.wait_ge(ls.y_lo_ready, count * 2)
                for kc in range(KC):
                    n = JOB[f"comb{layer}_{kc}"]
                    dst = opened(n)[:, 0:NTOK]
                    for b_ in range(MAX_BLOCKS):
                        for part in (yhi_e, ylo_e):
                            ins = pe.matmul(dst, part[:, b_, kc * P:(kc + 1) * P], back[:, b_, :],
                                            start=b_ == 0 and part is yhi_e,
                                            stop=b_ == MAX_BLOCKS - 1 and part is ylo_e)
                    ins.then_inc(jobs_done, 1)

            moe(0)

            norm(2)
            n = JOB["dt"]
            dst = opened(n)
            split_in("dtw")
            wh = piece(whi, "dtw")[:, 0:512].rearrange("p (k f) -> p k f", k=KC)
            wl = piece(wlo, "dtw")[:, 0:512].rearrange("p (k f) -> p k f", k=KC)
            for kc in range(KC):
                pe.wait_ge(hlo_ready, 2 * KC + kc + 1)
                ins = mm3(dst[0:64, 0:NTOK], wh[:, kc, :], wl[:, kc, :], hhi[:, kc, :], hlo[:, kc, :],
                          kc == 0, kc == KC - 1)
            ins.then_inc(jobs_done, 1)
            pair("bc01", [JOB["bc0"], JOB["bc1"]], hhi, hlo)
            n = JOB["dtT"]
            dst = opened(n)
            taken(pe, JOB["dt"])
            for t in range(TILES):
                ins = pe.transpose(dst[:, t * 64:(t + 1) * 64], acsT[0:64, t * P:(t + 1) * P], k("ident")[0:64, 0:64])
            ins.then_inc(jobs_done, 1)
            pair("bc23", [JOB["bc2"], JOB["bc3"]], hhi, hlo)
            pe.wait_ge(dt_ready, 1)
            pe.wait_ge(kssd_in, 32)
            dta = dts[:, 1, :].rearrange("p (t d) -> p t d", t=TILES)
            n = JOB["cs0"]
            dst = opened(n)[:, 0:384].rearrange("p (w t d) -> p w t d", w=2, t=TILES)
            for dr, name in enumerate(("upto", "since")):
                r = slice(32 * dr, 32 * dr + 32)
                pe.matmul(dst[:, 0, :, r], ks(name), dta[:, :, r], start=True, stop=True)
            pe.matmul(dst[:, 1, :, :], ones, dta, start=True, stop=True).then_inc(jobs_done, 1)
            n = JOB["cs1"]
            dst = opened(n)[:, 0:192].rearrange("p (t d) -> p t d", t=TILES)
            for dr in range(2):
                r = slice(32 * dr, 32 * dr + 32)
                ins = pe.matmul(dst[:, :, r], kcum[:, dr, :], dta[:, :, r], start=True, stop=True)
            ins.then_inc(jobs_done, 1)
            pair("bc45", [JOB["bc4"], JOB["bc5"]], hhi, hlo)
            n = JOB["csT"]
            dst = opened(n)
            taken(pe, JOB["cs0"])
            for t in range(TILES):
                ins = pe.transpose(dst[0:64, t * P:(t + 1) * P], dts[:, 5, t * 64:(t + 1) * 64], k("ident"))
            ins.then_inc(jobs_done, 1)
            pair("bc67", [JOB["bc6"], JOB["bc7"]], hhi, hlo)
            for i in range(8):
                pair(f"xsw{i}", [JOB[f"xs{2 * i}"], JOB[f"xs{2 * i + 1}"]], hhi, hlo)
            for i in range(8):
                pair(f"zw{i}", [JOB[f"z{2 * i}"], JOB[f"z{2 * i + 1}"]], hhi, hlo)

            pe.wait_ge(conv_out, 24)

            def turned(hg):
                if hg % 2 == 0:
                    g = hg // 2
                    dst = opened(JOB[f"bt{g}"])
                    for t in range(TILES):
                        ins = pe.transpose(dst[:, t * P:(t + 1) * P], bc[:, g, t * P:(t + 1) * P], k("ident"))
                    ins.then_inc(jobs_done, 1)
                    dst = opened(JOB[f"cb{g}"])
                    for t in range(TILES):
                        ts = slice(t * P, (t + 1) * P)
                        ins = pe.matmul(dst[:, ts], bc[:, g, ts], bc[:, 4 + g, ts], start=True, stop=True)
                    ins.then_inc(jobs_done, 1)
                for j, tiles in enumerate(((0, 1), (2,))):
                    dst = opened(JOB[f"xt{hg}_{j}"])
                    for a, t in enumerate(tiles):
                        for c in range(2):
                            ins = pe.transpose(dst[:, (2 * a + c) * P:(2 * a + c + 1) * P],
                                               xf[:, 2 * hg + c, t * P:(t + 1) * P], k("ident"))
                    ins.then_inc(jobs_done, 1)

            def states(hg):
                taken(pe, JOB[f"bt{hg // 2}"])
                pe.wait_ge(xw_ready, 4 * hg + 4)
                for j in range(2):
                    dst = opened(JOB[f"st{hg}_{j}"])
                    for a in range(2):
                        t = 0 if j == 0 else 1 + a
                        ins = pe.matmul(dst[:, a * 256:(a + 1) * 256], btok[:, t, :], xw[:, 2 * j + a, :],
                                        start=True, stop=True)
                    ins.then_inc(jobs_done, 1)

            def outputs(hg, t):
                n = TILES * hg + t
                dst = opened(JOB[f"y{hg}_{t}"])
                pe.wait_ge(seg_masked, 2 * n + 2)
                pe.wait_ge(xdt_ready, 2 * n + 2)
                if t:
                    pe.wait_ge(ce_ready, 4 * hg + 2 * t)
                    pe.wait_ge(s0_in[hg % 2], 16 * (hg // 2 + 1))
                    taken(pe, JOB[f"st{hg}_1"])
                for c in range(2):
                    terms = []
                    for dr in range(2):
                        for p_ in range(2):
                            i = 2 * c + p_
                            terms.append((p_, xdt[:, n % 2, dr, i * 64:(i + 1) * 64],
                                          seg[:, n % 2, dr, i * P:(i + 1) * P]))
                    if t:
                        for dr in range(2):
                            first_chunk = (t == 1) if dr == 0 else (t == 2)
                            st = s0[:, hg % 2, :] if first_chunk else s1[hg % 2][:, :]
                            for p_ in range(2):
                                i = 2 * c + p_
                                o = dr * 256 + i * 64
                                terms.append((p_, st[:, o:o + 64], ce[:, n % 2, dr, i * P:(i + 1) * P]))
                    for j, (p_, lhs, rhs) in enumerate(terms):
                        ins = pe.matmul(dst[64 * p_:64 * p_ + 64, c * P:(c + 1) * P], lhs, rhs,
                                        start=j < 2, stop=j >= len(terms) - 2, skip_group_check=True)
                ins.then_inc(jobs_done, 1)

            turned(0)
            states(0)
            for hg in range(2 * SSD_G):
                outputs(hg, 0)
                if hg + 1 < 2 * SSD_G:
                    turned(hg + 1)
                outputs(hg, 1)
                outputs(hg, 2)
                if hg + 1 < 2 * SSD_G:
                    states(hg + 1)
            def group_sum(g):
                dst = opened(JOB[f"N_y{g}"])[:, 0:NTOK]
                for c in range(4 * g, 4 * g + 4):
                    pe.wait_ge(ysq_ready, c + 1)
                    ins = pe.matmul(dst, ones, ysq[:, c % 2, :], start=c % 4 == 0, stop=c % 4 == 3)
                    if c % 4 < 3:
                        ins.then_inc(ysq_used, 1)
                ins.then_inc(jobs_done, 1)

            def out_parts(i):
                wh = piece(whi, f"sow{i}").rearrange("p (k f) -> p k f", k=XCH)
                wl = piece(wlo, f"sow{i}").rearrange("p (k f) -> p k f", k=XCH)
                return wh, wl

            def out_chunks(jobs, g):
                for kc in range(4 * g, 4 * g + 4):
                    pe.wait_ge(ylo_ready, kc + 1)
                    for i in jobs:
                        wh, wl = out_parts(i)
                        ins = mm3(bk(JOB[f"so{i}"])[:, 0:NTOK], wh[:, kc, :], wl[:, kc, :], yhi[:, kc, :],
                                  ylo[:, kc, :], kc == 0, kc == XCH - 1)
                        if kc == XCH - 1:
                            ins.then_inc(jobs_done, 1)

            group_sum(0)
            group_sum(1)
            for i in range(SPL):
                split_in(f"sow{i}")
                opened(JOB[f"so{i}"])
            for g in range(SSD_G):
                out_chunks(range(SPL), g)
                if g + 2 < SSD_G:
                    group_sum(g + 2)
            for i in range(SPL, KC):
                split_in(f"sow{i}")
                opened(JOB[f"so{i}"])
                for g in range(SSD_G):
                    out_chunks([i], g)
            moe(1)


_OUTS = {"yT": (P, KC, NTOK), "new_ak": (P, HEADS, NPROMPT), "new_av": (P, HEADS * P), "new_ckv": (P, 2, NPROMPT),
         "new_kr": (64, NPROMPT), "new_s": (P, 2, SSD_H * SSD_P)}


def chunks_of(w, starts):
    k = w.shape[0] // P
    return np.stack([w[:, s:s + P].reshape(k, P, P).transpose(1, 0, 2) for s in starts], axis=1)


def lay_stream(a):
    stream = np.zeros((len(STREAM), P, PIECE), np.float32)
    w_in, wq, wkv = a["attn_w_in"][0], a["b_wq_up"][0], a["b_wkv_up"][0]
    ssd_in, ssd_out, attn_out = a["ssd_w_in"][0], a["ssd_w_out"][0], a["attn_w_out"][0]
    c_kr = 2176
    w_kr = np.concatenate([w_in[:, c_kr:], w_in[:, c_kr:]], axis=1)
    wq_cols = np.concatenate([wq[:, h * B_DQK:h * B_DQK + P] for h in range(HEADS)] +
                             [wq[:, h * B_DQK + P:(h + 1) * B_DQK] for h in range(HEADS)], axis=1)
    kv4 = wkv.reshape(2 * P, HEADS, 2 * P)
    fixed = {
        "bqc01": chunks_of(w_in, (1536, 1664)), "kv01": chunks_of(w_in, (1920, 2048)),
        "bqc2kr": np.concatenate([chunks_of(w_in, (1792,)), chunks_of(w_kr, (0,))], axis=1),
        "aq01": chunks_of(w_in, (0, 128)), "aq23": chunks_of(w_in, (256, 384)),
        "ak01": chunks_of(w_in, (512, 640)), "ak23": chunks_of(w_in, (768, 896)),
        "wq012": chunks_of(wq_cols, (0, 128, 256)), "wq345": chunks_of(wq_cols, (384, 512, 640)),
        "wkv": np.concatenate([
            chunks_of(kv4[:, :, :P].reshape(2 * P, HEADS * P), range(0, HEADS * P, P)).reshape(P, -1),
            kv4[:, :, P:].reshape(2, P, HEADS * P).transpose(1, 0, 2).reshape(P, -1)], axis=1),
        "dtw": ssd_in[:, 5120:].reshape(KC, P, 64).transpose(1, 0, 2),
    }
    values = w_in[:, 1024:1536].reshape(KC, P, HEADS * P).transpose(1, 0, 2)
    fixed["va_lo"], fixed["va_hi"] = values[:, :4], values[:, 4:]
    for i in range(4):
        fixed[f"wo{i}"] = chunks_of(attn_out, (256 * i, 256 * i + P))
        fixed[f"bc{2 * i}{2 * i + 1}"] = chunks_of(ssd_in, (4096 + 256 * i, 4096 + 256 * i + P))
    for i in range(8):
        fixed[f"xsw{i}"] = chunks_of(ssd_in, (2048 + 256 * i, 2048 + 256 * i + P))
        fixed[f"zw{i}"] = chunks_of(ssd_in, (256 * i, 256 * i + P))
        fixed[f"sow{i}"] = chunks_of(ssd_out, (P * i,))
    for layer in range(DEPTH):
        sh_in, sh_out = a["shared_w_in"][layer], a["shared_w_out"][layer]
        fixed[f"sa{layer}"] = chunks_of(sh_in, (0, 256))
        fixed[f"sb{layer}"] = chunks_of(sh_in, (128, 384))
        fixed[f"sd{layer}"] = chunks_of(sh_out, range(0, D, P))
    for n, (kind, name) in enumerate(STREAM):
        if kind == "mod":
            layer, s, m = name
            stream[n] = a["mod_w"][layer, m * P:(m + 1) * P, s * PIECE:(s + 1) * PIECE]
            continue
        w = fixed[name]
        w = w.reshape(P, -1)
        stream[n, :, :w.shape[1]] = w
    return stream


def lay_experts(a):
    out = np.empty((DEPTH, NGRP, GRP_UNITS, P, UNIT), np.float32)
    for layer in range(DEPTH):
        for g in range(NGRP):
            for j, name in enumerate(EXPERT_ORDER):
                e, part = g * PER_GRP + int(name[1]), int(name[3])
                which = "moe_w_in" if name[0] == "u" else "moe_w_out"
                w = a[which][layer, e]
                w = w.reshape(-1, UNIT // w.shape[1], P, w.shape[1])[part]
                out[layer, g, j] = w.transpose(1, 0, 2).reshape(P, UNIT)
    return out.reshape(-1, P, UNIT)


def column(x, n=1):
    return x.reshape(n, P).T


def rows(x):
    return np.broadcast_to(x.reshape(1, -1), (P, x.size))


def lay_vectors(a):
    def twice(x):
        return np.concatenate([x, x])

    norm_g = np.stack([a["norm1_g"], a["norm2_g"]], axis=1).reshape(2 * DEPTH * KC, P)
    cols = {
        "c": np.stack([column(a["c_ctx"], KC), column(a["c"][0], KC)], axis=2).reshape(P, -1),
        "norm_g": np.repeat(norm_g.T, 2, axis=1),
        "gq_a": column(twice(a["a_qk_g"][0, 0])), "gk_a": column(twice(a["a_qk_g"][0, 1])),
        "sub_g": column(a["a_sub_g"][0]), "bqa_g": column(a["b_qa_g"][0], 3), "bkva_g": column(a["b_kva_g"][0], 2),
        "gq_bn": column(a["b_qk_g"][0, 0, :P]), "gq_br": column(twice(a["b_qk_g"][0, 0, P:])),
        "gk_bn": column(a["b_qk_g"][0, 1, :P]), "gk_br": column(twice(a["b_qk_g"][0, 1, P:])),
        "rbias": rows(a["router_bias"]),
        "conv_w": column(a["ssd_conv_w"][0], 72), "conv_b": column(a["ssd_conv_b"][0], 24),
        "ssd_d": column(np.repeat(a["ssd_d"][0], SSD_P), XCH), "ssd_g": column(a["ssd_norm_g"][0], XCH),
        "dt_bias": rows(a["ssd_dt_bias"][0]), "a_log": rows(a["ssd_a_log"][0]),
        "router": a["router_w"].reshape(KC, P, NEXP).transpose(1, 0, 2).reshape(P, -1),
    }
    return np.ascontiguousarray(np.concatenate([cols[n] for n, _ in _VEC], axis=1))


def constants():
    f = np.float32
    i = np.arange(P)
    eye = np.eye(P, dtype=f)
    kon = np.concatenate([eye, np.ones((P, P), f), np.full((P, 1), EPS, f), np.ones((P, 1), f),
                          rows(np.arange(NEXP, 0, -1).astype(f)), rows(np.arange(NGRP, 0, -1).astype(f))], axis=1)
    rot = np.zeros((P, P), f)
    for m in range(P):
        if m % 64 < 32:
            rot[m + 32, m] = -1.0
        else:
            rot[m - 32, m] = 1.0
    tok = np.arange(NLAT)
    inv = (f(ROPE_BASE) ** (f(-2.0) * np.arange(16, dtype=f) / f(32))).astype(f)
    ang = np.concatenate([(tok // GRID_W).astype(f)[:, None] * inv, (tok % GRID_W).astype(f)[:, None] * inv], axis=1)
    ang = ang.T[i % 32]
    katt = np.concatenate([(i[:, None] // 64 == i[None] // 64).astype(f), rot, np.cos(ang), np.sin(ang)], axis=1)
    r, c = i[:, None], i[None]
    kssd = np.concatenate([r <= c, r >= c], axis=1).astype(f)
    kcum = np.stack([r > c, r < c], axis=1).astype(f)
    kmoe = np.concatenate([rows(np.arange(BLOCK_COLS * P).astype(f)), (r < c).astype(f),
                           rows(np.arange(8).astype(f))], axis=1)
    return kon, katt.astype(f), kmoe, kssd, kcum


def kernel(**inputs):
    import concourse.bacc as bacc
    from concourse.bass_utils import run_bass_kernel_spmd

    a = {n: np.asarray(x) for n, x in inputs.items()}
    kon, katt, kmoe, kssd, kcum = constants()
    x = np.concatenate([a["x_prompt"][0], a["x_sample"][0]], axis=0)
    kr = a["cache_b_krope"][0, 0].T
    mod_b = a["mod_b"].reshape(DEPTH, 6 * KC, P).transpose(2, 0, 1)
    arrays = {
        "stream": lay_stream(a), "vec": lay_vectors(a), "kon": kon, "katt": katt, "kmoe": kmoe, "kssd": kssd, "kcum": kcum,
        "lam": rows(a["a_lambda"][0]), "experts": lay_experts(a),
        "modb": np.repeat(mod_b, 2, axis=2).reshape(P, DEPTH, MOD_SETS, MOD_W),
        "xT": x.T.reshape(KC, P, NTOK).transpose(1, 0, 2),
        "cache_ak": a["cache_a_k"][0, 0].transpose(2, 3, 1, 0).reshape(P, HEADS, P),
        "cache_av": a["cache_a_v"][0, 0].reshape(P, HEADS * P),
        "cache_ckv": a["cache_b_ckv"][0, 0].T.reshape(2, P, P).transpose(1, 0, 2),
        "cache_kr": np.concatenate([kr, kr], axis=0),
        "s0T": a["state_ssd"][0, 0].transpose(3, 0, 1, 2).reshape(P, 2, SSD_H * SSD_P),
    }
    nc = bacc.Bacc("TRN2", target_bir_lowering=False, num_devices=1)
    inp, out = {}, {}
    for n in list(arrays):
        arrays[n] = np.ascontiguousarray(arrays[n])
        inp[n] = nc.dram_tensor(n, arrays[n].shape, mybir.dt.from_np(arrays[n].dtype), kind="ExternalInput").ap()
    for n, shape in _OUTS.items():
        out[n] = nc.dram_tensor(n, shape, F32, kind="ExternalOutput").ap()
    build(nc, inp, out)
    r = run_bass_kernel_spmd(nc, [arrays], core_ids=[0]).results[0]
    y = r["yT"].transpose(1, 0, 2).reshape(D, NTOK).T
    new_ak = r["new_ak"].reshape(2, DQK, HEADS, NPROMPT).transpose(3, 2, 0, 1)
    new_ckv = r["new_ckv"].transpose(1, 0, 2).reshape(2 * P, NPROMPT).T
    new_s = r["new_s"].transpose(1, 2, 0).reshape(2, SSD_H, SSD_P, P)
    return (y[None, :NPROMPT], y[None, NPROMPT:], new_ak[None, None], r["new_av"].reshape(1, 1, NPROMPT, HEADS, P),
            new_ckv[None, None], r["new_kr"].T[None, None], new_s[None, None])
```
